# Optimizing a Trainium2 kernel written in Bass

```python
import math
import jax, jax.numpy as jnp
from jax import lax
import numpy as np

D_MODEL = 1024
BATCH = 1
SEQ = 256
DEPTH = 2

HEAD_DIM = 64
ATTN_WIDTH = D_MODEL // 2
ATTN_HEADS = ATTN_WIDTH // HEAD_DIM
KV_HEADS = 2
GROUP = ATTN_HEADS // KV_HEADS
IDX_HEADS = 16
IDX_DIM = 64
INDEX_TOPK = 256
Q_BLOCK = 128
CONV_WIDTH = D_MODEL // 4
CONV_KERNEL = 31
POOL_WIDTH = D_MODEL // 4
POOL_GROUPS = 4
POOL_GROUP_DIM = POOL_WIDTH // POOL_GROUPS
POOL_WINDOWS = (2, 4, 8, 16)
POOL_PAD = max(POOL_WINDOWS)
MIX_WIDTH = ATTN_WIDTH + CONV_WIDTH + POOL_WIDTH
D_FF = 4 * D_MODEL
PLE_DIM = 256
ROPE_THETA = 500000.0
ROPE_DIM = HEAD_DIM // 4
MAX_POS_OFFSET = 1024
NORM_EPS = 1e-6
LN_EPS = 1e-5

IN_SIZES = (
    ATTN_WIDTH,
    KV_HEADS * HEAD_DIM,
    KV_HEADS * HEAD_DIM,
    IDX_HEADS * IDX_DIM,
    IDX_DIM,
    IDX_HEADS,
    2 * CONV_WIDTH,
    POOL_WIDTH,
)
IN_WIDTH = int(sum(IN_SIZES))
IN_SPLITS = [int(v) for v in np.cumsum(IN_SIZES)[:-1]]


def rmsnorm(x, g):
    xf = x.astype(jnp.float32)
    y = xf * lax.rsqrt(jnp.mean(xf * xf, axis=-1, keepdims=True) + NORM_EPS)
    return (y * g.astype(jnp.float32)).astype(x.dtype)

def layernorm(x, g, b):
    xf = x.astype(jnp.float32)
    mu = jnp.mean(xf, axis=-1, keepdims=True)
    var = jnp.mean(jnp.square(xf - mu), axis=-1, keepdims=True)
    y = (xf - mu) * lax.rsqrt(var + LN_EPS)
    return (y * g.astype(jnp.float32) + b.astype(jnp.float32)).astype(x.dtype)

def rope_tables(positions):
    inv_freq = ROPE_THETA ** (-jnp.arange(0, ROPE_DIM, 2, dtype=jnp.float32) / ROPE_DIM)
    ang = positions.astype(jnp.float32)[..., None] * inv_freq
    return jnp.cos(ang)[:, :, None, :], jnp.sin(ang)[:, :, None, :]

def partial_rope(x, cos, sin):
    half = ROPE_DIM // 2
    cos = cos.astype(x.dtype)
    sin = sin.astype(x.dtype)
    x1 = x[..., :half]
    x2 = x[..., half:ROPE_DIM]
    return jnp.concatenate([x1 * cos - x2 * sin, x2 * cos + x1 * sin, x[..., ROPE_DIM:]], axis=-1)

def dsa_sparse_attention(q, k, v, qi, ki, wi):
    B, S = q.shape[0], q.shape[1]
    n_blk = S // Q_BLOCK
    k_sel = min(INDEX_TOPK, S // 4)
    idx_scale = (IDX_DIM ** -0.5) * (IDX_HEADS ** -0.5)
    att_scale = HEAD_DIM ** -0.5
    neg = jnp.finfo(jnp.float32).min
    key_pos = jnp.arange(S)
    b_idx = jnp.arange(B)[:, None, None]
    ki_f = ki.astype(jnp.float32)

    def to_blocks(t):
        return jnp.moveaxis(t.reshape((B, n_blk, Q_BLOCK) + t.shape[2:]), 1, 0)

    q_b = to_blocks(q.reshape(B, S, KV_HEADS, GROUP, HEAD_DIM))
    qi_b = to_blocks(qi)
    wi_b = to_blocks(wi)
    t_b = key_pos.reshape(n_blk, Q_BLOCK)

    def block(args):
        q_blk, qi_blk, wi_blk, t_blk = args
        dots = jnp.einsum('bthd,bsd->bths', qi_blk.astype(jnp.float32), ki_f)
        idx = jnp.einsum('bths,bth->bts', jax.nn.relu(dots), wi_blk.astype(jnp.float32)) * idx_scale
        causal = key_pos[None, :] <= t_blk[:, None]
        idx = jnp.where(causal[None], idx, -jnp.inf)
        _, sel = lax.top_k(idx, k_sel)
        valid = sel <= t_blk[None, :, None]
        k_g = k[b_idx, sel]
        v_g = v[b_idx, sel]
        s = jnp.einsum('bthgd,btnhd->bthgn', q_blk, k_g).astype(jnp.float32) * att_scale
        s = jnp.where(valid[:, :, None, None, :], s, neg)
        pr = jax.nn.softmax(s, axis=-1).astype(v.dtype)
        o = jnp.einsum('bthgn,btnhd->bthgd', pr, v_g)
        return o.reshape(B, Q_BLOCK, ATTN_WIDTH)

    out = lax.map(block, (q_b, qi_b, wi_b, t_b))
    return jnp.moveaxis(out, 0, 1).reshape(B, S, ATTN_WIDTH)

def conformer_conv(u, conv_dw, conv_b, ln_g, ln_b, conv_pw):
    a, g = jnp.split(u, 2, axis=-1)
    y = a * jax.nn.sigmoid(g)
    y = lax.conv_general_dilated(
        y, conv_dw[:, None, :], window_strides=(1,), padding=[(CONV_KERNEL - 1, 0)],
        dimension_numbers=('NWC', 'WIO', 'NWC'), feature_group_count=CONV_WIDTH)
    y = y + conv_b
    y = jax.nn.silu(layernorm(y, ln_g, ln_b))
    return jnp.einsum('bsc,cd->bsd', y, conv_pw)

def multiscale_pool(u, pool_w, pool_scale):
    B, S, _ = u.shape
    uf = u.astype(jnp.float32)
    c = jnp.cumsum(uf, axis=1)
    c_pad = jnp.concatenate([jnp.zeros((B, POOL_PAD, POOL_WIDTH), jnp.float32), c], axis=1)
    t = jnp.arange(S)
    outs = []
    for gi, w in enumerate(POOL_WINDOWS):
        sl = slice(gi * POOL_GROUP_DIM, (gi + 1) * POOL_GROUP_DIM)
        win_sum = c[:, :, sl] - c_pad[:, POOL_PAD - w:POOL_PAD - w + S, sl]
        count = jnp.minimum(t + 1, w).astype(jnp.float32)[None, :, None]
        outs.append(win_sum / count - uf[:, :, sl])
    y = jnp.stack(outs, axis=2).astype(u.dtype)
    y = jnp.einsum('bsgc,gcd->bsgd', y, pool_w).reshape(B, S, POOL_WIDTH)
    return y * pool_scale

def first_inputs(seed: int = 0) -> dict:
    key = jax.random.key(seed)
    ks = jax.random.split(key, 24)
    nrm = jax.random.normal
    f32 = jnp.float32
    L = DEPTH
    x = nrm(ks[0], (BATCH, SEQ, D_MODEL), f32)
    p = nrm(ks[1], (DEPTH, BATCH, SEQ, PLE_DIM), f32)
    offs = jax.random.randint(ks[2], (BATCH, 1), 0, MAX_POS_OFFSET, dtype=jnp.int32)
    positions = (offs + jnp.arange(SEQ, dtype=jnp.int32)[None, :]).astype(jnp.int32)
    return {
        "x": x,
        "p": p,
        "positions": positions,
        "norm_mix_pre": 1.0 + 0.1 * nrm(ks[3], (L, D_MODEL), f32),
        "w_in": nrm(ks[4], (L, D_MODEL, IN_WIDTH), f32) * D_MODEL ** -0.5,
        "conv_dw": nrm(ks[5], (L, CONV_KERNEL, CONV_WIDTH), f32) * CONV_KERNEL ** -0.5,
        "conv_b": 0.02 * nrm(ks[6], (L, CONV_WIDTH), f32),
        "conv_ln_g": 1.0 + 0.1 * nrm(ks[7], (L, CONV_WIDTH), f32),
        "conv_ln_b": 0.02 * nrm(ks[8], (L, CONV_WIDTH), f32),
        "conv_pw": nrm(ks[9], (L, CONV_WIDTH, CONV_WIDTH), f32) * CONV_WIDTH ** -0.5,
        "pool_w": nrm(ks[10], (L, POOL_GROUPS, POOL_GROUP_DIM, POOL_GROUP_DIM), f32) * POOL_GROUP_DIM ** -0.5,
        "pool_scale": 1.0 + 0.1 * nrm(ks[11], (L, POOL_WIDTH), f32),
        "w_out": nrm(ks[12], (L, MIX_WIDTH, D_MODEL), f32) * MIX_WIDTH ** -0.5,
        "norm_mix_post": 1.0 + 0.1 * nrm(ks[13], (L, D_MODEL), f32),
        "norm_mlp_pre": 1.0 + 0.1 * nrm(ks[14], (L, D_MODEL), f32),
        "w_up": nrm(ks[15], (L, D_MODEL, D_FF), f32) * D_MODEL ** -0.5,
        "w_down": nrm(ks[16], (L, D_FF, D_MODEL), f32) * D_FF ** -0.5,
        "norm_mlp_post": 1.0 + 0.1 * nrm(ks[17], (L, D_MODEL), f32),
        "ple_proj": nrm(ks[18], (L, PLE_DIM, D_MODEL), f32) * PLE_DIM ** -0.5,
        "ple_gate": nrm(ks[19], (L, D_MODEL, D_MODEL), f32) * D_MODEL ** -0.5,
    }

def first_block(x, p, positions, norm_mix_pre, w_in, conv_dw, conv_b, conv_ln_g, conv_ln_b,
              conv_pw, pool_w, pool_scale, w_out, norm_mix_post, norm_mlp_pre, w_up, w_down,
              norm_mlp_post, ple_proj, ple_gate):
    B, S, _ = x.shape
    cos, sin = rope_tables(positions)
    h = x
    for i in range(DEPTH):
        a = rmsnorm(h, norm_mix_pre[i])
        u = jnp.einsum('bsd,de->bse', a, w_in[i])
        q, k, v, qi, ki, wi, u_conv, u_pool = jnp.split(u, IN_SPLITS, axis=-1)
        q = partial_rope(q.reshape(B, S, ATTN_HEADS, HEAD_DIM), cos, sin)
        k = partial_rope(k.reshape(B, S, KV_HEADS, HEAD_DIM), cos, sin)
        v = v.reshape(B, S, KV_HEADS, HEAD_DIM)
        qi = partial_rope(qi.reshape(B, S, IDX_HEADS, IDX_DIM), cos, sin)
        ki = partial_rope(ki[:, :, None, :], cos, sin)[:, :, 0, :]
        y_attn = dsa_sparse_attention(q, k, v, qi, ki, wi)
        y_conv = conformer_conv(u_conv, conv_dw[i], conv_b[i], conv_ln_g[i],
                                conv_ln_b[i], conv_pw[i])
        y_pool = multiscale_pool(u_pool, pool_w[i], pool_scale[i])
        mix = jnp.concatenate([y_attn, y_conv, y_pool], axis=-1)
        mix = jnp.einsum('bse,ed->bsd', mix, w_out[i])
        h = h + rmsnorm(mix, norm_mix_post[i])
        m = rmsnorm(h, norm_mlp_pre[i])
        m = jnp.square(jax.nn.relu(jnp.einsum('bsd,df->bsf', m, w_up[i])))
        m = jnp.einsum('bsf,fd->bsd', m, w_down[i])
        h = h + rmsnorm(m, norm_mlp_post[i])
        gate = jax.nn.sigmoid(jnp.einsum('bsd,de->bse', h, ple_gate[i]))
        h = h + gate * jnp.einsum('bsp,pd->bsd', p[i], ple_proj[i])
    return h


CHUNK = 64
EPS = 1e-6
LRU_WIDTH = D_MODEL
LRU_BLOCKS = 16
LRU_BLOCK_DIM = LRU_WIDTH // LRU_BLOCKS
LRU_CONV = 4
LRU_C = 8.0
RET_QK_DIM = 256
RET_V_DIM = 512
RET_HEADS = D_MODEL // RET_QK_DIM
RET_QK = RET_HEADS * RET_QK_DIM
RET_V = RET_HEADS * RET_V_DIM
ROPE_BASE = 10000.0
SC_WIDTH = D_MODEL
SC_CONV = 3
D_FF_2 = 2816
SPLIT_SIZES = (LRU_WIDTH, LRU_WIDTH, RET_QK, RET_QK, RET_V, RET_V,
               SC_WIDTH, SC_WIDTH, SC_WIDTH, 3 * D_MODEL)
MIX_IN = sum(SPLIT_SIZES)


def rmsnorm_2(x, g):
    xf = x.astype(jnp.float32)
    xf = xf * lax.rsqrt(jnp.mean(xf * xf, axis=-1, keepdims=True) + EPS)
    return xf.astype(x.dtype) * g

def swiglu(u, w_in, w_out):
    gate, up = jnp.split(u @ w_in, 2, axis=-1)
    return (jax.nn.silu(gate) * up) @ w_out

def causal_depthwise_conv(x, w):
    K, C = w.shape
    return lax.conv_general_dilated(
        x, w[:, None, :].astype(x.dtype), window_strides=(1,), padding=[(K - 1, 0)],
        dimension_numbers=("NWC", "WIO", "NWC"), feature_group_count=C)

def _lin_rec_combine(e1, e2):
    a1, b1 = e1
    a2, b2 = e2
    return a1 * a2, a2 * b1 + b2

def rg_lru(x, w_a, b_a, w_x, b_x, lam):
    Bsz, S, W = x.shape
    xf = x.astype(jnp.float32)
    xb = xf.reshape(Bsz, S, LRU_BLOCKS, LRU_BLOCK_DIM)
    r = jax.nn.sigmoid(jnp.einsum("bsgi,gij->bsgj", xb, w_a.astype(jnp.float32)).reshape(Bsz, S, W)
                       + b_a.astype(jnp.float32))
    i = jax.nn.sigmoid(jnp.einsum("bsgi,gij->bsgj", xb, w_x.astype(jnp.float32)).reshape(Bsz, S, W)
                       + b_x.astype(jnp.float32))
    log_a = -LRU_C * r * jax.nn.softplus(-lam.astype(jnp.float32))
    a = jnp.exp(log_a)
    u = jnp.sqrt(-jnp.expm1(2.0 * log_a)) * (i * xf)
    _, h = lax.associative_scan(_lin_rec_combine, (a, u), axis=1)
    return h.astype(x.dtype)

def rope(t, positions):
    half = t.shape[-1] // 2
    inv_freq = jnp.power(ROPE_BASE, -jnp.arange(half, dtype=jnp.float32) / half)
    ang = positions.astype(jnp.float32)[:, None] * inv_freq[None, :]
    cos = jnp.cos(ang)[None, :, None, :]
    sin = jnp.sin(ang)[None, :, None, :]
    t1, t2 = t[..., :half], t[..., half:]
    return jnp.concatenate([t1 * cos - t2 * sin, t1 * sin + t2 * cos], axis=-1)

def retention(q, k, v, positions):
    Bsz, S, H, dk = q.shape
    dv = v.shape[-1]
    N = S // CHUNK
    q = rope(q.astype(jnp.float32), positions)
    k = rope(k.astype(jnp.float32), positions) * (dk ** -0.5)
    v = v.astype(jnp.float32)
    log_g = jnp.log1p(-jnp.power(2.0, -5.0 - jnp.arange(H, dtype=jnp.float32)))
    idx = jnp.arange(CHUNK, dtype=jnp.float32)
    intra_decay = jnp.exp(log_g[:, None, None] * jnp.abs(idx[:, None] - idx[None, :]))
    q_decay = jnp.exp(log_g[:, None] * (idx[None, :] + 1.0))
    k_decay = jnp.exp(log_g[:, None] * (CHUNK - 1.0 - idx[None, :]))
    chunk_decay = jnp.exp(log_g * CHUNK)

    def to_chunks(t):
        return t.reshape(Bsz, N, CHUNK, H, t.shape[-1]).transpose(1, 0, 3, 2, 4)

    qc, kc, vc = to_chunks(q), to_chunks(k), to_chunks(v)
    scores = jnp.einsum("nbhid,nbhjd->nbhij", qc, kc) * intra_decay
    intra = jnp.einsum("nbhij,nbhje->nbhie", scores, vc)

    def step(state, inp):
        qn, kn, vn = inp
        cross = jnp.einsum("bhid,bhde->bhie", qn, state) * q_decay[None, :, :, None]
        state = state * chunk_decay[None, :, None, None] + jnp.einsum(
            "bhjd,bhje->bhde", kn * k_decay[None, :, :, None], vn)
        return state, cross

    state0 = jnp.zeros((Bsz, H, dk, dv), jnp.float32)
    _, cross = lax.scan(step, state0, (qc, kc, vc))
    out = (intra + cross).transpose(1, 0, 3, 2, 4).reshape(Bsz, S, H, dv)
    out = out * lax.rsqrt(jnp.mean(out * out, axis=-1, keepdims=True) + EPS)
    return out

def hybrid_mixer(u, positions, w_in, lru_conv_w, lru_conv_b, lru_w_a, lru_b_a, lru_w_x, lru_b_x,
                 lru_lambda, w_lru_out, w_ret_out, sc_conv_w, w_sc_out, w_out):
    Bsz, S, _ = u.shape
    proj = u @ w_in
    cuts = [int(c) for c in np.cumsum(SPLIT_SIZES)[:-1]]
    xa, ya, q, k, v, g, sb, sc, sh, gates = jnp.split(proj, cuts, axis=-1)
    xa = causal_depthwise_conv(xa, lru_conv_w) + lru_conv_b
    ha = rg_lru(xa, lru_w_a, lru_b_a, lru_w_x, lru_b_x, lru_lambda)
    oa = (ha * jax.nn.gelu(ya)) @ w_lru_out
    ret = retention(q.reshape(Bsz, S, RET_HEADS, RET_QK_DIM),
                    k.reshape(Bsz, S, RET_HEADS, RET_QK_DIM),
                    v.reshape(Bsz, S, RET_HEADS, RET_V_DIM), positions)
    ob = (jax.nn.silu(g) * ret.reshape(Bsz, S, RET_V).astype(u.dtype)) @ w_ret_out
    oc = (sb * causal_depthwise_conv(sc * sh, sc_conv_w)) @ w_sc_out
    ga, gb, gc = jnp.split(jax.nn.sigmoid(gates), 3, axis=-1)
    return (ga * oa + gb * ob + gc * oc) @ w_out

def second_inputs(seed: int = 0) -> dict:
    key = jax.random.key(seed)
    ks = jax.random.split(key, 32)
    L = DEPTH

    def nrm(k, shape, scale):
        return jax.random.normal(k, shape, jnp.float32) * scale

    def gain(k):
        return 1.0 + 0.02 * jax.random.normal(k, (L, D_MODEL), jnp.float32)

    a_target = jax.random.uniform(ks[2], (L, LRU_WIDTH), jnp.float32, minval=0.9, maxval=0.999)
    s = a_target ** (1.0 / LRU_C)
    lru_lambda = jnp.log(s) - jnp.log1p(-s)
    offset = CHUNK * jax.random.randint(ks[3], (), 0, 64, dtype=jnp.int32)
    return {
        "x": nrm(ks[0], (BATCH, SEQ, D_MODEL), 1.0),
        "positions": offset + jnp.arange(SEQ, dtype=jnp.int32),
        "ffn1_pre_g": gain(ks[4]),
        "ffn1_w_in": nrm(ks[5], (L, D_MODEL, 2 * D_FF_2), D_MODEL ** -0.5),
        "ffn1_w_out": nrm(ks[6], (L, D_FF_2, D_MODEL), D_FF_2 ** -0.5),
        "ffn1_post_g": gain(ks[7]),
        "mix_pre_g": gain(ks[8]),
        "w_mix_in": nrm(ks[9], (L, D_MODEL, MIX_IN), D_MODEL ** -0.5),
        "lru_conv_w": nrm(ks[10], (L, LRU_CONV, LRU_WIDTH), LRU_CONV ** -0.5),
        "lru_conv_b": nrm(ks[11], (L, LRU_WIDTH), 0.01),
        "lru_w_a": nrm(ks[12], (L, LRU_BLOCKS, LRU_BLOCK_DIM, LRU_BLOCK_DIM), LRU_BLOCK_DIM ** -0.5),
        "lru_b_a": nrm(ks[13], (L, LRU_WIDTH), 0.01),
        "lru_w_x": nrm(ks[14], (L, LRU_BLOCKS, LRU_BLOCK_DIM, LRU_BLOCK_DIM), LRU_BLOCK_DIM ** -0.5),
        "lru_b_x": nrm(ks[15], (L, LRU_WIDTH), 0.01),
        "lru_lambda": lru_lambda,
        "w_lru_out": nrm(ks[16], (L, LRU_WIDTH, D_MODEL), LRU_WIDTH ** -0.5),
        "w_ret_out": nrm(ks[17], (L, RET_V, D_MODEL), RET_V ** -0.5),
        "sc_conv_w": nrm(ks[18], (L, SC_CONV, SC_WIDTH), SC_CONV ** -0.5),
        "w_sc_out": nrm(ks[19], (L, SC_WIDTH, D_MODEL), SC_WIDTH ** -0.5),
        "w_mix_out": nrm(ks[20], (L, D_MODEL, D_MODEL), D_MODEL ** -0.5),
        "mix_post_g": gain(ks[21]),
        "ffn2_pre_g": gain(ks[22]),
        "ffn2_w_in": nrm(ks[23], (L, D_MODEL, 2 * D_FF_2), D_MODEL ** -0.5),
        "ffn2_w_out": nrm(ks[24], (L, D_FF_2, D_MODEL), D_FF_2 ** -0.5),
        "ffn2_post_g": gain(ks[25]),
    }

def second_block(x, positions, ffn1_pre_g, ffn1_w_in, ffn1_w_out, ffn1_post_g, mix_pre_g, w_mix_in,
              lru_conv_w, lru_conv_b, lru_w_a, lru_b_a, lru_w_x, lru_b_x, lru_lambda, w_lru_out,
              w_ret_out, sc_conv_w, w_sc_out, w_mix_out, mix_post_g, ffn2_pre_g, ffn2_w_in,
              ffn2_w_out, ffn2_post_g):
    for l in range(DEPTH):
        h = swiglu(rmsnorm_2(x, ffn1_pre_g[l]), ffn1_w_in[l], ffn1_w_out[l])
        x = x + 0.5 * rmsnorm_2(h, ffn1_post_g[l])
        h = hybrid_mixer(rmsnorm_2(x, mix_pre_g[l]), positions, w_mix_in[l], lru_conv_w[l],
                         lru_conv_b[l], lru_w_a[l], lru_b_a[l], lru_w_x[l], lru_b_x[l],
                         lru_lambda[l], w_lru_out[l], w_ret_out[l], sc_conv_w[l], w_sc_out[l],
                         w_mix_out[l])
        x = x + rmsnorm_2(h, mix_post_g[l])
        h = swiglu(rmsnorm_2(x, ffn2_pre_g[l]), ffn2_w_in[l], ffn2_w_out[l])
        x = x + 0.5 * rmsnorm_2(h, ffn2_post_g[l])
    return x


def setup_inputs(seed=0):
    out = dict(first_inputs(seed))
    for name, value in second_inputs(seed + 1).items():
        if name != "x":
            out[name + "_2"] = value
    return out


def reference(
    x, p, positions, norm_mix_pre, w_in, conv_dw, conv_b, conv_ln_g, conv_ln_b, conv_pw, pool_w,
    pool_scale, w_out, norm_mix_post, norm_mlp_pre, w_up, w_down, norm_mlp_post, ple_proj,
    ple_gate, positions_2, ffn1_pre_g_2, ffn1_w_in_2, ffn1_w_out_2, ffn1_post_g_2, mix_pre_g_2,
    w_mix_in_2, lru_conv_w_2, lru_conv_b_2, lru_w_a_2, lru_b_a_2, lru_w_x_2, lru_b_x_2,
    lru_lambda_2, w_lru_out_2, w_ret_out_2, sc_conv_w_2, w_sc_out_2, w_mix_out_2, mix_post_g_2,
    ffn2_pre_g_2, ffn2_w_in_2, ffn2_w_out_2, ffn2_post_g_2,
):
    x = first_block(
        x, p, positions, norm_mix_pre, w_in, conv_dw, conv_b, conv_ln_g, conv_ln_b, conv_pw,
        pool_w, pool_scale, w_out, norm_mix_post, norm_mlp_pre, w_up, w_down, norm_mlp_post,
        ple_proj, ple_gate,
    )
    return second_block(
        x, positions_2, ffn1_pre_g_2, ffn1_w_in_2, ffn1_w_out_2, ffn1_post_g_2, mix_pre_g_2,
        w_mix_in_2, lru_conv_w_2, lru_conv_b_2, lru_w_a_2, lru_b_a_2, lru_w_x_2, lru_b_x_2,
        lru_lambda_2, w_lru_out_2, w_ret_out_2, sc_conv_w_2, w_sc_out_2, w_mix_out_2,
        mix_post_g_2, ffn2_pre_g_2, ffn2_w_in_2, ffn2_w_out_2, ffn2_post_g_2,
    )


_drawn_inputs = setup_inputs


def setup_inputs(seed=0):
    import zlib

    import numpy as np

    out = dict(_drawn_inputs(seed))
    spreads = {}
    factors = {'conv_ln_b': 3.102,
     'ffn1_pre_g_2': 5.729,
     'ffn1_post_g_2': 8.0,
     'mix_pre_g_2': 2.745,
     'lru_conv_b_2': 5.661,
     'lru_b_a_2': 64.0,
     'lru_b_x_2': 64.0,
     'mix_post_g_2': 5.007,
     'ffn2_pre_g_2': 7.332,
     'ffn2_post_g_2': 26.484}
    for name, (base, spread) in spreads.items():
        noise = np.random.default_rng([zlib.crc32(name.encode()), seed]).standard_normal(out[name].shape)
        drawn = base * np.exp(spread * noise) if base else spread * noise
        out[name] = __import__('jax').numpy.asarray(drawn.astype(out[name].dtype))
    for name, factor in factors.items():
        out[name] = (out[name] * factor).astype(out[name].dtype)
    return out
```

```python
import math
import numpy as np

P = 128
S = 256
D = 1024
KT = D // P
LAYERS = 2
RING = 4
RAW = 2
CHUNK_TILES = 16
CHUNK = CHUNK_TILES * P
FFN1 = 4096
FFN2 = 2816
FFN2_TILES = FFN2 // P
EPS = 1e-6
LN_EPS = 1e-5
TAPS = 31
TOPK = 64
IDX_HEADS = 16
HEADS = 8
RET_HEADS = 4
MASKED = -3.0e38
TAKEN = -3.3e38
OFF = -1.0e30
C1 = dict(inp=0, out=11, up=15, down=31, gate=47, ple=51, end=52)
G1 = dict(inp=0, out=12, up=16, down=32, gate=36, ple=40)
C2 = dict(f1in=0, f1out=22, xa=38, q=42, k=46, v=50, ya=58, lru=62, ga=66, g=70, ret=78, gb=86,
          sc=90, sco=102, gc=106, mix=110, f2in=114, f2out=136, end=152)
G2 = dict(f1in=0, f1out=24, xa=28, q=32, k=36, v=40, ya=48, lru=52, ga=56, g=60, ret=68, gb=72,
          sc=76, sco=88, gc=92, mix=96, f2in=100, f2out=124)
P1 = dict(mix_pre=0, mix_post=8, mlp_pre=16, mlp_post=24, dw=32, conv_b=94, ln_g=96, ln_b=98,
          pool_scale=100, conv_pw=102, pool_w=614, end=870)
P2 = dict(f1_pre=0, f1_post=8, mix_pre=16, conv_w=24, conv_b=56, b_a=64, b_x=72, lam=80,
          mix_post=88, f2_pre=96, f2_post=104, sc_w=112, w_a=136, w_x=1160, end=2184)
K = dict(ident=0, swap=128, tri=256, rcount=384, freq=896, end=898)
RSPAN = 384


class Count:

    def __init__(self, sem):
        self.sem, self.n, self.dyn = sem, 0, None

    def value(self):
        return self.n if self.dyn is None else self.n + self.dyn


class Line:

    def __init__(self, eng, own):
        self.eng, self.own, self.last = eng, own, None

    def do(self, ins, count=None, by=1):
        count = count or self.own
        ins.then_inc(count.sem, by)
        count.n += by
        self.last = count
        return count.n

    def settle(self):
        if self.last is not None:
            self.eng.wait_ge(self.last.sem, self.last.value())

    def loop(self, times, per, last):
        return _Loop(self, times, per, last)


class _Loop:

    def __init__(self, line, times, per, last):
        self.line, self.times, self.per, self.last = line, times, per, last

    def __enter__(self):
        self.fori = self.line.eng.Fori(0, self.times)
        i = self.fori.__enter__()
        self.base = [c.n for c, _ in self.per]
        for c, k in self.per:
            c.dyn = i * k
        self.line.last = self.last
        return i

    def __exit__(self, *a):
        for (c, k), base in zip(self.per, self.base):
            assert c.n - base == k, (c.n - base, k)
            c.n, c.dyn = base + k * self.times, None
        return self.fori.__exit__(*a)


def build(nc, a, out):
    import concourse.bass as bass
    from concourse import mybir
    from contextlib import ExitStack

    f32, f32r, i32 = mybir.dt.float32, mybir.dt.float32r, mybir.dt.int32
    ACT, ALU, AX = mybir.ActivationFunctionType, mybir.AluOpType, mybir.AxisListType
    ds = bass.ds

    with ExitStack() as ctx:
        def psum(name):
            return ctx.enter_context(nc.psum_tensor(name, [P, 512], f32))

        place = [16640]

        def sb(name, units, dtype=f32, at=None, shape=None):
            shape = shape or [P, units, S]
            if at is None:
                at = place[0]
                place[0] += -(-int(np.prod(shape[1:])) * 4 // 32) * 32
                assert place[0] <= 229344, (name, place[0])
            return nc.alloc_sbuf_tensor_at(name, shape, dtype, offset=at)

        UNIT = S * 4
        raw = sb("raw", 0, shape=[P, RAW, CHUNK])
        whi = sb("whi", 0, f32r, shape=[P, RING, CHUNK])
        wlo = sb("wlo", 0, f32r, shape=[P, RING, CHUNK])
        h = sb("h", KT)
        sqy_at = place[0]
        xhi = sb("xhi", KT, f32r)
        sqy = sb("sqy", 0, at=sqy_at, shape=[P, 4, 512])
        y_at = place[0]
        xlo = sb("xlo", KT, f32r)
        Y = sb("Y", KT, at=y_at)
        hi_at = place[0]
        bhi = sb("bhi", 32, f32r)
        lo_at = place[0]
        blo = sb("blo", 32, f32r)
        tS = sb("tS", 0, shape=[P, 2, 512])
        tX = sb("tX", 0, shape=[P, 2, 512])
        sq = sb("sq", 0, shape=[P, 2, 512])
        cst = sb("cst", 0, shape=[P, K["end"]])
        onesm = sb("onesm", 0, shape=[P, P])
        mcol = sb("mcol", 0, shape=[P, 4])
        half = sb("half", 0, shape=[P, 2])
        diag = sb("diag", 0, shape=[P, 2, P])
        var = sb("var", 0, shape=[P, 2])
        rstd = sb("rstd", 0, shape=[P, 2])
        small = sb("small", 0, shape=[P, 8, 8])
        trig2 = sb("trig2", 3)
        free_at = place[0]

        ident, swap = cst[:, 0:P], cst[:, K["swap"]:K["swap"] + P]
        tri = cst[:, K["tri"]:K["tri"] + P]

        trig1 = sb("trig1", 2)
        par1 = sb("par1", 0, shape=[P, P1["end"]])
        best = sb("best", 0, shape=[P, 2, 8])
        rmax = sb("rmax", 0, shape=[P, HEADS, 2])
        rsum = sb("rsum", 0, shape=[P, HEADS, 2])
        rinv = sb("rinv", 0, shape=[P, HEADS, 2])
        wi = sb("wi", 0, shape=[P, 2, IDX_HEADS])
        A0, B0 = hi_at + 8 * UNIT, lo_at + 8 * UNIT
        KI = sb("KI", 1, at=A0)
        KR = sb("KR", 1, at=A0 + 1 * UNIT)
        VP = sb("VP", 0, at=A0 + 2 * UNIT, shape=[P, 2, 2, P])
        QI = sb("QI", 8, at=A0 + 4 * UNIT)
        Q = sb("Q", 4, at=A0 + 12 * UNIT)
        acc = sb("acc", 0, at=A0 + 16 * UNIT, shape=[P, RSPAN])
        work = sb("work", 0, at=A0 + 18 * UNIT, shape=[P, 2, RSPAN])
        cacc = sb("cacc", 2, at=A0 + 22 * UNIT)
        YC = sb("YC", 0, at=B0, shape=[P, 2, TAPS - 1 + S])
        UP = sb("UP", 0, at=B0 + 3 * UNIT, shape=[P, 2, 16 + S])
        W2 = sb("W2", 0, at=B0 + 6 * UNIT, shape=[P, 2, 16 + S])
        W4 = sb("W4", 0, at=B0 + 9 * UNIT, shape=[P, 2, 16 + S])
        PO = sb("PO", 2, at=B0 + 12 * UNIT)
        bias = sb("bias", 0, at=B0 + 14 * UNIT, shape=[P, RSPAN])
        sm = sb("sm", 0, at=B0 + 16 * UNIT, shape=[P, 2, RSPAN])
        pt = sb("pt", 0, at=B0 + 19 * UNIT, shape=[P, 2, RSPAN])
        cact = sb("cact", 2, at=B0 + 22 * UNIT)
        GATE = sb("GATE", KT, at=hi_at)
        PT = sb("PT", 2, at=free_at + 7 * UNIT)
        pthi = sb("pthi", 2, f32r, at=free_at + 9 * UNIT)
        ptlo = sb("ptlo", 2, f32r, at=free_at + 11 * UNIT)
        assert place[0] <= free_at + 7 * UNIT and free_at + 13 * UNIT <= 229344

        par2 = sb("par2", 0, at=free_at, shape=[P, P2["end"]])
        XA = sb("XA", 0, at=free_at + 9 * UNIT, shape=[P, 8, 3 + S])
        assert free_at + 9 * UNIT + 8 * (3 + S) * 4 <= 229344, free_at
        Rg = sb("Rg", 8, at=hi_at + 8 * UNIT)
        Ag = sb("Ag", 8, at=hi_at)
        Ig = sb("Ig", 8, at=lo_at)
        Cg = sb("Cg", 8, at=lo_at + 8 * UNIT)
        RET = sb("RET", 16, at=hi_at)
        V = sb("V", 0, at=hi_at + 16 * UNIT, shape=[P, 2, 2048])
        q2 = sb("q2", 8, at=lo_at + 16 * UNIT)
        k2 = sb("k2", 8, at=lo_at + 24 * UNIT)
        O = sb("O", 8, at=hi_at + 24 * UNIT)
        MA = sb("MA", 8, at=lo_at + 24 * UNIT)
        DEC = sb("DEC", 0, at=free_at + 1 * UNIT, shape=[P, RET_HEADS * RSPAN])
        SCP = sb("SCP", 0, at=free_at + 1 * UNIT, shape=[P, 2, 2 + S])
        SCC = sb("SCC", 2, at=free_at + 4 * UNIT)
        SM = sb("SM", 0, at=free_at + 9 * UNIT + 8 * (3 + S) * 4, shape=[P, RSPAN])

        main = ctx.enter_context(nc.psum_tensor("main", [P, 4, 512], f32))
        aux = [psum(f"aux{n}") for n in range(4)]
        rb = aux[0][:, 0:S]
        stat = aux[1][:, 510:512]

        names = ("mean_done decay_in par_in w_in0 w_in1 w_hi w_lo split_free groups_free credit act_out sq_ready stat_done "
                 "var_ready rstd_ready diag_ready rb_ready h_ready x_ready y_ready act_own dve_own "
                 "pool_own hid_ready perm_done aux_ready aux_free prod_ready scores_done probs_ready "
                 "pt_done pt_ready pv_done c_ready gates_done sig_ready exp_ready root_in root_ready "
                 "coef_ready relu_used pads_ready ha_ready qk_ready sm_ready ret_ready pool_in pool_out p_in wi_ready dots_done "
                 "relu_ready v_ready out_done cst_in").split()
        sem = {n: ctx.enter_context(nc.semaphore(n)) for n in names}

        def clear_all():
            with nc.Block() as block:
                @block.gpsimd
                def _(pool):
                    for n in names:
                        pool.sem_clear(sem[n])

        with nc.Block() as block:
            ang = sq[:, 0, 0:S]
            turns = sq[:, 0, S:512]
            posf = sq[:, 1, 0:S]
            posi = nc.alloc_sbuf_tensor_at("posi", [P, 2, S], i32, offset=hi_at)

            @block.sync
            def _(sp):
                sp.dma_start(cst[:, :], a["consts"]).then_inc(sem["cst_in"], 16)
                sp.dma_start(h[:, :, :], a["x"]).then_inc(sem["cst_in"], 16)
                sp.dma_start(posi[:, :, :], a["pos"]).then_inc(sem["cst_in"], 16)
                sp.wait_ge(sem["cst_in"], 48)

            @block.gpsimd
            def _(pool):
                pool.memset(onesm[:, :], 1.0)
                pool.memset(half[:, :], -0.5)
                for n, width in enumerate((1024, 512, 256, 1)):
                    pool.memset(mcol[:, n:n + 1], 1.0 / width)

            @block.scalar
            def _(act):
                for m, t in ((0, trig1), (1, trig2)):
                    act.wait_ge(sem["x_ready"], m + 1)
                    act.activation(t[:, 1, :], Y[:, 2 * m, :], ACT.Sin)
                    ins = act.activation(t[:, 0, :], Y[:, 2 * m + 1, :], ACT.Sin).then_inc(sem["act_out"], 1)

            @block.vector
            def _(dve):
                line = Line(dve, Count(sem["dve_own"]))
                do, settle = line.do, line.settle
                dve.wait_ge(sem["cst_in"], 48)
                c1 = 6.28125
                c2 = float(np.float32(np.floor((2 * math.pi - c1) * 2 ** 20) / 2 ** 20))
                c3 = float(np.float32(2 * math.pi - c1 - c2))
                magic = 12582912.0
                pi = float(np.nextafter(np.float32(math.pi), np.float32(0)))
                for m in range(2):
                    do(dve.tensor_copy(posf, posi[:, m, :]))
                    settle()
                    do(dve.tensor_scalar(ang, posf, cst[:, K["freq"] + m:K["freq"] + m + 1], None, ALU.mult))
                    settle()
                    do(dve.tensor_scalar(turns, ang, 1.0 / (2 * math.pi), magic, ALU.mult, ALU.add))
                    settle()
                    do(dve.tensor_scalar(turns, turns, -magic, None, ALU.add))
                    for c in (c1, c2, c3):
                        settle()
                        do(dve.scalar_tensor_tensor(ang, turns, -c, ang, ALU.mult, ALU.add))
                    settle()
                    do(dve.tensor_scalar(Y[:, 2 * m, :], ang, -pi, pi, ALU.max, ALU.min))
                    settle()
                    do(dve.scalar_tensor_tensor(posf, Y[:, 2 * m, :], -1.0, Y[:, 2 * m, :], ALU.mult, ALU.max))
                    settle()
                    do(dve.tensor_scalar(Y[:, 2 * m + 1, :], posf, -1.0, math.pi / 2, ALU.mult, ALU.add))
                    settle()
                    dve.memset(small[:, 0, 0:1], 0.0).then_inc(sem["x_ready"], 1)
                dve.wait_ge(sem["act_out"], 2)
                dve.tensor_copy(trig2[:, 2, :], trig2[:, 0, :])
        clear_all()


        class Stream:

            def __init__(self, line, end):
                self.line, self.end = line, end
                self.hi_n, self.lo_n = Count(sem["w_hi"]), Count(sem["w_lo"])

            def hi(self, s, i=None):
                if s >= self.end:
                    return
                e, k = self.line.eng, 0 if i is None else i
                e.wait_ge(sem[f"w_in{s % RAW}"], 16 * (s // RAW + 1) + k * 32)
                e.wait_ge(sem["split_free"], s + 1 + k * 4)
                self.line.do(e.activation(whi[:, s % RING, :], raw[:, s % RAW, :], ACT.Copy), self.hi_n)

            def lo(self, s, i=None):
                if s >= self.end:
                    return
                e, k = self.line.eng, 0 if i is None else i
                e.wait_ge(sem["w_hi"], s + 1 + k * 4)
                self.line.do(e.tensor_tensor(wlo[:, s % RING, :], raw[:, s % RAW, :],
                                             whi[:, s % RING, :].bitcast(f32), ALU.subtract), self.lo_n)

        def used(e, s, i=None):
            e.wait_ge(sem["split_free"], s + 1 + RING + (0 if i is None else i * 4))

        def load_stream(sp, src, L, spans, end):
            def one(s, i, width):
                k = 0 if i is None else i
                if s >= RAW:
                    sp.wait_ge(sem["w_lo"], s - 1 + k * 2)
                sp.dma_start(raw[:, s % RAW, 0:width],
                             src[ds(L * (end * P) + (s + k * 2) * P, P), 0:width]).then_inc(sem[f"w_in{s % RAW}"], 16)
            for c0, c1, width in spans:
                first = c0
                if c0 == 0:
                    for s in range(4):
                        one(s, None, width)
                    first = 4
                if c1 - first > 2:
                    with sp.Fori(0, (c1 - first) // 2) as i:
                        one(first, i, width)
                        one(first + 1, i, width)
                else:
                    for s in range(first, c1):
                        one(s, None, width)

        class Tensor:
            def __init__(self, pe):
                self.pe = pe
                self.norms = self.pieces = 0

            def tile(self, out_, s, t, hi_, lo_, first, last):
                w_h, w_l = whi[:, s % RING, t * P:(t + 1) * P], wlo[:, s % RING, t * P:(t + 1) * P]
                self.pe.matmul(out_, w_h, hi_, start=first, stop=False)
                self.pe.matmul(out_, w_h, lo_, start=False, stop=False)
                return self.pe.matmul(out_, w_l, hi_, start=False, stop=last)

            def arrive(self, s, i=None):
                self.pe.wait_ge(sem["w_lo"], s + 1 + (0 if i is None else i * 4))

            def bank(self, g, i=None, step=4):
                self.pe.wait_ge(sem["groups_free"], g + 1 + (0 if i is None else i * step))

            def pair(self, s, g, i=None, tok=(False, False), cols=(P, P)):
                self.arrive(s, i)
                self.bank(g, i)
                for f in range(2):
                    if not tok[f]:
                        for kt in range(KT):
                            last = self.tile(main[:, g % 4, f * S:(f + 1) * S], s, f * KT + kt,
                                             xhi[:, kt, :], xlo[:, kt, :], kt == 0, kt == KT - 1)
                    else:
                        for t in range(2):
                            o = main[:, g % 4, f * S + t * P:f * S + t * P + cols[f]]
                            for kt in range(KT):
                                c = (f * KT + kt) * P
                                w_h, w_l = (w[:, s % RING, c:c + cols[f]] for w in (whi, wlo))
                                x_h, x_l = (x[:, kt, t * P:(t + 1) * P] for x in (xhi, xlo))
                                self.pe.matmul(o, x_h, w_h, start=kt == 0, stop=False)
                                self.pe.matmul(o, x_l, w_h, start=False, stop=False)
                                last = self.pe.matmul(o, x_h, w_l, start=False, stop=kt == KT - 1)
                last.then_inc(sem["split_free"], 1)

            def from_units(self, s, g, hi_, lo_, base):
                self.arrive(s)
                self.bank(g)
                for f in range(2):
                    for kt in range(KT):
                        last = self.tile(main[:, g % 4, f * S:(f + 1) * S], s, f * KT + kt,
                                         hi_[:, base + kt, :], lo_[:, base + kt, :], kt == 0, kt == KT - 1)
                last.then_inc(sem["split_free"], 1)

            def long(self, c0, g0, groups, tiles, per):
                with self.pe.Fori(0, groups) as i:
                    assert g0 % 4 == 0 and groups <= 4
                    self.bank(g0, i, 1)
                    for f in range(2):
                        for c in range(per):
                            n = f * per + c
                            s = c0 + n
                            self.pe.wait_ge(sem["w_lo"], s + 1 + i * (2 * per))
                            for t in range(tiles):
                                last = self.tile(
                                    main[:, ds(i, 1), f * S:(f + 1) * S].rearrange("p a n -> p (a n)"),
                                    s, t, bhi[:, c * tiles + t, :], blo[:, c * tiles + t, :],
                                    c == 0 and t == 0, c == per - 1 and t == tiles - 1)
                            last.then_inc(sem["split_free"], 1)

            def stats(self, pieces, col, src=None, y=False):
                if self.norms:
                    self.pe.wait_ge(sem["var_ready"], self.norms)
                for p in range(pieces):
                    if src is None:
                        self.pe.wait_ge(sem["sq_ready"], self.pieces + p + 1)
                    for k in range(2):
                        for t in range(2):
                            x = sqy[:, p, :] if y else sq[:, (self.pieces + p) % 2, :] if src is None else src
                            last = self.pe.matmul(stat[:, t:t + 1], x[:, k * S + t * P:k * S + (t + 1) * P],
                                                  mcol[:, col:col + 1], start=(p == 0 and k == 0 and t == 0),
                                                  stop=(p == pieces - 1 and k == 1), skip_group_check=True)
                    last.then_inc(sem["stat_done" if src is None else "mean_done"], 1)
                self.pieces += pieces if src is None else 0
                self.norms += 1

            def spread(self):
                self.pe.wait_ge(sem["diag_ready"], self.norms)
                self.pe.matmul(rb, onesm[:, :], diag[:, :, :].rearrange("p a b -> p (a b)"),
                               start=True, stop=True).then_inc(sem["rb_ready"], 1)

        class Scalar:
            def __init__(self, act, end):
                self.line = Line(act, Count(sem["act_own"]))
                self.act, self.do, self.settle = act, self.line.do, self.line.settle
                self.w = Stream(self.line, end)
                self.outs, self.sqs = Count(sem["act_out"]), Count(sem["sq_ready"])

            def squares_y(self, p):
                self.do(self.act.activation(sqy[:, p, :], two(Y, 2 * p), ACT.Square), self.sqs)

            def squares(self, src, p):
                if self.sqs.n >= 2:
                    self.act.wait_ge(sem["stat_done"], self.sqs.n - 1)
                self.do(self.act.activation(sq[:, self.sqs.n % 2, :], src, ACT.Square), self.sqs)

            def hs(self, s0, s1):
                for s in range(s0, s1):
                    self.w.hi(s)

        class Vector:
            def __init__(self, dve, end):
                self.line = Line(dve, Count(sem["dve_own"]))
                self.dve, self.do, self.settle = dve, self.line.do, self.line.settle
                self.w = Stream(self.line, end)
                self.free = Count(sem["groups_free"])
                self.vars, self.diags = Count(sem["var_ready"]), Count(sem["diag_ready"])
                self.xs, self.hs, self.ys = Count(sem["x_ready"]), Count(sem["h_ready"]), Count(sem["y_ready"])
                self.stats = self.roots = self.took = 0

            def credits(self):
                self.dve.memset(small[:, 0, 0:1], 0.0).then_inc(sem["split_free"], RING)
                self.do(self.dve.memset(small[:, 0, 1:2], 0.0), self.free, by=4)

            def factor(self, pieces, eps=EPS, scale=1.0, mean=False):
                if mean:
                    self.dve.wait_ge(sem["mean_done"], 1)
                else:
                    self.stats += pieces
                    self.dve.wait_ge(sem["stat_done"], self.stats)
                self.settle()
                if mean:
                    self.do(self.dve.tensor_copy(rstd[:, :], stat), self.vars)
                    self.settle()
                else:
                    self.do(self.dve.tensor_scalar(var[:, :], stat, eps, None, ALU.add), self.vars)
                    self.roots += 1
                    self.dve.wait_ge(sem["rstd_ready"], self.roots)
                for t in range(2):
                    ins = self.dve.tensor_scalar(diag[:, t, :], ident, rstd[:, t:t + 1], scale, ALU.mult, ALU.mult)
                    self.do(ins, self.diags if t else None)

            def spread_done(self):
                self.dve.wait_ge(sem["rb_ready"], self.diags.n)

            def split(self, hi_, lo_, src, count, by=1):
                self.settle()
                self.do(self.dve.tensor_copy(hi_, src))
                self.settle()
                self.do(self.dve.tensor_tensor(lo_, src, hi_.bitcast(f32), ALU.subtract), count, by)

            def post_norm(self, par, gain, scale=1.0):
                self.factor(4, scale=scale)
                self.spread_done()
                for p in range(4):
                    self.settle()
                    for k in range(2):
                        kt = 2 * p + k
                        self.do(self.dve.scalar_tensor_tensor(tX[:, p % 2, k * S:(k + 1) * S], Y[:, kt, :],
                                                              par[:, gain + kt:gain + kt + 1], rb,
                                                              ALU.mult, ALU.mult))
                    self.settle()
                    piece = h[:, 2 * p:2 * p + 2, :].rearrange("p a n -> p (a n)")
                    self.do(self.dve.tensor_tensor(piece, piece, tX[:, p % 2, :], ALU.add), self.hs)

            def pre_norm(self, par, gain):
                self.factor(4)
                self.spread_done()
                for p in range(4):
                    self.settle()
                    for k in range(2):
                        kt = 2 * p + k
                        self.do(self.dve.scalar_tensor_tensor(tX[:, p % 2, k * S:(k + 1) * S], h[:, kt, :],
                                                              par[:, gain + kt:gain + kt + 1], rb,
                                                              ALU.mult, ALU.mult))
                    self.split(two(xhi, 2 * p), two(xlo, 2 * p), tX[:, p % 2, :], self.xs)

            def copy_out(self, dst, g, count=None):
                self.settle()
                self.do(self.dve.tensor_copy(dst, main[:, g % 4, :]), self.free)

            def copied_y(self, s, g, p):
                used(self.dve, s)
                self.copy_out(two(Y, 2 * p), g)

        def two(t, u):
            return t[:, u:u + 2, :].rearrange("p a n -> p (a n)")

        def wide(t, u=0, n=8):
            return t[:, u:u + n, :].rearrange("p a n -> p (a n)")

        def over(t, n):
            return t.broadcast_to([P, n, S])

        def units(t):
            return t.rearrange("p (a n) -> p a n", n=S)

        def roots(pool, values):
            for v in values:
                pool.wait_ge(sem["var_ready"], v)
                pool.tensor_tensor(rstd[:, :], var[:, :], half[:, :], ALU.pow).then_inc(sem["rstd_ready"], 1)

        with nc.Fori(0, LAYERS) as L:
            with nc.Block() as block:
                @block.sync
                def _(sp):
                    load_stream(sp, a["w1"], L, [(0, C1["end"], CHUNK)], C1["end"])

                @block.gpsimd
                def _(pool):
                    line = Line(pool, Count(sem["pool_own"]))
                    do, settle = line.do, line.settle
                    pool.memset(VP[:, :, :, :], 0.0)
                    pool.memset(YC[:, :, 0:TAPS - 1], 0.0)
                    pool.memset(W2[:, :, :], 0.0)
                    pool.memset(W4[:, :, :], 0.0)
                    pool.memset(UP[:, :, 0:16], 0.0).then_inc(sem["pads_ready"], 1)
                    roots(pool, [1])
                    pool.wait_ge(sem["pads_ready"], 1)
                    pool.wait_ge(sem["pool_in"], 1)
                    end = 16 + S
                    do(pool.tensor_tensor(W2[:, :, 1:end], UP[:, :, 1:end], UP[:, :, 0:end - 1], ALU.add))
                    settle()
                    do(pool.tensor_tensor(W4[:, :, 3:end], W2[:, :, 3:end], W2[:, :, 1:end - 2], ALU.add))
                    settle()
                    do(pool.tensor_tensor(W2[:, 1, 7:end], W4[:, 1, 7:end], W4[:, 1, 3:end - 4], ALU.add))
                    settle()
                    do(pool.tensor_tensor(W4[:, 1, 15:end], W2[:, 1, 15:end], W2[:, 1, 7:end - 8], ALU.add))
                    settle()
                    for f in range(2):
                        rc = cst[:, K["rcount"] + f * S:K["rcount"] + (f + 1) * S]
                        for lo_p, w in ((0, W2), (64, W4)):
                            do(pool.tensor_tensor(PO[lo_p:lo_p + 64, f, :], w[lo_p:lo_p + 64, f, 16:end],
                                                  rc[lo_p:lo_p + 64, :], ALU.mult))
                    settle()
                    pool.tensor_tensor(PO[:, :, :], PO[:, :, :], UP[:, :, 16:end], ALU.subtract).then_inc(sem["pool_out"], 1)
                    roots(pool, [3, 4, 5, 6])

                @block.scalar
                def _(act):
                    act.dma_start(par1[:, :], a["par1"][ds(L * P, P), :]).then_inc(sem["par_in"], 16)
                    act.dma_start(PT[:, :, :].rearrange("p a n -> p (a n)"), a["p"][ds(L * P, P), :]).then_inc(sem["p_in"], 16)
                    A = Scalar(act, C1["end"])
                    do, settle, w = A.do, A.settle, A.w
                    for p in range(4):
                        A.squares(two(h, 2 * p), p)
                    A.hs(0, 3)
                    act.wait_ge(sem["par_in"], 16)

                    def relus(p):
                        for hd in range(4 * p, 4 * p + 4):
                            act.wait_ge(sem["dots_done"], hd + 1)
                            if hd >= 2:
                                act.wait_ge(sem["relu_used"], hd - 1)
                            act.activation(sm[:, hd % 2, :], aux[2 + hd % 2][:, 0:RSPAN], ACT.Relu)\
                               .then_inc(sem["relu_ready"], 1)

                    for s in range(11):
                        w.hi(s + 3)
                        if 6 <= s <= 9:
                            relus(s - 6)
                        used(act, s)
                        if s >= 2 and s < 10:
                            act.wait_ge(sem["perm_done"], s - 1)
                        if s < 8:
                            n = S if s < 2 else 2 * S
                            do(act.activation(tS[:, s % 2, 0:n], main[:, s % 4, 0:n], ACT.Copy), A.outs)
                        elif s < 10:
                            do(act.activation(tS[:, s % 2, 0:S], main[:, s % 4, S:2 * S], ACT.Sigmoid), A.outs)

                    exps_n = Count(sem["exp_ready"])

                    def exps(hh):
                        act.wait_ge(sem["sm_ready"], hh + 1)
                        for t, (c0, c1) in enumerate(((0, P), (P, RSPAN))):
                            do(act.activation(sm[:, hh % 2, c0:c1], sm[:, hh % 2, c0:c1], ACT.Exp,
                                              bias=rmax[:, hh, t:t + 1], accum_out=rsum[:, hh, t:t + 1]),
                               exps_n if t else None)

                    def turned(hh):
                        act.wait_ge(sem["pt_done"], hh + 1)
                        if hh >= 2:
                            act.wait_ge(sem["pv_done"], hh - 1)
                        act.activation(work[:, hh % 2, :], aux[1][:, 0:RSPAN], ACT.Copy).then_inc(sem["pt_ready"], 1)

                    exps(0)
                    for hh in range(HEADS):
                        if hh + 1 < HEADS:
                            exps(hh + 1)
                        turned(hh)

                    act.wait_ge(sem["c_ready"], 2)
                    A.squares(two(cacc, 0), 0)
                    act.wait_ge(sem["c_ready"], 3)
                    for f in range(2):
                        ins = act.activation(cact[:, f, :], cacc[:, f, :], ACT.Silu,
                                             bias=par1[:, P1["ln_b"] + f:P1["ln_b"] + f + 1],
                                             scale=par1[:, P1["ln_g"] + f:P1["ln_g"] + f + 1])
                    ins.then_inc(sem["sig_ready"], 1)

                    def ys(c0, g0, per):
                        for p in range(4):
                            for c in range(per):
                                w.hi(c0 + p * per + c + 3)
                            act.wait_ge(sem["groups_free"], g0 + p + 5)
                            A.squares_y(p)

                    def hsq(first):
                        for p in range(4):
                            act.wait_ge(sem["h_ready"], first + p + 1)
                            A.squares(two(h, 2 * p), p)

                    ys(C1["out"], G1["out"], 1)
                    hsq(0)
                    with A.line.loop(4, [(w.hi_n, 4), (A.outs, 4), (A.line.own, 4)], A.outs) as i:
                        for j in range(4):
                            s, g = C1["up"] + j, G1["up"] + j
                            w.hi(s + 3, i)
                            used(act, s, i)
                            act.wait_ge(sem["groups_free"], g + 3 + i * 4)
                            do(act.activation(tS[:, j % 2, :], main[:, j, :], ACT.Relu))
                            settle()
                            do(act.activation(tX[:, j % 2, :], tS[:, j % 2, :], ACT.Square), A.outs)
                    ys(C1["down"], G1["down"], 4)
                    for p in range(4):
                        s = C1["gate"] + p
                        w.hi(s + 3)
                        used(act, s)
                        do(act.activation(two(GATE, 2 * p), main[:, p, :], ACT.Sigmoid), A.outs)

                @block.vector
                def _(dve):
                    V1 = Vector(dve, C1["end"])
                    do, settle, w = V1.do, V1.settle, V1.w
                    qk, sms, prods, cs = (Count(sem[n]) for n in ("qk_ready", "sm_ready", "prod_ready", "c_ready"))
                    V1.credits()
                    dve.wait_ge(sem["par_in"], 16)
                    w.lo(0)
                    V1.pre_norm(par1, P1["mix_pre"])
                    w.lo(1)
                    w.lo(2)
                    dve.wait_ge(sem["p_in"], 16)
                    do(dve.tensor_copy(acc[:, 0:P], tri))
                    do(dve.memset(acc[:, P:2 * P], 0.0))
                    do(dve.tensor_copy(acc[:, 2 * P:3 * P], tri))
                    dve.wait_ge(sem["pads_ready"], 1)
                    cos, sin = trig1[:, 0:1, :], trig1[:, 1:2, :]
                    rope_to = {0: (KI, 0, 1), 1: (KR, 0, 1)}
                    for p in range(4):
                        rope_to[2 + p] = (QI, 2 * p, 2)
                    for p in range(2):
                        rope_to[6 + p] = (Q, 2 * p, 2)

                    def rope_finish(s):
                        t, u, n = rope_to[s]
                        dve.wait_ge(sem["perm_done"], s + 1)
                        settle()
                        do(dve.tensor_tensor(units(tX[:, s % 2, 0:n * S]), units(aux[1][:, 0:n * S]),
                                             over(sin, n), ALU.mult), aux_free)
                        settle()
                        do(dve.tensor_tensor(t[:, u:u + n, :], t[:, u:u + n, :], units(tX[:, s % 2, 0:n * S]),
                                             ALU.add), qk)

                    aux_free = Count(sem["aux_free"])
                    reads = Count(sem["relu_used"])

                    def index_sum(p):
                        for hd in range(4 * p, 4 * p + 4):
                            dve.wait_ge(sem["relu_ready"], hd + 1)
                            settle()
                            for t, (c0, c1) in enumerate(((0, P), (P, RSPAN))):
                                do(dve.scalar_tensor_tensor(acc[:, c0:c1], sm[:, hd % 2, c0:c1],
                                                            wi[:, t, hd:hd + 1], acc[:, c0:c1],
                                                            ALU.mult, ALU.add), reads if t else None)

                    for s in range(11):
                        w.lo(s + 3)
                        if 2 <= s <= 9:
                            rope_finish(s - 2)
                        if 6 <= s <= 9:
                            index_sum(s - 6)
                        bank = main[:, s % 4, :]
                        if s < 10:
                            dve.wait_ge(sem["act_out"], s + 1)
                        else:
                            used(dve, s)
                        settle()
                        if s < 8:
                            t, u, n = rope_to[s]
                            if s == 0:
                                wts = bank[:, S:2 * S].rearrange("p (t c) -> p t c", t=2)[:, :, 0:IDX_HEADS]
                                do(dve.tensor_scalar(wi[:, :, :], wts, 1.0 / 32, None, ALU.mult))
                            if s == 1:
                                vs = bank[:, S:2 * S].rearrange("p (t c) -> p t c", t=2)
                                for kv in range(2):
                                    do(dve.tensor_copy(VP[:, kv, :, kv * 64:kv * 64 + 64], vs[:, :, kv * 64:kv * 64 + 64]))
                            do(dve.tensor_tensor(t[:, u:u + n, :], units(bank[:, 0:n * S]), over(cos, n), ALU.mult), V1.free)
                        elif s < 10:
                            do(dve.tensor_tensor(YC[:, s - 8, TAPS - 1:], bank[:, 0:S], tS[:, s % 2, 0:S], ALU.mult), V1.free)
                        else:
                            do(dve.tensor_copy(UP[:, :, 16:], units(bank)), V1.free, by=2)
                            settle()
                            dve.memset(small[:, 0, 2:3], 0.0).then_inc(sem["pool_in"], 1)

                    spans = ((0, P), (P, RSPAN))
                    cur = acc[:, :]
                    for r in range(TOPK // 8):
                        nxt = work[:, r % 2, :]
                        settle()
                        for t, (c0, c1) in enumerate(spans):
                            do(dve.max(best[:, t, :], cur[:, c0:c1]))
                        settle()
                        for t, (c0, c1) in enumerate(spans):
                            do(dve.match_replace(nxt[:, c0:c1], best[:, t, :], cur[:, c0:c1], TAKEN))
                        cur = nxt
                    settle()
                    do(dve.tensor_scalar(bias[:, :], cur, TAKEN, OFF, ALU.not_equal, ALU.mult))
                    settle()
                    do(dve.tensor_tensor(bias[:, 0:P], bias[:, 0:P], tri, ALU.add))
                    do(dve.tensor_tensor(bias[:, 2 * P:], bias[:, 2 * P:], tri, ALU.add))

                    def masked(hh):
                        dve.wait_ge(sem["scores_done"], hh + 1)
                        settle()
                        do(dve.scalar_tensor_tensor(sm[:, hh % 2, :], aux[2 + hh % 2][:, 0:RSPAN], 0.125, bias[:, :],
                                                    ALU.mult, ALU.add))
                        settle()
                        for t, (c0, c1) in enumerate(spans):
                            do(dve.tensor_reduce(rmax[:, hh, t:t + 1], sm[:, hh % 2, c0:c1], AX.X, ALU.max,
                                                 negate=True), sms if t else None)

                    probs = Count(sem["probs_ready"])

                    def normed(hh):
                        dve.wait_ge(sem["exp_ready"], hh + 1)
                        if hh >= 2:
                            dve.wait_ge(sem["pt_done"], hh - 1)
                        do(dve.reciprocal(rinv[:, hh, :], rsum[:, hh, :]))
                        settle()
                        for t, (c0, c1) in enumerate(spans):
                            do(dve.tensor_scalar(pt[:, hh % 2, c0:c1], sm[:, hh % 2, c0:c1],
                                                 rinv[:, hh, t:t + 1], None, ALU.mult), probs if t else None)

                    def attended(f):
                        dve.wait_ge(sem["pv_done"], 2 * f + 2)
                        V1.split(bhi[:, f, :], blo[:, f, :], main[:, f, 0:S], prods)

                    masked(0)
                    for hh in range(HEADS):
                        if hh + 1 < HEADS:
                            masked(hh + 1)
                        normed(hh)
                        if hh % 2 and hh > 1:
                            attended(hh // 2 - 1)
                    attended(HEADS // 2 - 1)

                    for k in range(TAPS):
                        settle()
                        for f in range(2):
                            src_ = YC[:, f, k:k + S]
                            wk = par1[:, P1["dw"] + f * TAPS + k:P1["dw"] + f * TAPS + k + 1]
                            count = cs if k == TAPS - 1 and f else None
                            if k == 0:
                                do(dve.tensor_scalar(cacc[:, f, :], src_, wk,
                                                     par1[:, P1["conv_b"] + f:P1["conv_b"] + f + 1],
                                                     ALU.mult, ALU.add), count)
                            else:
                                do(dve.scalar_tensor_tensor(cacc[:, f, :], src_, wk, cacc[:, f, :],
                                                            ALU.mult, ALU.add), count)
                    V1.factor(1, mean=True)
                    V1.spread_done()
                    settle()
                    do(dve.tensor_tensor(cacc[:, :, :], cacc[:, :, :], over(rb.unsqueeze(1), 2), ALU.subtract), cs)
                    V1.factor(1, eps=LN_EPS)
                    V1.spread_done()
                    settle()
                    do(dve.tensor_tensor(cacc[:, :, :], cacc[:, :, :], over(rb.unsqueeze(1), 2), ALU.mult), cs)
                    dve.wait_ge(sem["aux_ready"], 1)
                    for f in range(2):
                        do(dve.tensor_scalar(tX[:, 0, f * S:(f + 1) * S], aux[2][:, f * S:(f + 1) * S],
                                             par1[:, P1["pool_scale"] + f:P1["pool_scale"] + f + 1], None, ALU.mult))
                    V1.split(two(bhi, 6), two(blo, 6), tX[:, 0, :], prods)
                    dve.wait_ge(sem["aux_ready"], 2)
                    V1.split(two(bhi, 4), two(blo, 4), aux[3][:, :], prods)

                    for p in range(4):
                        s = C1["out"] + p
                        w.lo(s + 3)
                        V1.copied_y(s, G1["out"] + p, p)
                    V1.post_norm(par1, P1["mix_post"])
                    V1.pre_norm(par1, P1["mlp_pre"])
                    settle()
                    with V1.line.loop(4, [(w.lo_n, 4), (V1.free, 4), (V1.line.own, 4)], V1.free) as i:
                        for j in range(4):
                            s = C1["up"] + j
                            w.lo(s + 3, i)
                            dve.wait_ge(sem["act_out"], 10 + j + 1 + i * 4)
                            settle()
                            uh = bhi[:, ds(i * 8 + 2 * j, 2), :]
                            ul = blo[:, ds(i * 8 + 2 * j, 2), :]
                            do(dve.tensor_copy(uh, units(tX[:, j % 2, :])))
                            settle()
                            do(dve.tensor_tensor(ul, units(tX[:, j % 2, :]), uh.bitcast(f32), ALU.subtract), V1.free)
                    for n in range(16):
                        s = C1["down"] + n
                        w.lo(s + 3)
                        if n % 4 == 3:
                            V1.copied_y(s, G1["down"] + n // 4, n // 4)
                    V1.post_norm(par1, P1["mlp_post"])
                    for p in range(4):
                        V1.split(two(xhi, 2 * p), two(xlo, 2 * p), two(h, 2 * p), V1.xs)
                    V1.split(two(pthi, 0), two(ptlo, 0), two(PT, 0), V1.xs)
                    for p in range(4):
                        w.lo(C1["gate"] + p + 3)
                        dve.wait_ge(sem["act_out"], 26 + p + 1)
                        do(dve.memset(small[:, 6, p:p + 1], 0.0), V1.free)
                    used(dve, C1["ple"])
                    for p in range(4):
                        settle()
                        do(dve.tensor_tensor(tX[:, p % 2, :], main[:, p, :], two(GATE, 2 * p), ALU.mult), V1.free)
                        settle()
                        do(dve.tensor_tensor(two(h, 2 * p), two(h, 2 * p), tX[:, p % 2, :], ALU.add))

                @block.tensor
                def _(pe):
                    T = Tensor(pe)
                    T.stats(4, 0)
                    T.spread()
                    pe.wait_ge(sem["x_ready"], 4)

                    def swap_rows(s):
                        n = S if s < 2 else 2 * S
                        pe.wait_ge(sem["act_out"], s + 1)
                        if s:
                            pe.wait_ge(sem["aux_free"], s)
                        pe.matmul(aux[1][:, 0:n], swap, tS[:, s % 2, 0:n], start=True, stop=True).then_inc(sem["perm_done"], 1)

                    def pairs(out_, q_, k_, off):
                        pe.matmul(out_[:, 0:P], q_[off:off + 64, 0:P], k_[off:off + 64, 0:P], start=True, stop=True)
                        return pe.matmul(out_[:, P:RSPAN], q_[off:off + 64, P:S], k_[off:off + 64, :], start=True, stop=True)

                    def dots(p):
                        pe.wait_ge(sem["qk_ready"], 3 + p)
                        for hd in range(4 * p, 4 * p + 4):
                            if hd >= 2:
                                pe.wait_ge(sem["relu_ready"], hd - 1)
                            pairs(aux[2 + hd % 2], QI[:, hd // 2, :], KI[:, 0, :], 64 * (hd % 2)).then_inc(sem["dots_done"], 1)

                    for s in range(11):
                        T.pair(s, s, tok=(False, s < 2), cols=(P, IDX_HEADS if s == 0 else P))
                        if 1 <= s <= 8:
                            swap_rows(s - 1)
                        if 5 <= s <= 8:
                            dots(s - 5)

                    def scores(hh):
                        if hh < 2:
                            pe.wait_ge(sem["relu_ready"], IDX_HEADS)
                            pe.wait_ge(sem["qk_ready"], 8)
                        else:
                            pe.wait_ge(sem["sm_ready"], hh - 1)
                        pairs(aux[2 + hh % 2], Q[:, hh // 2, :], KR[:, 0, :], 64 * (hh % 2)).then_inc(sem["scores_done"], 1)

                    def turn(hh):
                        pe.wait_ge(sem["probs_ready"], hh + 1)
                        if hh:
                            pe.wait_ge(sem["pt_ready"], hh)
                        for n in range(3):
                            last = pe.transpose(aux[1][:, n * P:(n + 1) * P], pt[:, hh % 2, n * P:(n + 1) * P], ident)
                        last.then_inc(sem["pt_done"], 1)

                    def mix_values(hh):
                        f, kv = hh // 2, hh % 2
                        pe.wait_ge(sem["pt_ready"], hh + 1)
                        o = main[:, f, 0:S]
                        pe.matmul(o, VP[:, kv, 0, :], work[:, hh % 2, 0:S], start=kv == 0, stop=kv == 1,
                                  skip_group_check=True)
                        pe.matmul(o[:, P:S], VP[:, kv, 1, :], work[:, hh % 2, S:RSPAN], start=False,
                                  stop=kv == 1, skip_group_check=True).then_inc(sem["pv_done"], 1)

                    pe.wait_ge(sem["groups_free"], 4 + 12)
                    scores(0)
                    scores(1)
                    for hh in range(HEADS):
                        turn(hh)
                        if hh + 2 < HEADS:
                            scores(hh + 2)
                        if hh:
                            mix_values(hh - 1)
                    mix_values(HEADS - 1)

                    pe.wait_ge(sem["c_ready"], 1)
                    T.stats(1, 2, src=cacc[:, :, :].rearrange("p a n -> p (a n)"))
                    T.spread()
                    T.stats(1, 2)
                    T.spread()
                    pe.wait_ge(sem["pool_out"], 1)
                    for f in range(2):
                        last = pe.matmul(aux[2][:, f * S:(f + 1) * S],
                                         par1[:, P1["pool_w"] + f * P:P1["pool_w"] + (f + 1) * P], PO[:, f, :],
                                         start=True, stop=True)
                    last.then_inc(sem["aux_ready"], 1)
                    pe.wait_ge(sem["sig_ready"], 1)
                    for f in range(2):
                        for k in range(2):
                            c = P1["conv_pw"] + (k * 2 + f) * P
                            last = pe.matmul(aux[3][:, f * S:(f + 1) * S], par1[:, c:c + P], cact[:, k, :],
                                             start=k == 0, stop=k == 1)
                    last.then_inc(sem["aux_ready"], 1)

                    pe.wait_ge(sem["prod_ready"], 6)
                    for p in range(4):
                        T.from_units(C1["out"] + p, G1["out"] + p, bhi, blo, 0)
                    T.stats(4, 0, y=True)
                    T.spread()
                    T.stats(4, 0)
                    T.spread()
                    pe.wait_ge(sem["x_ready"], 8)
                    with pe.Fori(0, 4) as i:
                        for j in range(4):
                            T.pair(C1["up"] + j, G1["up"] + j, i)
                    pe.wait_ge(sem["groups_free"], 4 + 32)
                    T.long(C1["down"], G1["down"], 4, 16, 2)
                    T.stats(4, 0, y=True)
                    T.spread()
                    pe.wait_ge(sem["x_ready"], 12)
                    for p in range(4):
                        T.pair(C1["gate"] + p, G1["gate"] + p)
                    pe.wait_ge(sem["x_ready"], 13)
                    T.arrive(C1["ple"])
                    for g in range(4):
                        T.bank(G1["ple"] + g)
                        for f in range(2):
                            for k in range(2):
                                last = T.tile(main[:, g, f * S:(f + 1) * S], C1["ple"], (2 * g + f) * 2 + k,
                                              pthi[:, k, :], ptlo[:, k, :], k == 0, k == 1)
                    last.then_inc(sem["split_free"], 1)
            clear_all()

        with nc.Fori(0, LAYERS) as L:
            with nc.Block() as block:
                narrow = FFN2_TILES // 2 * P

                @block.sync
                def _(sp):
                    load_stream(sp, a["w2"], L, [(0, 22, CHUNK), (22, 38, narrow), (38, 136, CHUNK),
                                                 (136, 152, narrow)], C2["end"])

                @block.gpsimd
                def _(pool):
                    pool.memset(XA[:, :, 0:3], 0.0).then_inc(sem["pads_ready"], 1)
                    roots(pool, range(1, 11))

                @block.scalar
                def _(act):
                    act.dma_start(par2[:, :], a["par2"][ds(L * P, P), :]).then_inc(sem["par_in"], 16)
                    A = Scalar(act, C2["end"])
                    do, settle, w = A.do, A.settle, A.w
                    for p in range(4):
                        A.squares(two(h, 2 * p), p)
                    A.hs(0, 3)
                    act.wait_ge(sem["root_in"], 1)
                    act.activation(small[:, 2, :], small[:, 1, :], ACT.Exp, scale=-1.0).then_inc(sem["root_ready"], 1)

                    def ys(c0, g0, per):
                        for p in range(4):
                            for c in range(per):
                                w.hi(c0 + p * per + c + 3)
                            act.wait_ge(sem["groups_free"], g0 + p + 5)
                            A.squares_y(p)

                    def hsq(first):
                        for p in range(4):
                            act.wait_ge(sem["h_ready"], first + p + 1)
                            A.squares(two(h, 2 * p), p)

                    def gates_in(c0, g0, first):
                        def one(j, i=None):
                            s, g = c0 + j, g0 + j
                            w.hi(s + 3, i)
                            used(act, s, i)
                            act.wait_ge(sem["groups_free"], g + 3 + (0 if i is None else i * 4))
                            do(act.activation(tS[:, j % 2, 0:S], main[:, j % 4, 0:S], ACT.Silu), A.outs)
                        with A.line.loop(5, [(w.hi_n, 4), (A.outs, 4)], A.outs) as i:
                            for j in range(4):
                                one(j, i)
                        one(20)
                        one(21)

                    def evac(s, g, func):
                        used(act, s)
                        act.wait_ge(sem["groups_free"], g + 3)
                        do(act.activation(tS[:, g % 2, :], main[:, g % 4, :], func), A.outs)

                    gates_in(C2["f1in"], G2["f1in"], 0)
                    ys(C2["f1out"], G2["f1out"], 4)
                    hsq(0)
                    act.wait_ge(sem["par_in"], 16)
                    act.wait_ge(sem["coef_ready"], 1)

                    def sigmoids(p):
                        for f in (2 * p, 2 * p + 1):
                            act.wait_ge(sem["gates_done"], f + 1)
                            bank = aux[1 + f % 2]
                            act.activation(Rg[:, f, :], bank[:, 0:S], ACT.Sigmoid,
                                           bias=par2[:, P2["b_a"] + f:P2["b_a"] + f + 1])
                            do(act.activation(Ig[:, f, :], bank[:, S:2 * S], ACT.Sigmoid,
                                              bias=par2[:, P2["b_x"] + f:P2["b_x"] + f + 1]), sigs)

                    def decays(half_):
                        settle()
                        for f in range(4 * half_, 4 * half_ + 4):
                            do(act.activation(Ag[:, f, :], Rg[:, f, :], ACT.Exp, scale=small[:, 7, f:f + 1]))
                        settle()
                        for f in range(4 * half_, 4 * half_ + 4):
                            do(act.activation(Rg[:, f, :], Rg[:, f, :], ACT.Tanh, scale=small[:, 7, f:f + 1]),
                               exps if f % 4 == 3 else None)

                    def retained(hd):
                        act.wait_ge(sem["pv_done"], hd + 1)
                        if hd == 0:
                            act.wait_ge(sem["ha_ready"], 2)
                        for n in range(2):
                            do(act.activation(two(RET, 4 * hd + 2 * n), aux[2 + n][:, :], ACT.Copy), rets)
                            A.squares(aux[2 + n][:, :], n)

                    sigs, exps, rets = (Count(sem[n]) for n in ("sig_ready", "exp_ready", "ret_ready"))
                    for s in range(C2["xa"], C2["mix"]):
                        w.hi(s + 3)
                        if 41 <= s <= 44:
                            sigmoids(s - 41)
                        if s in (45, 46):
                            decays(s - 45)
                        if s == 46:
                            act.wait_ge(sem["gates_done"], 8)
                            act.dma_start(DEC[:, :], a["decay"]).then_inc(sem["decay_in"], 16)
                        if s == 49:
                            act.wait_ge(sem["root_in"], 2)
                            act.activation(wide(Rg), wide(Rg), ACT.Sqrt, scale=-1.0).then_inc(sem["root_ready"], 1)
                        if s in (53, 55, 57, 59):
                            retained((s - 53) // 2)
                        for name, func in (("ya", ACT.Gelu_apprx_tanh), ("ga", ACT.Sigmoid), ("gb", ACT.Sigmoid),
                                           ("gc", ACT.Sigmoid), ("g", ACT.Silu)):
                            n = 8 if name == "g" else 4
                            if C2[name] <= s < C2[name] + n:
                                evac(s, G2[name] + s - C2[name], func)
                    ys(C2["mix"], G2["mix"], 1)
                    hsq(4)
                    gates_in(C2["f2in"], G2["f2in"], 46)
                    ys(C2["f2out"], G2["f2out"], 4)

                @block.vector
                def _(dve):
                    V2 = Vector(dve, C2["end"])
                    do, settle, w = V2.do, V2.settle, V2.w
                    qk, sms, prods, cs, has, roots_in = (
                        Count(sem[n]) for n in ("qk_ready", "sm_ready", "prod_ready", "c_ready", "ha_ready", "root_in"))
                    V2.credits()
                    dve.wait_ge(sem["par_in"], 16)
                    w.lo(0)
                    V2.pre_norm(par2, P2["f1_pre"])
                    w.lo(1)
                    w.lo(2)

                    lam = par2[:, P2["lam"]:P2["lam"] + 8]
                    relu_, e_, t_, t2_, s_, coef = (small[:, n, :] for n in (0, 2, 3, 4, 5, 7))
                    settle()
                    do(dve.tensor_scalar(relu_, lam, -1.0, 0.0, ALU.mult, ALU.max))
                    do(dve.scalar_tensor_tensor(small[:, 1, :], lam, -1.0, lam, ALU.mult, ALU.max), roots_in)
                    dve.wait_ge(sem["root_ready"], 1)
                    do(dve.tensor_scalar(t_, e_, 2.0, None, ALU.add))
                    settle()
                    do(dve.reciprocal(s_, t_))
                    settle()
                    do(dve.tensor_tensor(t_, s_, e_, ALU.mult))
                    settle()
                    do(dve.tensor_tensor(t2_, t_, t_, ALU.mult))
                    settle()
                    do(dve.tensor_scalar(s_, t2_, 1.0 / 17, None, ALU.mult))
                    for n in range(15, 2, -2):
                        settle()
                        do(dve.scalar_tensor_tensor(s_, s_, 1.0 / n, t2_, ALU.add, ALU.mult))
                    settle()
                    do(dve.scalar_tensor_tensor(s_, s_, 1.0, t_, ALU.add, ALU.mult))
                    settle()
                    do(dve.scalar_tensor_tensor(s_, s_, 2.0, relu_, ALU.mult, ALU.add))
                    settle()
                    do(dve.tensor_scalar(coef, s_, -8.0, None, ALU.mult), Count(sem["coef_ready"]))
                    settle()

                    def hidden(c0, g0, outs):
                        def one(j, i=None, by=1):
                            k = 0 if i is None else i * 4
                            w.lo(c0 + j + 3, i)
                            dve.wait_ge(sem["act_out"], outs + j + 1 + k)
                            settle()
                            x = tX[:, j % 2, 0:S]
                            do(dve.tensor_tensor(x, tS[:, j % 2, 0:S], main[:, j % 4, S:2 * S], ALU.mult))
                            if i is None:
                                uh, ul = bhi[:, j, :], blo[:, j, :]
                            else:
                                uh, ul = (u[:, ds(i * 4 + j, 1), :].rearrange("p a n -> p (a n)") for u in (bhi, blo))
                            V2.split(uh, ul, x, V2.free, by)
                        with V2.line.loop(5, [(w.lo_n, 4), (V2.free, 4), (V2.line.own, 8)], V2.free) as i:
                            for j in range(4):
                                one(j, i)
                        one(20)
                        one(21, by=3)

                    def narrow_out(c0, g0):
                        for n in range(16):
                            w.lo(c0 + n + 3)
                            if n % 4 == 3:
                                V2.copied_y(c0 + n, g0 + n // 4, n // 4)

                    hidden(C2["f1in"], G2["f1in"], 0)
                    narrow_out(C2["f1out"], G2["f1out"])
                    V2.post_norm(par2, P2["f1_post"], scale=0.5)
                    V2.pre_norm(par2, P2["mix_pre"])

                    cos_sin, sin_cos = trig2[:, 0:2, :], trig2[:, 1:3, :]
                    took = [22]

                    def take():
                        took[0] += 1
                        dve.wait_ge(sem["act_out"], took[0])
                        settle()

                    def before(s):
                        if s == 45:
                            dve.wait_ge(sem["sig_ready"], 8)
                            settle()
                            do(dve.tensor_tensor(wide(Ig), wide(Ig), wide(Cg), ALU.mult))
                        if s == 47:
                            dve.wait_ge(sem["exp_ready"], 2)
                            settle()
                            do(dve.tensor_tensor(wide(Cg), wide(Ag), wide(Ag), ALU.mult))
                        if s == 48:
                            settle()
                            do(dve.scalar_tensor_tensor(wide(Rg), wide(Cg), 1.0, wide(Rg), ALU.add, ALU.mult), roots_in)
                        if s == 50:
                            dve.wait_ge(sem["root_ready"], 2)
                            settle()
                            do(dve.tensor_tensor(wide(Ig), wide(Ig), wide(Rg), ALU.mult))
                        if s in (51, 52):
                            settle()
                            for f in range((s - 51) * 4, (s - 50) * 4):
                                do(dve.tensor_tensor_scan(XA[:, f, 3:], Ag[:, f, :], Ig[:, f, :], 0.0,
                                                          ALU.mult, ALU.add), has if f % 4 == 3 else None)
                        if s in (52, 54, 56, 58):
                            hd = (s - 52) // 2
                            dve.wait_ge(sem["scores_done"], hd + 1)
                            if hd:
                                dve.wait_ge(sem["pv_done"], hd)
                            dve.wait_ge(sem["decay_in"], 16)
                            do(dve.tensor_tensor(SM[:, :], aux[1][:, 0:RSPAN], DEC[:, hd * RSPAN:(hd + 1) * RSPAN],
                                                 ALU.mult), sms)
                        if s in (54, 56, 58, 60):
                            V2.factor(2)
                        if s in (55, 57, 59, 61):
                            hd = (s - 55) // 2
                            V2.spread_done()
                            dve.wait_ge(sem["ret_ready"], 2 * hd + 2)
                            settle()
                            do(dve.tensor_tensor(RET[:, 4 * hd:4 * hd + 4, :], RET[:, 4 * hd:4 * hd + 4, :],
                                                 over(rb.unsqueeze(1), 4), ALU.mult))

                    for s in range(C2["xa"], C2["mix"]):
                        w.lo(s + 3)
                        before(s)
                        if s < C2["q"]:
                            p = s - C2["xa"]
                            used(dve, s)
                            dve.wait_ge(sem["pads_ready"], 1)
                            settle()
                            g = G2["xa"] + p
                            do(dve.tensor_copy(XA[:, 2 * p:2 * p + 2, 3:], units(main[:, g % 4, :])), V2.free)
                            for k in range(4):
                                settle()
                                for f in (2 * p, 2 * p + 1):
                                    wk = par2[:, P2["conv_w"] + f * 4 + k:P2["conv_w"] + f * 4 + k + 1]
                                    count = cs if k == 3 and f % 2 else None
                                    if k == 0:
                                        do(dve.tensor_scalar(Cg[:, f, :], XA[:, f, 0:S], wk,
                                                             par2[:, P2["conv_b"] + f:P2["conv_b"] + f + 1],
                                                             ALU.mult, ALU.add))
                                    else:
                                        do(dve.scalar_tensor_tensor(Cg[:, f, :], XA[:, f, k:k + S], wk, Cg[:, f, :],
                                                                    ALU.mult, ALU.add), count)
                        elif s < C2["v"]:
                            dst, u, g = ((q2, 2 * (s - C2["q"]), G2["q"] + s - C2["q"]) if s < C2["k"] else
                                         (k2, 2 * (s - C2["k"]), G2["k"] + s - C2["k"]))
                            used(dve, s)
                            settle()
                            bank = units(main[:, g % 4, :])
                            do(dve.tensor_tensor(units(tX[:, 0, :]), bank, cos_sin, ALU.mult))
                            do(dve.tensor_tensor(units(tX[:, 1, :]), bank, sin_cos, ALU.mult), V2.free)
                            settle()
                            do(dve.tensor_tensor(dst[:, u, :], tX[:, 0, 0:S], tX[:, 0, S:], ALU.subtract))
                            do(dve.tensor_tensor(dst[:, u + 1, :], tX[:, 1, 0:S], tX[:, 1, S:], ALU.add), qk)
                        elif s < C2["ya"]:
                            p = s - C2["v"]
                            used(dve, s)
                            settle()
                            do(dve.tensor_copy(V[:, :, p * S:(p + 1) * S], units(main[:, (G2["v"] + p) % 4, :])), V2.free)
                        elif s < C2["lru"]:
                            p = s - C2["ya"]
                            take()
                            if p == 3:
                                dve.wait_ge(sem["pv_done"], RET_HEADS)
                            do(dve.tensor_tensor(units(tX[:, p % 2, :]), units(tS[:, p % 2, :]),
                                                 XA[:, 2 * p:2 * p + 2, 3:], ALU.mult), V2.free)
                            V2.split(two(bhi, 16 + 2 * p), two(blo, 16 + 2 * p), tX[:, p % 2, :], prods)
                        elif s < C2["ga"]:
                            p = s - C2["lru"]
                            used(dve, s)
                            V2.copy_out(two(O, 2 * p), G2["lru"] + p)
                        elif s < C2["g"]:
                            p = s - C2["ga"]
                            take()
                            do(dve.tensor_tensor(two(MA, 2 * p), tS[:, p % 2, :], two(O, 2 * p), ALU.mult), V2.free)
                        elif s < C2["ret"]:
                            p = s - C2["g"]
                            take()
                            do(dve.tensor_tensor(tX[:, p % 2, :], tS[:, p % 2, :], two(RET, 2 * p), ALU.mult), V2.free)
                            V2.split(two(bhi, 2 * p), two(blo, 2 * p), tX[:, p % 2, :], prods)
                        elif s < C2["gb"]:
                            p = (s - C2["ret"]) // 2
                            if (s - C2["ret"]) % 2:
                                used(dve, s)
                                V2.copy_out(two(O, 2 * p), G2["ret"] + p)
                        elif s < C2["sc"]:
                            p = s - C2["gb"]
                            if p == 0:
                                do(dve.memset(SCP[:, :, 0:2], 0.0))
                            take()
                            do(dve.tensor_tensor(tX[:, p % 2, :], tS[:, p % 2, :], two(O, 2 * p), ALU.mult), V2.free)
                            settle()
                            do(dve.tensor_tensor(two(MA, 2 * p), two(MA, 2 * p), tX[:, p % 2, :], ALU.add))
                        elif s < C2["sco"]:
                            p, part = divmod(s - C2["sc"], 3)
                            g = G2["sc"] + s - C2["sc"]
                            used(dve, s)
                            settle()
                            bank = units(main[:, g % 4, :])
                            if part == 0:
                                do(dve.tensor_copy(tX[:, 0, :], main[:, g % 4, :]), V2.free)
                            elif part == 1:
                                do(dve.tensor_tensor(SCP[:, :, 2:], bank, units(tX[:, 0, :]), ALU.mult), V2.free)
                                for k in range(3):
                                    settle()
                                    for f in range(2):
                                        c = P2["sc_w"] + (2 * p + f) * 3 + k
                                        if k == 0:
                                            do(dve.tensor_scalar(SCC[:, f, :], SCP[:, f, 0:S], par2[:, c:c + 1],
                                                                 None, ALU.mult))
                                        else:
                                            do(dve.scalar_tensor_tensor(SCC[:, f, :], SCP[:, f, k:k + S],
                                                                        par2[:, c:c + 1], SCC[:, f, :],
                                                                        ALU.mult, ALU.add))
                            else:
                                do(dve.tensor_tensor(units(tX[:, 1, :]), bank, SCC[:, :, :], ALU.mult), V2.free)
                                V2.split(two(bhi, 16 + 2 * p), two(blo, 16 + 2 * p), tX[:, 1, :], prods)
                        elif s < C2["gc"]:
                            p = s - C2["sco"]
                            used(dve, s)
                            V2.copy_out(two(O, 2 * p), G2["sco"] + p)
                        else:
                            p = s - C2["gc"]
                            take()
                            do(dve.tensor_tensor(tX[:, 0, :], tS[:, p % 2, :], two(O, 2 * p), ALU.mult), V2.free)
                            settle()
                            do(dve.tensor_tensor(tX[:, 1, :], tX[:, 0, :], two(MA, 2 * p), ALU.add))
                            V2.split(two(bhi, 2 * p), two(blo, 2 * p), tX[:, 1, :], prods)
                    for p in range(4):
                        w.lo(C2["mix"] + p + 3)
                        V2.copied_y(C2["mix"] + p, G2["mix"] + p, p)
                    V2.post_norm(par2, P2["mix_post"])
                    V2.pre_norm(par2, P2["f2_pre"])
                    hidden(C2["f2in"], G2["f2in"], took[0])
                    narrow_out(C2["f2out"], G2["f2out"])
                    V2.post_norm(par2, P2["f2_post"], scale=0.5)

                @block.tensor
                def _(pe):
                    T = Tensor(pe)

                    def ffn(c0, g0, c1, g1):
                        with pe.Fori(0, 5) as i:
                            for j in range(4):
                                T.pair(c0 + j, g0 + j, i)
                        T.pair(c0 + 20, g0 + 20)
                        T.pair(c0 + 21, g0 + 21)
                        pe.wait_ge(sem["groups_free"], 4 + g0 + 24)
                        T.long(c1, g1, 4, FFN2_TILES // 2, 2)
                        T.stats(4, 0, y=True)
                        T.spread()

                    def lru_gates(p):
                        pe.wait_ge(sem["c_ready"], p + 1)
                        for f in (2 * p, 2 * p + 1):
                            if f >= 2:
                                pe.wait_ge(sem["sig_ready"], f - 1)
                            for n, wn in enumerate(("w_a", "w_x")):
                                c = P2[wn] + f * P
                                last = pe.matmul(aux[1 + f % 2][:, n * S:(n + 1) * S], par2[:, c:c + P], Cg[:, f, :],
                                                 start=True, stop=True)
                            last.then_inc(sem["gates_done"], 1)

                    def scores(hd):
                        pe.wait_ge(sem["qk_ready"], 8)
                        pe.wait_ge(sem["sig_ready"], 8)
                        if hd:
                            pe.wait_ge(sem["sm_ready"], hd)
                        for t, c0 in ((0, 0), (1, P)):
                            for k in range(2):
                                u = 2 * hd + k
                                last = pe.matmul(aux[1][:, t * S:t * S + S - c0], k2[:, u, t * P:(t + 1) * P],
                                                 q2[:, u, c0:S], start=k == 0, stop=k == 1)
                        last.then_inc(sem["scores_done"], 1)

                    def values(hd):
                        pe.wait_ge(sem["sm_ready"], hd + 1)
                        pe.wait_ge(sem["groups_free"], 4 + G2["v"] + 2 * hd + 2)
                        if hd:
                            pe.wait_ge(sem["sq_ready"], T.pieces)
                        for e in range(4):
                            o = aux[2 + e // 2][:, e % 2 * S:(e % 2 + 1) * S]
                            c = hd * 512 + e * P
                            pe.matmul(o, V[:, 0, c:c + P], SM[:, 0:S], start=True, stop=True, skip_group_check=True)
                            last = pe.matmul(o[:, P:S], V[:, 1, c:c + P], SM[:, S:RSPAN], start=False, stop=True,
                                             skip_group_check=True)
                        last.then_inc(sem["pv_done"], 1)

                    T.stats(4, 0)
                    T.spread()
                    pe.wait_ge(sem["x_ready"], 4)
                    ffn(C2["f1in"], G2["f1in"], C2["f1out"], G2["f1out"])
                    T.stats(4, 0)
                    T.spread()
                    pe.wait_ge(sem["x_ready"], 8)

                    for s in range(C2["xa"], C2["lru"]):
                        g = (G2["xa"] if s < C2["v"] else G2["v"]) + s - (C2["xa"] if s < C2["v"] else C2["v"])
                        if C2["v"] <= s < C2["ya"]:
                            T.arrive(s)
                            T.bank(g)
                            for t in range(2):
                                o = main[:, g % 4, t * S:(t + 1) * S].rearrange("p (f c) -> p f c", f=2)
                                for kt in range(KT):
                                    w_h, w_l = (x[:, s % RING, :].rearrange("p (f k c) -> p k f c", f=2, k=KT)[:, kt]
                                                for x in (whi, wlo))
                                    x_h, x_l = (x[:, kt, t * P:(t + 1) * P] for x in (xhi, xlo))
                                    pe.matmul(o, x_h, w_h, start=kt == 0, stop=False)
                                    pe.matmul(o, x_l, w_h, start=False, stop=False)
                                    last = pe.matmul(o, x_h, w_l, start=False, stop=kt == KT - 1)
                            last.then_inc(sem["split_free"], 1)
                        else:
                            T.pair(s, g)
                        if 40 <= s <= 43:
                            lru_gates(s - 40)
                        if s in (54, 56, 58, 60):
                            T.spread()
                        if s in (53, 55, 57, 59):
                            T.stats(2, 1)
                        if s in (52, 54, 56, 58):
                            values((s - 52) // 2)
                        if s in (51, 53, 55, 57):
                            scores((s - 51) // 2)
                    pe.wait_ge(sem["prod_ready"], 4)
                    for p in range(4):
                        T.from_units(C2["lru"] + p, G2["lru"] + p, bhi, blo, 16)
                    for p in range(4):
                        T.pair(C2["ga"] + p, G2["ga"] + p)
                    with pe.Fori(0, 2) as i:
                        for j in range(4):
                            T.pair(C2["g"] + j, G2["g"] + j, i)
                    pe.wait_ge(sem["prod_ready"], 12)
                    for n in range(8):
                        s, g = C2["ret"] + n, G2["ret"] + n // 2
                        T.arrive(s)
                        if n % 2 == 0:
                            T.bank(g)
                        for t in range(16):
                            last = T.tile(main[:, g % 4, n % 2 * S:(n % 2 + 1) * S], s, t, bhi[:, t, :], blo[:, t, :],
                                          t == 0, t == 15)
                        last.then_inc(sem["split_free"], 1)
                    for p in range(4):
                        T.pair(C2["gb"] + p, G2["gb"] + p)
                    with pe.Fori(0, 3) as i:
                        for j in range(4):
                            T.pair(C2["sc"] + j, G2["sc"] + j, i)
                    pe.wait_ge(sem["prod_ready"], 16)
                    for p in range(4):
                        T.from_units(C2["sco"] + p, G2["sco"] + p, bhi, blo, 16)
                    for p in range(4):
                        T.pair(C2["gc"] + p, G2["gc"] + p)
                    pe.wait_ge(sem["prod_ready"], 20)
                    for p in range(4):
                        T.from_units(C2["mix"] + p, G2["mix"] + p, bhi, blo, 0)
                    T.stats(4, 0, y=True)
                    T.spread()
                    T.stats(4, 0)
                    T.spread()
                    pe.wait_ge(sem["x_ready"], 12)
                    ffn(C2["f2in"], G2["f2in"], C2["f2out"], G2["f2out"])
            clear_all()

        with nc.Block() as block:
            @block.sync
            def _(sp):
                sp.dma_start(out, h[:, :, :]).then_inc(sem["out_done"], 16)
                sp.wait_ge(sem["out_done"], 16)



def constants():
    c = np.zeros((P, K["end"]), np.float32)
    c[:, 0:P] = np.eye(P)
    for base in (0, 64):
        for r in range(8):
            c[base + r + 8, K["swap"] + base + r] = -1.0
            c[base + r, K["swap"] + base + r + 8] = 1.0
    t = np.arange(P)
    c[:, K["tri"]:K["tri"] + P] = np.where(t[None, :] <= t[:, None], 0.0, MASKED)
    tok = np.arange(S)
    decay = np.zeros((P, RET_HEADS * RSPAN), np.float32)
    for hd in range(RET_HEADS):
        log_g = math.log1p(-2.0 ** (-5.0 - hd))
        d = np.exp(log_g * np.abs(tok[None, :] - tok[:, None])) / 16.0
        d = np.where(tok[:, None] // 64 <= tok[None, :] // 64, d, 0.0)
        decay[:, hd * RSPAN:hd * RSPAN + S] = d[0:P, :]
        decay[:, hd * RSPAN + S:(hd + 1) * RSPAN] = d[P:S, P:S]
    for n, win in enumerate((2, 4, 8, 16)):
        f, lo = n // 2, 64 * (n % 2)
        c[lo:lo + 64, K["rcount"] + f * S:K["rcount"] + (f + 1) * S] = 1.0 / np.minimum(tok + 1, win)
    for base in (0, 64):
        for r in range(16):
            c[base + r, K["freq"]] = np.float32(500000.0) ** np.float32(-(2 * (r % 8)) / 16)
    c[:, K["freq"] + 1] = np.float32(10000.0) ** (-np.arange(P, dtype=np.float32) / np.float32(P))
    return c, decay


def tiles(m):
    k, n = m.shape
    return m.reshape(k // P, P, n // P, P).transpose(2, 0, 1, 3).reshape(-1, P, P)


def chunks(t, per=CHUNK_TILES):
    c = t.reshape(-1, per, P, P).transpose(0, 2, 1, 3).reshape(-1, P, per * P)
    out = np.zeros((c.shape[0], P, CHUNK), np.float32)
    out[:, :, 0:per * P] = c
    return out


def units_of(v):
    v = v.reshape(v.shape[0] // P, P, -1)
    return v.transpose(1, 0, 2).reshape(P, -1)


def blocks(w, n):
    out = np.zeros((P, n, P), np.float32)
    for f in range(n):
        out[0:64, f, 0:64] = w[2 * f]
        out[64:P, f, 64:P] = w[2 * f + 1]
    return out.reshape(P, n * P)


def feature_major(x):
    return np.ascontiguousarray(x.T.reshape(-1, P, S).transpose(1, 0, 2))


def lay_out(v):
    w1, w2, par1, par2, ps = [], [], [], [], []
    heads = [half * 4 + f for f in range(4) for half in range(2)]
    for l in range(LAYERS):
        w = v["w_in"][l]
        q, k, vv, qi, ki, wi, conv, pool = np.split(w, [512, 640, 768, 1792, 1856, 1872, 2384], axis=1)
        q = q.reshape(D, HEADS, 64)[:, heads].reshape(D, 512)
        wi_ = np.zeros((D, P), np.float32)
        wi_[:, 0:IDX_HEADS] = wi
        order = [ki, ki, wi_, k, vv, qi, q, conv[:, 0:128], conv[:, 256:384], conv[:, 128:256], conv[:, 384:512], pool]
        w_out = v["w_out"][l]
        w_out = np.concatenate([w_out[0:512].reshape(HEADS, 64, D)[heads].reshape(512, D), w_out[512:]], axis=0)
        w1 += [chunks(tiles(np.concatenate(order, axis=1))), chunks(tiles(w_out)), chunks(tiles(v["w_up"][l])),
               chunks(tiles(v["w_down"][l])), chunks(tiles(v["ple_gate"][l])), chunks(tiles(v["ple_proj"][l]))]
        cp = v["conv_pw"][l]
        par1.append(np.concatenate(
            [units_of(v[n][l]) for n in ("norm_mix_pre", "norm_mix_post", "norm_mlp_pre", "norm_mlp_post")]
            + [units_of(v["conv_dw"][l].T), units_of(v["conv_b"][l]), units_of(v["conv_ln_g"][l]),
               units_of(v["conv_ln_b"][l]), units_of(v["pool_scale"][l]), units_of(cp), blocks(v["pool_w"][l], 2)],
            axis=1))
        ps.append(feature_major(v["p"][l, 0]).reshape(P, 2 * S))

        def ffn(n):
            w = v[n + "_w_in_2"][l]
            both = np.stack([w[:, 0:FFN2].reshape(D, FFN2_TILES, P), w[:, FFN2:].reshape(D, FFN2_TILES, P)], axis=2)
            return [chunks(tiles(both.reshape(D, 2 * FFN2))), chunks(tiles(v[n + "_w_out_2"][l]), FFN2_TILES // 2)]

        m = v["w_mix_in_2"][l]
        xa, ya, q, k, vv, g, sb, sc, sh, gates = np.split(m, [1024, 2048, 3072, 4096, 6144, 8192, 9216, 10240, 11264], axis=1)
        ga, gb, gc = np.split(gates, 3, axis=1)
        thirds = np.stack([z.reshape(D, 4, 256) for z in (sc, sh, sb)], axis=2).reshape(D, 3072)
        w2 += ffn("ffn1") + [chunks(tiles(z)) for z in (
            xa, q, k, vv, ya, v["w_lru_out_2"][l], ga, g, v["w_ret_out_2"][l], gb, thirds, v["w_sc_out_2"][l], gc,
            v["w_mix_out_2"][l])] + ffn("ffn2")
        par2.append(np.concatenate(
            [units_of(v[n + "_2"][l]) for n in ("ffn1_pre_g", "ffn1_post_g", "mix_pre_g")]
            + [units_of(v["lru_conv_w_2"][l].T)]
            + [units_of(v[n + "_2"][l]) for n in ("lru_conv_b", "lru_b_a", "lru_b_x", "lru_lambda", "mix_post_g",
                                                  "ffn2_pre_g", "ffn2_post_g")]
            + [units_of(v["sc_conv_w_2"][l].T), blocks(v["lru_w_a_2"][l], 8), blocks(v["lru_w_x_2"][l], 8)], axis=1))
    consts, decay = constants()
    pos = np.stack([v["positions"].reshape(S), v["positions_2"].reshape(S)])
    return {
        "x": feature_major(v["x"][0]),
        "pos": np.ascontiguousarray(np.broadcast_to(pos[None], (P, 2, S))),
        "consts": consts,
        "decay": decay,
        "par1": np.concatenate(par1, axis=0),
        "par2": np.concatenate(par2, axis=0),
        "p": np.concatenate(ps, axis=0),
        "w1": np.concatenate(w1, axis=0).reshape(-1, CHUNK),
        "w2": np.concatenate(w2, axis=0).reshape(-1, CHUNK),
    }


def kernel(**inputs):
    import concourse.bacc as bacc
    from concourse import mybir
    from concourse.bass_utils import run_bass_kernel_spmd

    arrays = lay_out({k: np.asarray(v) for k, v in inputs.items()})
    nc = bacc.Bacc("TRN2", target_bir_lowering=False, num_devices=1)
    drams = {n: nc.dram_tensor(f"in_{n}", z.shape, mybir.dt.from_np(z.dtype), kind="ExternalInput").ap()
             for n, z in arrays.items()}
    out = nc.dram_tensor("out_h", (P, KT, S), mybir.dt.float32, kind="ExternalOutput").ap()
    build(nc, drams, out)
    r = run_bass_kernel_spmd(nc, [{f"in_{n}": z for n, z in arrays.items()}], core_ids=[0])
    got = np.asarray(r.results[0]["out_h"])
    return np.ascontiguousarray(got.transpose(1, 0, 2).reshape(1, D, S).transpose(0, 2, 1))
```

```python
import math
import numpy as np

P = 128
S = 256
D = 1024
KT = D // P
LAYERS = 2
RING = 4
RAW = 2
CHUNK_TILES = 16
CHUNK = CHUNK_TILES * P
FFN1 = 4096
FFN2 = 2816
FFN2_TILES = FFN2 // P
NARROW = FFN2_TILES // 2 * P
EPS = 1e-6
LN_EPS = 1e-5
TAPS = 31
TOPK = 64
IDX_HEADS = 16
HEADS = 8
RET_HEADS = 4
MASKED = -3.0e38
TAKEN = -3.3e38
OFF = -1.0e30
C1 = dict(inp=0, out=11, up=15, down=31, gate=47, ple=51, end=52)
G1 = dict(inp=0, out=12, up=16, down=32, gate=36, ple=40)
C2 = dict(f1in=0, f1out=22, xa=38, q=42, k=46, v=50, ya=58, lru=62, ga=66, g=70, ret=78, gb=86,
          sc=90, sco=102, gc=106, mix=110, f2in=114, f2out=136, end=152)
G2 = dict(f1in=0, f1out=24, xa=28, q=32, k=36, v=40, ya=48, lru=52, ga=56, g=60, ret=68, gb=72,
          sc=76, sco=88, gc=92, mix=96, f2in=100, f2out=124)
P1 = dict(mix_pre=0, mix_post=8, mlp_pre=16, mlp_post=24, dw=32, conv_b=94, ln_g=96, ln_b=98,
          pool_scale=100, conv_pw=102, pool_w=614, end=870)
P2 = dict(f1_pre=0, f1_post=8, mix_pre=16, conv_w=24, conv_b=56, b_a=64, b_x=72, lam=80,
          mix_post=88, f2_pre=96, f2_post=104, sc_w=112, w_a=136, w_x=1160, end=2184)
K = dict(ident=0, swap=128, tri=256, rcount=384, freq=896, end=898)
RSPAN = 384


class Count:

    def __init__(self, sem):
        self.sem, self.n, self.dyn = sem, 0, None

    def value(self):
        return self.n if self.dyn is None else self.n + self.dyn


class Line:

    def __init__(self, eng, own):
        self.eng, self.own, self.last = eng, own, None

    def do(self, ins, count=None, by=1):
        count = count or self.own
        ins.then_inc(count.sem, by)
        count.n += by
        self.last = count
        return count.n

    def settle(self):
        if self.last is not None:
            self.eng.wait_ge(self.last.sem, self.last.value())

    def loop(self, times, per, last):
        return _Loop(self, times, per, last)


class _Loop:

    def __init__(self, line, times, per, last):
        self.line, self.times, self.per, self.last = line, times, per, last

    def __enter__(self):
        self.fori = self.line.eng.Fori(0, self.times)
        i = self.fori.__enter__()
        self.base = [c.n for c, _ in self.per]
        for c, k in self.per:
            c.dyn = i * k
        self.line.last = self.last
        return i

    def __exit__(self, *a):
        for (c, k), base in zip(self.per, self.base):
            assert c.n - base == k, (c.n - base, k)
            c.n, c.dyn = base + k * self.times, None
        return self.fori.__exit__(*a)


def build(nc, a, out):
    import concourse.bass as bass
    from concourse import mybir
    from contextlib import ExitStack

    f32, f32r, i32 = mybir.dt.float32, mybir.dt.float32r, mybir.dt.int32
    ACT, ALU, AX = mybir.ActivationFunctionType, mybir.AluOpType, mybir.AxisListType
    ds = bass.ds

    with ExitStack() as ctx:
        def psum(name):
            return ctx.enter_context(nc.psum_tensor(name, [P, 512], f32))

        place = [16640]

        def sb(name, units, dtype=f32, at=None, shape=None):
            shape = shape or [P, units, S]
            if at is None:
                at = place[0]
                place[0] += -(-int(np.prod(shape[1:])) * 4 // 32) * 32
                assert place[0] <= 229344, (name, place[0])
            return nc.alloc_sbuf_tensor_at(name, shape, dtype, offset=at)

        UNIT = S * 4
        raw = sb("raw", 0, shape=[P, RAW, CHUNK])
        whi = sb("whi", 0, f32r, shape=[P, RING, CHUNK])
        wlo = sb("wlo", 0, f32r, shape=[P, RING, CHUNK])
        h = sb("h", KT)
        sqy_at = place[0]
        xhi = sb("xhi", KT, f32r)
        sqy = sb("sqy", 0, at=sqy_at, shape=[P, 4, 512])
        HG = sb("HG", KT, at=sqy_at)
        y_at = place[0]
        xlo = sb("xlo", KT, f32r)
        Y = sb("Y", KT, at=y_at)
        hi_at = place[0]
        bhi = sb("bhi", 32, f32r)
        lo_at = place[0]
        blo = sb("blo", 32, f32r)
        tS = sb("tS", 0, shape=[P, 2, 512])
        tX = sb("tX", 0, shape=[P, 2, 512])
        sq = sb("sq", 0, shape=[P, 2, 512])
        cst = sb("cst", 0, shape=[P, K["end"]])
        onesm = sb("onesm", 0, shape=[P, P])
        mcol = sb("mcol", 0, shape=[P, 4])
        half = sb("half", 0, shape=[P, 2])
        diag = sb("diag", 0, shape=[P, 2, P])
        var = sb("var", 0, shape=[P, 2])
        rstd = sb("rstd", 0, shape=[P, 2])
        small = sb("small", 0, shape=[P, 8, 8])
        trig2 = sb("trig2", 3)
        free_at = place[0]

        ident, swap = cst[:, 0:P], cst[:, K["swap"]:K["swap"] + P]
        tri = cst[:, K["tri"]:K["tri"] + P]

        trig1 = sb("trig1", 2)
        par1 = sb("par1", 0, shape=[P, P1["end"]])
        best = sb("best", 0, shape=[P, 2, 8])
        rmax = sb("rmax", 0, shape=[P, HEADS, 2])
        rsum = sb("rsum", 0, shape=[P, HEADS, 2])
        rinv = sb("rinv", 0, shape=[P, HEADS, 2])
        wi = sb("wi", 0, shape=[P, 2, IDX_HEADS])
        A0, B0 = hi_at + 8 * UNIT, lo_at + 8 * UNIT
        KI = sb("KI", 1, at=A0)
        KR = sb("KR", 1, at=A0 + 1 * UNIT)
        VP = sb("VP", 0, at=A0 + 2 * UNIT, shape=[P, 2, 2, P])
        QI = sb("QI", 8, at=A0 + 4 * UNIT)
        Q = sb("Q", 4, at=A0 + 12 * UNIT)
        acc = sb("acc", 0, at=A0 + 16 * UNIT, shape=[P, RSPAN])
        work = sb("work", 0, at=A0 + 18 * UNIT, shape=[P, 2, RSPAN])
        cacc = sb("cacc", 2, at=A0 + 22 * UNIT)
        YC = sb("YC", 0, at=B0, shape=[P, 2, TAPS - 1 + S])
        UP = sb("UP", 0, at=B0 + 3 * UNIT, shape=[P, 2, 16 + S])
        W2 = sb("W2", 0, at=B0 + 6 * UNIT, shape=[P, 2, 16 + S])
        W4 = sb("W4", 0, at=B0 + 9 * UNIT, shape=[P, 2, 16 + S])
        PO = sb("PO", 2, at=B0 + 12 * UNIT)
        bias = sb("bias", 0, at=B0 + 14 * UNIT, shape=[P, RSPAN])
        sm = sb("sm", 0, at=B0 + 16 * UNIT, shape=[P, 2, RSPAN])
        pt = sb("pt", 0, at=B0 + 19 * UNIT, shape=[P, 2, RSPAN])
        cact = sb("cact", 2, at=B0 + 22 * UNIT)
        GATE = sb("GATE", KT, at=hi_at)
        PT = sb("PT", 2, at=free_at + 7 * UNIT)
        pthi = sb("pthi", 2, f32r, at=free_at + 9 * UNIT)
        ptlo = sb("ptlo", 2, f32r, at=free_at + 11 * UNIT)
        assert place[0] <= free_at + 7 * UNIT and free_at + 13 * UNIT <= 229344

        par2 = sb("par2", 0, at=free_at, shape=[P, P2["end"]])
        XA = sb("XA", 0, at=free_at + 9 * UNIT, shape=[P, 8, 3 + S])
        assert free_at + 9 * UNIT + 8 * (3 + S) * 4 <= 229344, free_at
        Rg = sb("Rg", 8, at=hi_at + 8 * UNIT)
        Ag = sb("Ag", 8, at=hi_at)
        Ig = sb("Ig", 8, at=lo_at)
        Cg = sb("Cg", 8, at=lo_at + 8 * UNIT)
        RET = sb("RET", 16, at=hi_at)
        V = sb("V", 0, at=hi_at + 16 * UNIT, shape=[P, 2, 2048])
        q2 = sb("q2", 8, at=lo_at + 16 * UNIT)
        k2 = sb("k2", 8, at=lo_at + 24 * UNIT)
        O = sb("O", 8, at=hi_at + 24 * UNIT)
        MA = sb("MA", 8, at=lo_at + 24 * UNIT)
        DEC = sb("DEC", 0, at=free_at + 1 * UNIT, shape=[P, RET_HEADS * RSPAN])
        SCP = sb("SCP", 0, at=free_at + 1 * UNIT, shape=[P, 2, 2 + S])
        SCC = sb("SCC", 2, at=free_at + 4 * UNIT)
        SM = sb("SM", 0, at=free_at + 9 * UNIT + 8 * (3 + S) * 4, shape=[P, RSPAN])

        main = ctx.enter_context(nc.psum_tensor("main", [P, 4, 512], f32))
        aux = [psum(f"aux{n}") for n in range(4)]
        rb = aux[0][:, 0:S]
        stat = aux[1][:, 510:512]

        names = ("gain_ready round_ready xf_ready big_par_in mean_done decay_in par_in w_in0 w_in1 w_hi w_lo split_free groups_free credit act_out sq_ready stat_done "
                 "var_ready rstd_ready diag_ready rb_ready h_ready x_ready act_own dve_own "
                 "pool_own hid_ready perm_done aux_ready aux_free prod_ready scores_done probs_ready "
                 "pt_done pt_ready pv_done c_ready gates_done sig_ready exp_ready root_in root_ready "
                 "coef_ready relu_used pads_ready ha_ready qk_ready sm_ready ret_ready pool_in pool_out p_in wi_ready dots_done "
                 "relu_ready v_ready out_done cst_in").split()
        sem = {n: ctx.enter_context(nc.semaphore(n)) for n in names}
        numbers = range(min(x.num for x in sem.values()), max(x.num for x in sem.values()) + 1)
        assert len(numbers) == len(names)

        def clear_all():
            with nc.Block() as block:
                @block.gpsimd
                def _(pool):
                    pool.sem_clear(numbers)

        with nc.Block() as block:
            ang = sq[:, 0, 0:S]
            turns = sq[:, 0, S:512]
            posf = sq[:, 1, 0:S]
            posi = nc.alloc_sbuf_tensor_at("posi", [P, 2, S], i32, offset=hi_at)

            @block.sync
            def _(sp):
                sp.dma_start(cst[:, :], a["consts"]).then_inc(sem["cst_in"], 16)
                sp.dma_start(h[:, :, :], a["x"]).then_inc(sem["cst_in"], 16)
                sp.dma_start(posi[:, :, :], a["pos"]).then_inc(sem["cst_in"], 16)
                sp.wait_ge(sem["cst_in"], 48)
                for s in range(RING):
                    if s >= RAW:
                        sp.wait_ge(sem["w_lo"], s - RAW + 1)
                    sp.dma_start(raw[:, s % RAW, :], a["w"][s * P:(s + 1) * P, :]).then_inc(sem[f"w_in{s % RAW}"], 16)

            @block.gpsimd
            def _(pool):
                pool.memset(onesm[:, :], 1.0)
                pool.memset(half[:, :], -0.5)
                for n, width in enumerate((1024, 512, 256, 1)):
                    pool.memset(mcol[:, n:n + 1], 1.0 / width)

            @block.scalar
            def _(act):
                for s in range(RING):
                    act.wait_ge(sem[f"w_in{s % RAW}"], 16 * (s // RAW + 1))
                    act.activation(whi[:, s, :], raw[:, s % RAW, :], ACT.Copy).then_inc(sem["w_hi"], 1)
                for m, t in ((0, trig1), (1, trig2)):
                    act.wait_ge(sem["x_ready"], m + 1)
                    act.activation(t[:, 1, :], Y[:, 2 * m, :], ACT.Sin)
                    ins = act.activation(t[:, 0, :], Y[:, 2 * m + 1, :], ACT.Sin).then_inc(sem["act_out"], 1)

            @block.vector
            def _(dve):
                line = Line(dve, Count(sem["dve_own"]))
                do, settle = line.do, line.settle
                dve.wait_ge(sem["cst_in"], 48)
                c1 = 6.28125
                c2 = float(np.float32(np.floor((2 * math.pi - c1) * 2 ** 20) / 2 ** 20))
                c3 = float(np.float32(2 * math.pi - c1 - c2))
                magic = 12582912.0
                pi = float(np.nextafter(np.float32(math.pi), np.float32(0)))
                for m in range(2):
                    do(dve.tensor_copy(posf, posi[:, m, :]))
                    settle()
                    do(dve.tensor_scalar(ang, posf, cst[:, K["freq"] + m:K["freq"] + m + 1], None, ALU.mult))
                    settle()
                    do(dve.tensor_scalar(turns, ang, 1.0 / (2 * math.pi), magic, ALU.mult, ALU.add))
                    settle()
                    do(dve.tensor_scalar(turns, turns, -magic, None, ALU.add))
                    for c in (c1, c2, c3):
                        settle()
                        do(dve.scalar_tensor_tensor(ang, turns, -c, ang, ALU.mult, ALU.add))
                    settle()
                    do(dve.tensor_scalar(Y[:, 2 * m, :], ang, -pi, pi, ALU.max, ALU.min))
                    settle()
                    do(dve.scalar_tensor_tensor(posf, Y[:, 2 * m, :], -1.0, Y[:, 2 * m, :], ALU.mult, ALU.max))
                    settle()
                    do(dve.tensor_scalar(Y[:, 2 * m + 1, :], posf, -1.0, math.pi / 2, ALU.mult, ALU.add))
                    settle()
                    dve.memset(small[:, 0, 0:1], 0.0).then_inc(sem["x_ready"], 1)
                for s in range(RING):
                    dve.wait_ge(sem["w_hi"], s + 1)
                    dve.tensor_tensor(wlo[:, s, :], raw[:, s % RAW, :], whi[:, s, :].bitcast(f32),
                                      ALU.subtract).then_inc(sem["w_lo"], 1)
                dve.wait_ge(sem["act_out"], 2)
                dve.tensor_copy(trig2[:, 2, :], trig2[:, 0, :])
        clear_all()


        class Stream:

            def __init__(self, line, end, narrow=()):
                self.line, self.end, self.narrow = line, end, narrow
                self.hi_n, self.lo_n = Count(sem["w_hi"]), Count(sem["w_lo"])

            def width(self, s, i):
                return NARROW if i is None and s in self.narrow else CHUNK

            def hi(self, s, i=None):
                if i is None and s < RING:
                    return
                e, k, n = self.line.eng, 0 if i is None else i, self.width(s, i)
                e.wait_ge(sem[f"w_in{s % RAW}"], 16 * ((s - RING) // RAW + 1) + k * 32)
                e.wait_ge(sem["split_free"], s - RING + 1 + k * 4)
                self.line.do(e.activation(whi[:, s % RING, 0:n], raw[:, s % RAW, 0:n], ACT.Copy), self.hi_n)

            def lo(self, s, i=None):
                if i is None and s < RING:
                    return
                e, k, n = self.line.eng, 0 if i is None else i, self.width(s, i)
                e.wait_ge(sem["w_hi"], s - RING + 1 + k * 4)
                self.line.do(e.tensor_tensor(wlo[:, s % RING, 0:n], raw[:, s % RAW, 0:n],
                                             whi[:, s % RING, 0:n].bitcast(f32), ALU.subtract), self.lo_n)

        def used(e, s, i=None):
            e.wait_ge(sem["split_free"], s + 1 + (0 if i is None else i * 4))

        def load_stream(sp, base, L, spans, end):
            def one(s, i, width):
                k = 0 if i is None else i
                if s >= RING + RAW:
                    sp.wait_ge(sem["w_lo"], s - RAW - RING + 1 + k * 2)
                sp.dma_start(raw[:, s % RAW, 0:width],
                             a["w"][ds(L * (end * P) + (base + s + k * 2) * P, P), 0:width])\
                  .then_inc(sem[f"w_in{s % RAW}"], 16)
            for c0, c1, width in spans:
                first = c0
                if c0 == RING:
                    one(RING, None, width)
                    one(RING + 1, None, width)
                    first = RING + RAW
                if c1 - first > 4:
                    with sp.Fori(0, (c1 - first) // 2) as i:
                        one(first, i, width)
                        one(first + 1, i, width)
                else:
                    for s in range(first, c1):
                        one(s, None, width)

        class Tensor:
            def __init__(self, pe):
                self.pe = pe
                self.norms = self.pieces = 0

            def tile(self, out_, s, t, hi_, lo_, first, last):
                w_h, w_l = whi[:, s % RING, t * P:(t + 1) * P], wlo[:, s % RING, t * P:(t + 1) * P]
                self.pe.matmul(out_, w_h, hi_, start=first, stop=False)
                self.pe.matmul(out_, w_h, lo_, start=False, stop=False)
                return self.pe.matmul(out_, w_l, hi_, start=False, stop=last)

            def arrive(self, s, i=None, step=4):
                if i is not None or s >= RING:
                    self.pe.wait_ge(sem["w_lo"], s - RING + 1 + (0 if i is None else i * step))

            def bank(self, g, i=None, step=4):
                self.pe.wait_ge(sem["groups_free"], g + 1 + (0 if i is None else i * step))

            def pair(self, s, g, i=None, tok=(False, False), cols=(P, P), x=None):
                self.arrive(s, i)
                self.bank(g, i)
                for f in range(2):
                    if not tok[f]:
                        for kt in range(KT):
                            if x is not None and f == 0 and kt % 2 == 0:
                                self.pe.wait_ge(sem["x_ready"], x + kt // 2 + 1)
                            last = self.tile(main[:, g % 4, f * S:(f + 1) * S], s, f * KT + kt,
                                             xhi[:, kt, :], xlo[:, kt, :], kt == 0, kt == KT - 1)
                    else:
                        for t in range(2):
                            o = main[:, g % 4, f * S + t * P:f * S + t * P + cols[f]]
                            for kt in range(KT):
                                c = (f * KT + kt) * P
                                w_h, w_l = (w[:, s % RING, c:c + cols[f]] for w in (whi, wlo))
                                x_h, x_l = (z[:, kt, t * P:(t + 1) * P] for z in (xhi, xlo))
                                self.pe.matmul(o, x_h, w_h, start=kt == 0, stop=False)
                                self.pe.matmul(o, x_l, w_h, start=False, stop=False)
                                last = self.pe.matmul(o, x_h, w_l, start=False, stop=kt == KT - 1)
                last.then_inc(sem["split_free"], 1)

            def from_units(self, s, g, hi_, lo_, base):
                self.arrive(s)
                self.bank(g)
                for f in range(2):
                    for kt in range(KT):
                        last = self.tile(main[:, g % 4, f * S:(f + 1) * S], s, f * KT + kt,
                                         hi_[:, base + kt, :], lo_[:, base + kt, :], kt == 0, kt == KT - 1)
                last.then_inc(sem["split_free"], 1)

            def long(self, c0, g0, groups, tiles, per):
                with self.pe.Fori(0, groups) as i:
                    assert g0 % 4 == 0 and groups <= 4
                    self.bank(g0, i, 1)
                    for f in range(2):
                        for c in range(per):
                            n = f * per + c
                            s = c0 + n
                            self.arrive(s, i, 2 * per)
                            for t in range(tiles):
                                last = self.tile(
                                    main[:, ds(i, 1), f * S:(f + 1) * S].rearrange("p a n -> p (a n)"),
                                    s, t, bhi[:, c * tiles + t, :], blo[:, c * tiles + t, :],
                                    c == 0 and t == 0, c == per - 1 and t == tiles - 1)
                            last.then_inc(sem["split_free"], 1)

            def stats(self, pieces, col, src=None, y=False):
                if self.norms:
                    self.pe.wait_ge(sem["var_ready"], self.norms)
                for p in range(pieces):
                    if src is None:
                        self.pe.wait_ge(sem["sq_ready"], self.pieces + p + 1)
                    for k in range(2):
                        for t in range(2):
                            x = sqy[:, p, :] if y else sq[:, (self.pieces + p) % 2, :] if src is None else src
                            last = self.pe.matmul(stat[:, t:t + 1], x[:, k * S + t * P:k * S + (t + 1) * P],
                                                  mcol[:, col:col + 1], start=(p == 0 and k == 0 and t == 0),
                                                  stop=(p == pieces - 1 and k == 1), skip_group_check=True)
                    last.then_inc(sem["stat_done" if src is None else "mean_done"], 1)
                self.pieces += pieces if src is None else 0
                self.norms += 1

            def spread(self):
                self.pe.wait_ge(sem["diag_ready"], self.norms)
                self.pe.matmul(rb, onesm[:, :], diag[:, :, :].rearrange("p a b -> p (a b)"),
                               start=True, stop=True).then_inc(sem["rb_ready"], 1)

        class Scalar:
            def __init__(self, act, end, narrow=()):
                self.line = Line(act, Count(sem["act_own"]))
                self.act, self.do, self.settle = act, self.line.do, self.line.settle
                self.w = Stream(self.line, end, narrow)
                self.outs, self.sqs = Count(sem["act_out"]), Count(sem["sq_ready"])
                self.gained, self.rounded = Count(sem["gain_ready"]), Count(sem["round_ready"])
                self.h_seen = 0

            def gains(self, dst, src, p, par, gain):
                for kt in (2 * p, 2 * p + 1):
                    self.do(self.act.activation(dst[:, kt, :], src[:, kt, :], ACT.Copy,
                                                scale=par[:, gain + kt:gain + kt + 1]),
                            self.gained if kt % 2 else None)

            def product_out(self, c0, g0, per, par, gain):
                for p in range(4):
                    last_one = p == 3
                    for c in range(per):
                        if not (last_one and c == per - 1):
                            self.w.hi(c0 + p * per + c + 3)
                    self.act.wait_ge(sem["groups_free"], g0 + p + 5)
                    self.squares_y(p)
                    self.settle()
                    self.gains(Y, Y, p, par, gain)
                    if last_one:
                        self.w.hi(c0 + 4 * per + 2)

            def h_in(self, par, gain, wait=True):
                for p in range(4):
                    if wait:
                        self.act.wait_ge(sem["h_ready"], self.h_seen + p + 1)
                    self.squares(two(h, 2 * p), p)
                    self.gains(HG, h, p, par, gain)
                self.h_seen += 4 if wait else 0

            def round_x(self):
                for p in range(4):
                    self.act.wait_ge(sem["xf_ready"], self.rounded.n + 1)
                    self.do(self.act.activation(two(xhi, 2 * p), tX[:, p % 2, :], ACT.Copy), self.rounded)

            def squares_y(self, p):
                self.do(self.act.activation(sqy[:, p, :], two(Y, 2 * p), ACT.Square), self.sqs)

            def squares(self, src, p):
                if self.sqs.n >= 2:
                    self.act.wait_ge(sem["stat_done"], self.sqs.n - 1)
                self.do(self.act.activation(sq[:, self.sqs.n % 2, :], src, ACT.Square), self.sqs)

            def hs(self, s0, s1):
                for s in range(s0, s1):
                    self.w.hi(s)

        class Vector:
            def __init__(self, dve, end, narrow=()):
                self.line = Line(dve, Count(sem["dve_own"]))
                self.dve, self.do, self.settle = dve, self.line.do, self.line.settle
                self.w = Stream(self.line, end, narrow)
                self.free = Count(sem["groups_free"])
                self.vars, self.diags = Count(sem["var_ready"]), Count(sem["diag_ready"])
                self.xs, self.hs, self.xfs = Count(sem["x_ready"]), Count(sem["h_ready"]), Count(sem["xf_ready"])
                self.gained = 0
                self.stats = self.roots = self.took = 0

            def credits(self):
                self.do(self.dve.memset(small[:, 0, 1:2], 0.0), self.free, by=4)

            def factor(self, pieces, eps=EPS, scale=1.0, mean=False):
                if mean:
                    self.dve.wait_ge(sem["mean_done"], 1)
                else:
                    self.stats += pieces
                    self.dve.wait_ge(sem["stat_done"], self.stats)
                self.settle()
                if mean:
                    self.do(self.dve.tensor_copy(rstd[:, :], stat), self.vars)
                    self.settle()
                else:
                    self.do(self.dve.tensor_scalar(var[:, :], stat, eps, None, ALU.add), self.vars)
                    self.roots += 1
                    self.dve.wait_ge(sem["rstd_ready"], self.roots)
                for t in range(2):
                    ins = self.dve.tensor_scalar(diag[:, t, :], ident, rstd[:, t:t + 1], scale, ALU.mult, ALU.mult)
                    self.do(ins, self.diags if t else None)

            def spread_done(self):
                self.dve.wait_ge(sem["rb_ready"], self.diags.n)

            def split(self, hi_, lo_, src, count, by=1):
                self.settle()
                self.do(self.dve.tensor_copy(hi_, src))
                self.settle()
                self.do(self.dve.tensor_tensor(lo_, src, hi_.bitcast(f32), ALU.subtract), count, by)

            def post_norm(self, scale=1.0):
                self.factor(4, scale=scale)
                self.spread_done()
                rb2 = over(rb.unsqueeze(1), 2)

                def scaled(p):
                    self.dve.wait_ge(sem["gain_ready"], self.gained + p + 1)
                    return self.do(self.dve.tensor_tensor(units(tX[:, p % 2, :]), Y[:, 2 * p:2 * p + 2, :], rb2, ALU.mult))

                self.settle()
                n = scaled(0)
                for p in range(4):
                    self.dve.wait_ge(sem["dve_own"], n)
                    if p >= 1:
                        self.dve.wait_ge(sem["h_ready"], self.hs.n)
                    if p < 3:
                        n = scaled(p + 1)
                    self.do(self.dve.tensor_tensor(two(h, 2 * p), two(h, 2 * p), tX[:, p % 2, :], ALU.add), self.hs)
                self.gained += 4

            def pre_norm(self):
                self.factor(4)
                self.spread_done()
                rb2 = over(rb.unsqueeze(1), 2)
                base = self.xfs.n

                def scaled(p):
                    self.dve.wait_ge(sem["gain_ready"], self.gained + p + 1)
                    self.do(self.dve.tensor_tensor(units(tX[:, p % 2, :]), HG[:, 2 * p:2 * p + 2, :], rb2, ALU.mult), self.xfs)

                self.settle()
                scaled(0)
                scaled(1)
                for p in range(4):
                    self.dve.wait_ge(sem["round_ready"], base + p + 1)
                    self.dve.wait_ge(sem["xf_ready"], base + min(p + 2, 4))
                    self.do(self.dve.tensor_tensor(two(xlo, 2 * p), tX[:, p % 2, :], two(xhi, 2 * p).bitcast(f32),
                                                   ALU.subtract), self.xs)
                    if p < 2:
                        self.settle()
                        scaled(p + 2)
                self.gained += 4

            def copy_out(self, dst, g, count=None):
                self.settle()
                self.do(self.dve.tensor_copy(dst, main[:, g % 4, :]), self.free)

            def product_out(self, c0, g0, per):
                for p in range(4):
                    for c in range(per):
                        if not (p == 3 and c == per - 1):
                            self.w.lo(c0 + p * per + c + 3)
                    used(self.dve, c0 + p * per + per - 1)
                    self.copy_out(two(Y, 2 * p), g0 + p)
                self.w.lo(c0 + 4 * per + 2)

        def two(t, u):
            return t[:, u:u + 2, :].rearrange("p a n -> p (a n)")

        def wide(t, u=0, n=8):
            return t[:, u:u + n, :].rearrange("p a n -> p (a n)")

        def over(t, n):
            return t.broadcast_to([P, n, S])

        def units(t):
            return t.rearrange("p (a n) -> p a n", n=S)

        def roots(pool, values):
            for v in values:
                pool.wait_ge(sem["var_ready"], v)
                pool.tensor_tensor(rstd[:, :], var[:, :], half[:, :], ALU.pow).then_inc(sem["rstd_ready"], 1)

        with nc.Fori(0, LAYERS) as L:
            with nc.Block() as block:
                @block.sync
                def _(sp):
                    load_stream(sp, 0, L, [(RING, C1["end"] + RING, CHUNK)], C1["end"])

                @block.gpsimd
                def _(pool):
                    line = Line(pool, Count(sem["pool_own"]))
                    do, settle = line.do, line.settle
                    pool.memset(VP[:, :, :, :], 0.0)
                    pool.memset(YC[:, :, 0:TAPS - 1], 0.0)
                    pool.memset(W2[:, :, :], 0.0)
                    pool.memset(W4[:, :, :], 0.0)
                    pool.memset(UP[:, :, 0:16], 0.0).then_inc(sem["pads_ready"], 1)
                    roots(pool, [1])
                    pool.wait_ge(sem["pads_ready"], 1)
                    pool.wait_ge(sem["pool_in"], 1)
                    end = 16 + S
                    do(pool.tensor_tensor(W2[:, :, 1:end], UP[:, :, 1:end], UP[:, :, 0:end - 1], ALU.add))
                    settle()
                    do(pool.tensor_tensor(W4[:, :, 3:end], W2[:, :, 3:end], W2[:, :, 1:end - 2], ALU.add))
                    settle()
                    do(pool.tensor_tensor(W2[:, 1, 7:end], W4[:, 1, 7:end], W4[:, 1, 3:end - 4], ALU.add))
                    settle()
                    do(pool.tensor_tensor(W4[:, 1, 15:end], W2[:, 1, 15:end], W2[:, 1, 7:end - 8], ALU.add))
                    settle()
                    for f in range(2):
                        rc = cst[:, K["rcount"] + f * S:K["rcount"] + (f + 1) * S]
                        for lo_p, w in ((0, W2), (64, W4)):
                            do(pool.tensor_tensor(PO[lo_p:lo_p + 64, f, :], w[lo_p:lo_p + 64, f, 16:end],
                                                  rc[lo_p:lo_p + 64, :], ALU.mult))
                    settle()
                    pool.tensor_tensor(PO[:, :, :], PO[:, :, :], UP[:, :, 16:end], ALU.subtract).then_inc(sem["pool_out"], 1)
                    roots(pool, [3, 4, 5, 6])

                @block.scalar
                def _(act):
                    cut = P1["conv_pw"]
                    act.dma_start(par1[:, 0:cut], a["par1"][ds(L * P, P), 0:cut]).then_inc(sem["par_in"], 16)
                    act.dma_start(par1[:, cut:], a["par1"][ds(L * P, P), cut:P1["end"]]).then_inc(sem["big_par_in"], 16)
                    act.dma_start(PT[:, :, :].rearrange("p a n -> p (a n)"), a["p"][ds(L * P, P), :]).then_inc(sem["p_in"], 16)
                    A = Scalar(act, C1["end"])
                    do, settle, w = A.do, A.settle, A.w
                    act.wait_ge(sem["par_in"], 16)
                    A.h_in(par1, P1["mix_pre"], wait=False)
                    A.round_x()

                    def relus(p):
                        for hd in range(4 * p, 4 * p + 4):
                            act.wait_ge(sem["dots_done"], hd + 1)
                            if hd >= 2:
                                act.wait_ge(sem["relu_used"], hd - 1)
                            act.activation(sm[:, hd % 2, :], aux[2 + hd % 2][:, 0:RSPAN], ACT.Relu)\
                               .then_inc(sem["relu_ready"], 1)

                    for s in range(11):
                        w.hi(s + 3)
                        if 6 <= s <= 9:
                            relus(s - 6)
                        used(act, s)
                        if s >= 2 and s < 10:
                            act.wait_ge(sem["perm_done"], s - 1)
                        if s < 8:
                            n = S if s < 2 else 2 * S
                            do(act.activation(tS[:, s % 2, 0:n], main[:, s % 4, 0:n], ACT.Copy), A.outs)
                        elif s < 10:
                            do(act.activation(tS[:, s % 2, 0:S], main[:, s % 4, S:2 * S], ACT.Sigmoid), A.outs)

                    exps_n = Count(sem["exp_ready"])

                    def exps(hh):
                        act.wait_ge(sem["sm_ready"], hh + 1)
                        for t, (c0, c1) in enumerate(((0, P), (P, RSPAN))):
                            do(act.activation(sm[:, hh % 2, c0:c1], sm[:, hh % 2, c0:c1], ACT.Exp,
                                              bias=rmax[:, hh, t:t + 1], accum_out=rsum[:, hh, t:t + 1]),
                               exps_n if t else None)

                    def turned(hh):
                        act.wait_ge(sem["pt_done"], hh + 1)
                        if hh >= 2:
                            act.wait_ge(sem["pv_done"], hh - 1)
                        act.activation(work[:, hh % 2, :], aux[1][:, 0:RSPAN], ACT.Copy).then_inc(sem["pt_ready"], 1)

                    exps(0)
                    for hh in range(HEADS):
                        if hh + 1 < HEADS:
                            exps(hh + 1)
                        turned(hh)

                    act.wait_ge(sem["c_ready"], 2)
                    A.squares(two(cacc, 0), 0)
                    act.wait_ge(sem["c_ready"], 3)
                    for f in range(2):
                        ins = act.activation(cact[:, f, :], cacc[:, f, :], ACT.Silu,
                                             bias=par1[:, P1["ln_b"] + f:P1["ln_b"] + f + 1],
                                             scale=par1[:, P1["ln_g"] + f:P1["ln_g"] + f + 1])
                    ins.then_inc(sem["sig_ready"], 1)

                    A.product_out(C1["out"], G1["out"], 1, par1, P1["mix_post"])
                    A.h_in(par1, P1["mlp_pre"])
                    A.round_x()
                    with A.line.loop(4, [(w.hi_n, 4), (A.outs, 4), (A.line.own, 4)], A.outs) as i:
                        for j in range(4):
                            s, g = C1["up"] + j, G1["up"] + j
                            w.hi(s + 3, i)
                            used(act, s, i)
                            act.wait_ge(sem["groups_free"], g + 3 + i * 4)
                            do(act.activation(tS[:, j % 2, :], main[:, j, :], ACT.Relu))
                            settle()
                            do(act.activation(tX[:, j % 2, :], tS[:, j % 2, :], ACT.Square), A.outs)
                    A.product_out(C1["down"], G1["down"], 4, par1, P1["mlp_post"])
                    for p in range(4):
                        s = C1["gate"] + p
                        w.hi(s + 3)
                        used(act, s)
                        do(act.activation(two(GATE, 2 * p), main[:, p, :], ACT.Sigmoid), A.outs)
                    w.hi(C1["end"] + 2)
                    w.hi(C1["end"] + 3)

                @block.vector
                def _(dve):
                    V1 = Vector(dve, C1["end"])
                    do, settle, w = V1.do, V1.settle, V1.w
                    qk, sms, prods, cs = (Count(sem[n]) for n in ("qk_ready", "sm_ready", "prod_ready", "c_ready"))
                    V1.credits()
                    dve.wait_ge(sem["par_in"], 16)
                    V1.pre_norm()
                    dve.wait_ge(sem["p_in"], 16)
                    do(dve.tensor_copy(acc[:, 0:P], tri))
                    do(dve.memset(acc[:, P:2 * P], 0.0))
                    do(dve.tensor_copy(acc[:, 2 * P:3 * P], tri))
                    dve.wait_ge(sem["pads_ready"], 1)
                    cos, sin = trig1[:, 0:1, :], trig1[:, 1:2, :]
                    rope_to = {0: (KI, 0, 1), 1: (KR, 0, 1)}
                    for p in range(4):
                        rope_to[2 + p] = (QI, 2 * p, 2)
                    for p in range(2):
                        rope_to[6 + p] = (Q, 2 * p, 2)

                    def rope_finish(s):
                        t, u, n = rope_to[s]
                        dve.wait_ge(sem["perm_done"], s + 1)
                        settle()
                        do(dve.tensor_tensor(units(tX[:, s % 2, 0:n * S]), units(aux[1][:, 0:n * S]),
                                             over(sin, n), ALU.mult), aux_free)
                        settle()
                        do(dve.tensor_tensor(t[:, u:u + n, :], t[:, u:u + n, :], units(tX[:, s % 2, 0:n * S]),
                                             ALU.add), qk)

                    aux_free = Count(sem["aux_free"])
                    reads = Count(sem["relu_used"])

                    def index_sum(p):
                        for hd in range(4 * p, 4 * p + 4):
                            dve.wait_ge(sem["relu_ready"], hd + 1)
                            settle()
                            for t, (c0, c1) in enumerate(((0, P), (P, RSPAN))):
                                do(dve.scalar_tensor_tensor(acc[:, c0:c1], sm[:, hd % 2, c0:c1],
                                                            wi[:, t, hd:hd + 1], acc[:, c0:c1],
                                                            ALU.mult, ALU.add), reads if t else None)

                    for s in range(11):
                        w.lo(s + 3)
                        if 2 <= s <= 9:
                            rope_finish(s - 2)
                        if 6 <= s <= 9:
                            index_sum(s - 6)
                        bank = main[:, s % 4, :]
                        if s < 10:
                            dve.wait_ge(sem["act_out"], s + 1)
                        else:
                            used(dve, s)
                        settle()
                        if s < 8:
                            t, u, n = rope_to[s]
                            if s == 0:
                                wts = bank[:, S:2 * S].rearrange("p (t c) -> p t c", t=2)[:, :, 0:IDX_HEADS]
                                do(dve.tensor_scalar(wi[:, :, :], wts, 1.0 / 32, None, ALU.mult))
                            if s == 1:
                                vs = bank[:, S:2 * S].rearrange("p (t c) -> p t c", t=2)
                                for kv in range(2):
                                    do(dve.tensor_copy(VP[:, kv, :, kv * 64:kv * 64 + 64], vs[:, :, kv * 64:kv * 64 + 64]))
                            do(dve.tensor_tensor(t[:, u:u + n, :], units(bank[:, 0:n * S]), over(cos, n), ALU.mult), V1.free)
                        elif s < 10:
                            do(dve.tensor_tensor(YC[:, s - 8, TAPS - 1:], bank[:, 0:S], tS[:, s % 2, 0:S], ALU.mult), V1.free)
                        else:
                            do(dve.tensor_copy(UP[:, :, 16:], units(bank)), V1.free, by=2)
                            settle()
                            dve.memset(small[:, 0, 2:3], 0.0).then_inc(sem["pool_in"], 1)

                    spans = ((0, P), (P, RSPAN))
                    cur = acc[:, :]
                    for r in range(TOPK // 8):
                        nxt = work[:, r % 2, :]
                        settle()
                        for t, (c0, c1) in enumerate(spans):
                            do(dve.max(best[:, t, :], cur[:, c0:c1]))
                        settle()
                        for t, (c0, c1) in enumerate(spans):
                            do(dve.match_replace(nxt[:, c0:c1], best[:, t, :], cur[:, c0:c1], TAKEN))
                        cur = nxt
                    settle()
                    do(dve.tensor_scalar(bias[:, :], cur, TAKEN, OFF, ALU.not_equal, ALU.mult))
                    settle()
                    do(dve.tensor_tensor(bias[:, 0:P], bias[:, 0:P], tri, ALU.add))
                    do(dve.tensor_tensor(bias[:, 2 * P:], bias[:, 2 * P:], tri, ALU.add))

                    def masked(hh):
                        dve.wait_ge(sem["scores_done"], hh + 1)
                        settle()
                        do(dve.scalar_tensor_tensor(sm[:, hh % 2, :], aux[2 + hh % 2][:, 0:RSPAN], 0.125, bias[:, :],
                                                    ALU.mult, ALU.add))
                        settle()
                        for t, (c0, c1) in enumerate(spans):
                            do(dve.tensor_reduce(rmax[:, hh, t:t + 1], sm[:, hh % 2, c0:c1], AX.X, ALU.max,
                                                 negate=True), sms if t else None)

                    probs = Count(sem["probs_ready"])

                    def normed(hh):
                        dve.wait_ge(sem["exp_ready"], hh + 1)
                        if hh >= 2:
                            dve.wait_ge(sem["pt_done"], hh - 1)
                        do(dve.reciprocal(rinv[:, hh, :], rsum[:, hh, :]))
                        settle()
                        for t, (c0, c1) in enumerate(spans):
                            do(dve.tensor_scalar(pt[:, hh % 2, c0:c1], sm[:, hh % 2, c0:c1],
                                                 rinv[:, hh, t:t + 1], None, ALU.mult), probs if t else None)

                    def attended(f):
                        dve.wait_ge(sem["pv_done"], 2 * f + 2)
                        V1.split(bhi[:, f, :], blo[:, f, :], main[:, f, 0:S], prods)

                    masked(0)
                    for hh in range(HEADS):
                        if hh + 1 < HEADS:
                            masked(hh + 1)
                        normed(hh)
                        if hh % 2 and hh > 1:
                            attended(hh // 2 - 1)
                    attended(HEADS // 2 - 1)

                    for k in range(TAPS):
                        settle()
                        for f in range(2):
                            src_ = YC[:, f, k:k + S]
                            wk = par1[:, P1["dw"] + f * TAPS + k:P1["dw"] + f * TAPS + k + 1]
                            count = cs if k == TAPS - 1 and f else None
                            if k == 0:
                                do(dve.tensor_scalar(cacc[:, f, :], src_, wk,
                                                     par1[:, P1["conv_b"] + f:P1["conv_b"] + f + 1],
                                                     ALU.mult, ALU.add), count)
                            else:
                                do(dve.scalar_tensor_tensor(cacc[:, f, :], src_, wk, cacc[:, f, :],
                                                            ALU.mult, ALU.add), count)
                    V1.factor(1, mean=True)
                    V1.spread_done()
                    settle()
                    do(dve.tensor_tensor(cacc[:, :, :], cacc[:, :, :], over(rb.unsqueeze(1), 2), ALU.subtract), cs)
                    V1.factor(1, eps=LN_EPS)
                    V1.spread_done()
                    settle()
                    do(dve.tensor_tensor(cacc[:, :, :], cacc[:, :, :], over(rb.unsqueeze(1), 2), ALU.mult), cs)
                    dve.wait_ge(sem["aux_ready"], 1)
                    for f in range(2):
                        do(dve.tensor_scalar(tX[:, 0, f * S:(f + 1) * S], aux[2][:, f * S:(f + 1) * S],
                                             par1[:, P1["pool_scale"] + f:P1["pool_scale"] + f + 1], None, ALU.mult))
                    V1.split(two(bhi, 6), two(blo, 6), tX[:, 0, :], prods)
                    dve.wait_ge(sem["aux_ready"], 2)
                    V1.split(two(bhi, 4), two(blo, 4), aux[3][:, :], prods)

                    V1.product_out(C1["out"], G1["out"], 1)
                    V1.post_norm()
                    V1.pre_norm()
                    settle()
                    with V1.line.loop(4, [(w.lo_n, 4), (V1.free, 4), (V1.line.own, 4)], V1.free) as i:
                        for j in range(4):
                            s = C1["up"] + j
                            w.lo(s + 3, i)
                            dve.wait_ge(sem["act_out"], 10 + j + 1 + i * 4)
                            settle()
                            uh = bhi[:, ds(i * 8 + 2 * j, 2), :]
                            ul = blo[:, ds(i * 8 + 2 * j, 2), :]
                            do(dve.tensor_copy(uh, units(tX[:, j % 2, :])))
                            settle()
                            do(dve.tensor_tensor(ul, units(tX[:, j % 2, :]), uh.bitcast(f32), ALU.subtract), V1.free)
                    V1.product_out(C1["down"], G1["down"], 4)
                    V1.post_norm()
                    for p in range(4):
                        V1.split(two(xhi, 2 * p), two(xlo, 2 * p), two(h, 2 * p), V1.xs)
                    V1.split(two(pthi, 0), two(ptlo, 0), two(PT, 0), V1.xs)
                    for p in range(4):
                        w.lo(C1["gate"] + p + 3)
                        dve.wait_ge(sem["act_out"], 26 + p + 1)
                        do(dve.memset(small[:, 6, p:p + 1], 0.0), V1.free)
                    w.lo(C1["ple"] + 3)
                    used(dve, C1["ple"])
                    for p in range(4):
                        settle()
                        do(dve.tensor_tensor(tX[:, p % 2, :], main[:, p, :], two(GATE, 2 * p), ALU.mult), V1.free)
                        settle()
                        do(dve.tensor_tensor(two(h, 2 * p), two(h, 2 * p), tX[:, p % 2, :], ALU.add))
                    w.lo(C1["end"] + 3)

                @block.tensor
                def _(pe):
                    T = Tensor(pe)
                    T.stats(4, 0)
                    T.spread()

                    def swap_rows(s):
                        n = S if s < 2 else 2 * S
                        pe.wait_ge(sem["act_out"], s + 1)
                        if s:
                            pe.wait_ge(sem["aux_free"], s)
                        pe.matmul(aux[1][:, 0:n], swap, tS[:, s % 2, 0:n], start=True, stop=True).then_inc(sem["perm_done"], 1)

                    def pairs(out_, q_, k_, off):
                        pe.matmul(out_[:, 0:P], q_[off:off + 64, 0:P], k_[off:off + 64, 0:P], start=True, stop=True)
                        return pe.matmul(out_[:, P:RSPAN], q_[off:off + 64, P:S], k_[off:off + 64, :], start=True, stop=True)

                    def dots(p):
                        pe.wait_ge(sem["qk_ready"], 3 + p)
                        for hd in range(4 * p, 4 * p + 4):
                            if hd >= 2:
                                pe.wait_ge(sem["relu_ready"], hd - 1)
                            pairs(aux[2 + hd % 2], QI[:, hd // 2, :], KI[:, 0, :], 64 * (hd % 2)).then_inc(sem["dots_done"], 1)

                    for s in range(11):
                        T.pair(s, s, tok=(False, s < 2), cols=(P, IDX_HEADS if s == 0 else P),
                               x=0 if s == 0 else None)
                        if 1 <= s <= 8:
                            swap_rows(s - 1)
                        if 5 <= s <= 8:
                            dots(s - 5)

                    def scores(hh):
                        if hh < 2:
                            pe.wait_ge(sem["relu_ready"], IDX_HEADS)
                            pe.wait_ge(sem["qk_ready"], 8)
                        else:
                            pe.wait_ge(sem["sm_ready"], hh - 1)
                        pairs(aux[2 + hh % 2], Q[:, hh // 2, :], KR[:, 0, :], 64 * (hh % 2)).then_inc(sem["scores_done"], 1)

                    def turn(hh):
                        pe.wait_ge(sem["probs_ready"], hh + 1)
                        if hh:
                            pe.wait_ge(sem["pt_ready"], hh)
                        for n in range(3):
                            last = pe.transpose(aux[1][:, n * P:(n + 1) * P], pt[:, hh % 2, n * P:(n + 1) * P], ident)
                        last.then_inc(sem["pt_done"], 1)

                    def mix_values(hh):
                        f, kv = hh // 2, hh % 2
                        pe.wait_ge(sem["pt_ready"], hh + 1)
                        o = main[:, f, 0:S]
                        pe.matmul(o, VP[:, kv, 0, :], work[:, hh % 2, 0:S], start=kv == 0, stop=kv == 1,
                                  skip_group_check=True)
                        pe.matmul(o[:, P:S], VP[:, kv, 1, :], work[:, hh % 2, S:RSPAN], start=False,
                                  stop=kv == 1, skip_group_check=True).then_inc(sem["pv_done"], 1)

                    pe.wait_ge(sem["groups_free"], 4 + 12)
                    scores(0)
                    scores(1)
                    for hh in range(HEADS):
                        turn(hh)
                        if hh + 2 < HEADS:
                            scores(hh + 2)
                        if hh:
                            mix_values(hh - 1)
                    mix_values(HEADS - 1)

                    pe.wait_ge(sem["c_ready"], 1)
                    T.stats(1, 2, src=cacc[:, :, :].rearrange("p a n -> p (a n)"))
                    T.spread()
                    T.stats(1, 2)
                    T.spread()
                    pe.wait_ge(sem["big_par_in"], 16)
                    pe.wait_ge(sem["pool_out"], 1)
                    for f in range(2):
                        last = pe.matmul(aux[2][:, f * S:(f + 1) * S],
                                         par1[:, P1["pool_w"] + f * P:P1["pool_w"] + (f + 1) * P], PO[:, f, :],
                                         start=True, stop=True)
                    last.then_inc(sem["aux_ready"], 1)
                    pe.wait_ge(sem["sig_ready"], 1)
                    for f in range(2):
                        for k in range(2):
                            c = P1["conv_pw"] + (k * 2 + f) * P
                            last = pe.matmul(aux[3][:, f * S:(f + 1) * S], par1[:, c:c + P], cact[:, k, :],
                                             start=k == 0, stop=k == 1)
                    last.then_inc(sem["aux_ready"], 1)

                    pe.wait_ge(sem["prod_ready"], 6)
                    for p in range(4):
                        T.from_units(C1["out"] + p, G1["out"] + p, bhi, blo, 0)
                    T.stats(4, 0, y=True)
                    T.spread()
                    T.stats(4, 0)
                    T.spread()
                    for j in range(4):
                        T.pair(C1["up"] + j, G1["up"] + j, x=4 if j == 0 else None)
                    with pe.Fori(0, 3) as i:
                        for j in range(4):
                            T.pair(C1["up"] + 4 + j, G1["up"] + 4 + j, i)
                    pe.wait_ge(sem["groups_free"], 4 + 32)
                    T.long(C1["down"], G1["down"], 4, 16, 2)
                    T.stats(4, 0, y=True)
                    T.spread()
                    for p in range(4):
                        T.pair(C1["gate"] + p, G1["gate"] + p, x=8 if p == 0 else None)
                    pe.wait_ge(sem["x_ready"], 13)
                    T.arrive(C1["ple"])
                    for g in range(4):
                        T.bank(G1["ple"] + g)
                        for f in range(2):
                            for k in range(2):
                                last = T.tile(main[:, g, f * S:(f + 1) * S], C1["ple"], (2 * g + f) * 2 + k,
                                              pthi[:, k, :], ptlo[:, k, :], k == 0, k == 1)
                    last.then_inc(sem["split_free"], 1)
            clear_all()

        with nc.Fori(0, LAYERS) as L:
            with nc.Block() as block:
                narrow = {*range(22, 38), *range(136, 152)}

                @block.sync
                def _(sp):
                    load_stream(sp, LAYERS * C1["end"], L, [(RING, 22, CHUNK), (22, 38, NARROW), (38, 136, CHUNK),
                                                            (136, 152, NARROW), (152, 156, CHUNK)], C2["end"])

                @block.gpsimd
                def _(pool):
                    pool.memset(XA[:, :, 0:3], 0.0).then_inc(sem["pads_ready"], 1)
                    roots(pool, range(1, 11))

                @block.scalar
                def _(act):
                    cut = P2["w_a"]
                    act.dma_start(par2[:, 0:cut], a["par2"][ds(L * P, P), 0:cut]).then_inc(sem["par_in"], 16)
                    act.dma_start(par2[:, cut:], a["par2"][ds(L * P, P), cut:P2["end"]]).then_inc(sem["big_par_in"], 16)
                    A = Scalar(act, C2["end"], narrow)
                    do, settle, w = A.do, A.settle, A.w
                    act.wait_ge(sem["par_in"], 16)
                    A.h_in(par2, P2["f1_pre"], wait=False)
                    A.round_x()
                    act.wait_ge(sem["root_in"], 1)
                    act.activation(small[:, 2, :], small[:, 1, :], ACT.Exp, scale=-1.0).then_inc(sem["root_ready"], 1)

                    def gates_in(c0, g0, first):
                        def one(j, i=None):
                            s, g = c0 + j, g0 + j
                            w.hi(s + 3, i)
                            used(act, s, i)
                            act.wait_ge(sem["groups_free"], g + 3 + (0 if i is None else i * 4))
                            do(act.activation(tS[:, j % 2, 0:S], main[:, j % 4, 0:S], ACT.Silu), A.outs)
                        for j in range(4):
                            one(j)
                        with A.line.loop(4, [(w.hi_n, 4), (A.outs, 4)], A.outs) as i:
                            for j in range(4):
                                one(4 + j, i)
                        one(20)
                        one(21)

                    def evac(s, g, func):
                        used(act, s)
                        act.wait_ge(sem["groups_free"], g + 3)
                        do(act.activation(tS[:, g % 2, :], main[:, g % 4, :], func), A.outs)

                    gates_in(C2["f1in"], G2["f1in"], 0)
                    A.product_out(C2["f1out"], G2["f1out"], 4, par2, P2["f1_post"])
                    A.h_in(par2, P2["mix_pre"])
                    A.round_x()
                    act.wait_ge(sem["coef_ready"], 1)

                    def sigmoids(p):
                        for f in (2 * p, 2 * p + 1):
                            act.wait_ge(sem["gates_done"], f + 1)
                            bank = aux[1 + f % 2]
                            act.activation(Rg[:, f, :], bank[:, 0:S], ACT.Sigmoid,
                                           bias=par2[:, P2["b_a"] + f:P2["b_a"] + f + 1])
                            do(act.activation(Ig[:, f, :], bank[:, S:2 * S], ACT.Sigmoid,
                                              bias=par2[:, P2["b_x"] + f:P2["b_x"] + f + 1]), sigs)

                    def decays(half_):
                        settle()
                        for f in range(4 * half_, 4 * half_ + 4):
                            do(act.activation(Ag[:, f, :], Rg[:, f, :], ACT.Exp, scale=small[:, 7, f:f + 1]))
                        settle()
                        for f in range(4 * half_, 4 * half_ + 4):
                            do(act.activation(Rg[:, f, :], Rg[:, f, :], ACT.Tanh, scale=small[:, 7, f:f + 1]),
                               exps if f % 4 == 3 else None)

                    def retained(hd):
                        act.wait_ge(sem["pv_done"], hd + 1)
                        if hd == 0:
                            act.wait_ge(sem["ha_ready"], 2)
                        for n in range(2):
                            do(act.activation(two(RET, 4 * hd + 2 * n), aux[2 + n][:, :], ACT.Copy), rets)
                            A.squares(aux[2 + n][:, :], n)

                    sigs, exps, rets = (Count(sem[n]) for n in ("sig_ready", "exp_ready", "ret_ready"))
                    for s in range(C2["xa"], C2["mix"]):
                        w.hi(s + 3)
                        if 41 <= s <= 44:
                            sigmoids(s - 41)
                        if s in (45, 46):
                            decays(s - 45)
                        if s == 46:
                            act.wait_ge(sem["gates_done"], 8)
                            act.dma_start(DEC[:, :], a["decay"]).then_inc(sem["decay_in"], 16)
                        if s == 49:
                            act.wait_ge(sem["root_in"], 2)
                            act.activation(wide(Rg), wide(Rg), ACT.Sqrt, scale=-1.0).then_inc(sem["root_ready"], 1)
                        if s in (53, 55, 57, 59):
                            retained((s - 53) // 2)
                        for name, func in (("ya", ACT.Gelu_apprx_tanh), ("ga", ACT.Sigmoid), ("gb", ACT.Sigmoid),
                                           ("gc", ACT.Sigmoid), ("g", ACT.Silu)):
                            n = 8 if name == "g" else 4
                            if C2[name] <= s < C2[name] + n:
                                evac(s, G2[name] + s - C2[name], func)
                    A.product_out(C2["mix"], G2["mix"], 1, par2, P2["mix_post"])
                    A.h_in(par2, P2["f2_pre"])
                    A.round_x()
                    gates_in(C2["f2in"], G2["f2in"], 46)
                    A.product_out(C2["f2out"], G2["f2out"], 4, par2, P2["f2_post"])
                    w.hi(C2["end"] + 3)

                @block.vector
                def _(dve):
                    V2 = Vector(dve, C2["end"], narrow)
                    do, settle, w = V2.do, V2.settle, V2.w
                    qk, sms, prods, cs, has, roots_in = (
                        Count(sem[n]) for n in ("qk_ready", "sm_ready", "prod_ready", "c_ready", "ha_ready", "root_in"))
                    V2.credits()
                    dve.wait_ge(sem["par_in"], 16)
                    V2.pre_norm()

                    lam = par2[:, P2["lam"]:P2["lam"] + 8]
                    relu_, e_, t_, t2_, s_, coef = (small[:, n, :] for n in (0, 2, 3, 4, 5, 7))
                    settle()
                    do(dve.tensor_scalar(relu_, lam, -1.0, 0.0, ALU.mult, ALU.max))
                    do(dve.scalar_tensor_tensor(small[:, 1, :], lam, -1.0, lam, ALU.mult, ALU.max), roots_in)
                    dve.wait_ge(sem["root_ready"], 1)
                    do(dve.tensor_scalar(t_, e_, 2.0, None, ALU.add))
                    settle()
                    do(dve.reciprocal(s_, t_))
                    settle()
                    do(dve.tensor_tensor(t_, s_, e_, ALU.mult))
                    settle()
                    do(dve.tensor_tensor(t2_, t_, t_, ALU.mult))
                    settle()
                    do(dve.tensor_scalar(s_, t2_, 1.0 / 17, None, ALU.mult))
                    for n in range(15, 2, -2):
                        settle()
                        do(dve.scalar_tensor_tensor(s_, s_, 1.0 / n, t2_, ALU.add, ALU.mult))
                    settle()
                    do(dve.scalar_tensor_tensor(s_, s_, 1.0, t_, ALU.add, ALU.mult))
                    settle()
                    do(dve.scalar_tensor_tensor(s_, s_, 2.0, relu_, ALU.mult, ALU.add))
                    settle()
                    do(dve.tensor_scalar(coef, s_, -8.0, None, ALU.mult), Count(sem["coef_ready"]))
                    settle()

                    def hidden(c0, g0, outs):
                        def one(j, i=None, by=1):
                            k = 0 if i is None else i * 4
                            w.lo(c0 + j + 3, i)
                            dve.wait_ge(sem["act_out"], outs + j + 1 + k)
                            settle()
                            x = tX[:, j % 2, 0:S]
                            do(dve.tensor_tensor(x, tS[:, j % 2, 0:S], main[:, j % 4, S:2 * S], ALU.mult))
                            if i is None:
                                uh, ul = bhi[:, j, :], blo[:, j, :]
                            else:
                                uh, ul = (u[:, ds(i * 4 + j, 1), :].rearrange("p a n -> p (a n)") for u in (bhi, blo))
                            V2.split(uh, ul, x, V2.free, by)
                        for j in range(4):
                            one(j)
                        with V2.line.loop(4, [(w.lo_n, 4), (V2.free, 4), (V2.line.own, 8)], V2.free) as i:
                            for j in range(4):
                                one(4 + j, i)
                        one(20)
                        one(21, by=3)

                    hidden(C2["f1in"], G2["f1in"], 0)
                    V2.product_out(C2["f1out"], G2["f1out"], 4)
                    V2.post_norm(scale=0.5)
                    V2.pre_norm()

                    cos_sin, sin_cos = trig2[:, 0:2, :], trig2[:, 1:3, :]
                    took = [22]

                    def take():
                        took[0] += 1
                        dve.wait_ge(sem["act_out"], took[0])
                        settle()

                    def before(s):
                        if s == 45:
                            dve.wait_ge(sem["sig_ready"], 8)
                            settle()
                            do(dve.tensor_tensor(wide(Ig), wide(Ig), wide(Cg), ALU.mult))
                        if s == 47:
                            dve.wait_ge(sem["exp_ready"], 2)
                            settle()
                            do(dve.tensor_tensor(wide(Cg), wide(Ag), wide(Ag), ALU.mult))
                        if s == 48:
                            settle()
                            do(dve.scalar_tensor_tensor(wide(Rg), wide(Cg), 1.0, wide(Rg), ALU.add, ALU.mult), roots_in)
                        if s == 50:
                            dve.wait_ge(sem["root_ready"], 2)
                            settle()
                            do(dve.tensor_tensor(wide(Ig), wide(Ig), wide(Rg), ALU.mult))
                        if s in (51, 52):
                            settle()
                            for f in range((s - 51) * 4, (s - 50) * 4):
                                do(dve.tensor_tensor_scan(XA[:, f, 3:], Ag[:, f, :], Ig[:, f, :], 0.0,
                                                          ALU.mult, ALU.add), has if f % 4 == 3 else None)
                        if s in (52, 54, 56, 58):
                            hd = (s - 52) // 2
                            dve.wait_ge(sem["scores_done"], hd + 1)
                            if hd:
                                dve.wait_ge(sem["pv_done"], hd)
                            dve.wait_ge(sem["decay_in"], 16)
                            do(dve.tensor_tensor(SM[:, :], aux[1][:, 0:RSPAN], DEC[:, hd * RSPAN:(hd + 1) * RSPAN],
                                                 ALU.mult), sms)
                        if s in (54, 56, 58, 60):
                            V2.factor(2)
                        if s in (55, 57, 59, 61):
                            hd = (s - 55) // 2
                            V2.spread_done()
                            dve.wait_ge(sem["ret_ready"], 2 * hd + 2)
                            settle()
                            do(dve.tensor_tensor(RET[:, 4 * hd:4 * hd + 4, :], RET[:, 4 * hd:4 * hd + 4, :],
                                                 over(rb.unsqueeze(1), 4), ALU.mult))

                    for s in range(C2["xa"], C2["mix"]):
                        w.lo(s + 3)
                        before(s)
                        if s < C2["q"]:
                            p = s - C2["xa"]
                            used(dve, s)
                            dve.wait_ge(sem["pads_ready"], 1)
                            settle()
                            g = G2["xa"] + p
                            do(dve.tensor_copy(XA[:, 2 * p:2 * p + 2, 3:], units(main[:, g % 4, :])), V2.free)
                            for k in range(4):
                                settle()
                                for f in (2 * p, 2 * p + 1):
                                    wk = par2[:, P2["conv_w"] + f * 4 + k:P2["conv_w"] + f * 4 + k + 1]
                                    count = cs if k == 3 and f % 2 else None
                                    if k == 0:
                                        do(dve.tensor_scalar(Cg[:, f, :], XA[:, f, 0:S], wk,
                                                             par2[:, P2["conv_b"] + f:P2["conv_b"] + f + 1],
                                                             ALU.mult, ALU.add))
                                    else:
                                        do(dve.scalar_tensor_tensor(Cg[:, f, :], XA[:, f, k:k + S], wk, Cg[:, f, :],
                                                                    ALU.mult, ALU.add), count)
                        elif s < C2["v"]:
                            dst, u, g = ((q2, 2 * (s - C2["q"]), G2["q"] + s - C2["q"]) if s < C2["k"] else
                                         (k2, 2 * (s - C2["k"]), G2["k"] + s - C2["k"]))
                            used(dve, s)
                            settle()
                            bank = units(main[:, g % 4, :])
                            do(dve.tensor_tensor(units(tX[:, 0, :]), bank, cos_sin, ALU.mult))
                            do(dve.tensor_tensor(units(tX[:, 1, :]), bank, sin_cos, ALU.mult), V2.free)
                            settle()
                            do(dve.tensor_tensor(dst[:, u, :], tX[:, 0, 0:S], tX[:, 0, S:], ALU.subtract))
                            do(dve.tensor_tensor(dst[:, u + 1, :], tX[:, 1, 0:S], tX[:, 1, S:], ALU.add), qk)
                        elif s < C2["ya"]:
                            p = s - C2["v"]
                            used(dve, s)
                            settle()
                            do(dve.tensor_copy(V[:, :, p * S:(p + 1) * S], units(main[:, (G2["v"] + p) % 4, :])), V2.free)
                        elif s < C2["lru"]:
                            p = s - C2["ya"]
                            take()
                            if p == 3:
                                dve.wait_ge(sem["pv_done"], RET_HEADS)
                            do(dve.tensor_tensor(units(tX[:, p % 2, :]), units(tS[:, p % 2, :]),
                                                 XA[:, 2 * p:2 * p + 2, 3:], ALU.mult), V2.free)
                            V2.split(two(bhi, 16 + 2 * p), two(blo, 16 + 2 * p), tX[:, p % 2, :], prods)
                        elif s < C2["ga"]:
                            p = s - C2["lru"]
                            used(dve, s)
                            V2.copy_out(two(O, 2 * p), G2["lru"] + p)
                        elif s < C2["g"]:
                            p = s - C2["ga"]
                            take()
                            do(dve.tensor_tensor(two(MA, 2 * p), tS[:, p % 2, :], two(O, 2 * p), ALU.mult), V2.free)
                        elif s < C2["ret"]:
                            p = s - C2["g"]
                            take()
                            do(dve.tensor_tensor(tX[:, p % 2, :], tS[:, p % 2, :], two(RET, 2 * p), ALU.mult), V2.free)
                            V2.split(two(bhi, 2 * p), two(blo, 2 * p), tX[:, p % 2, :], prods)
                        elif s < C2["gb"]:
                            p = (s - C2["ret"]) // 2
                            if (s - C2["ret"]) % 2:
                                used(dve, s)
                                V2.copy_out(two(O, 2 * p), G2["ret"] + p)
                        elif s < C2["sc"]:
                            p = s - C2["gb"]
                            if p == 0:
                                do(dve.memset(SCP[:, :, 0:2], 0.0))
                            take()
                            do(dve.tensor_tensor(tX[:, p % 2, :], tS[:, p % 2, :], two(O, 2 * p), ALU.mult), V2.free)
                            settle()
                            do(dve.tensor_tensor(two(MA, 2 * p), two(MA, 2 * p), tX[:, p % 2, :], ALU.add))
                        elif s < C2["sco"]:
                            p, part = divmod(s - C2["sc"], 3)
                            g = G2["sc"] + s - C2["sc"]
                            used(dve, s)
                            settle()
                            bank = units(main[:, g % 4, :])
                            if part == 0:
                                do(dve.tensor_copy(tX[:, 0, :], main[:, g % 4, :]), V2.free)
                            elif part == 1:
                                do(dve.tensor_tensor(SCP[:, :, 2:], bank, units(tX[:, 0, :]), ALU.mult), V2.free)
                                for k in range(3):
                                    settle()
                                    for f in range(2):
                                        c = P2["sc_w"] + (2 * p + f) * 3 + k
                                        if k == 0:
                                            do(dve.tensor_scalar(SCC[:, f, :], SCP[:, f, 0:S], par2[:, c:c + 1],
                                                                 None, ALU.mult))
                                        else:
                                            do(dve.scalar_tensor_tensor(SCC[:, f, :], SCP[:, f, k:k + S],
                                                                        par2[:, c:c + 1], SCC[:, f, :],
                                                                        ALU.mult, ALU.add))
                            else:
                                do(dve.tensor_tensor(units(tX[:, 1, :]), bank, SCC[:, :, :], ALU.mult), V2.free)
                                V2.split(two(bhi, 16 + 2 * p), two(blo, 16 + 2 * p), tX[:, 1, :], prods)
                        elif s < C2["gc"]:
                            p = s - C2["sco"]
                            used(dve, s)
                            V2.copy_out(two(O, 2 * p), G2["sco"] + p)
                        else:
                            p = s - C2["gc"]
                            take()
                            do(dve.tensor_tensor(tX[:, 0, :], tS[:, p % 2, :], two(O, 2 * p), ALU.mult), V2.free)
                            settle()
                            do(dve.tensor_tensor(tX[:, 1, :], tX[:, 0, :], two(MA, 2 * p), ALU.add))
                            V2.split(two(bhi, 2 * p), two(blo, 2 * p), tX[:, 1, :], prods)
                    V2.product_out(C2["mix"], G2["mix"], 1)
                    V2.post_norm()
                    V2.pre_norm()
                    hidden(C2["f2in"], G2["f2in"], took[0])
                    V2.product_out(C2["f2out"], G2["f2out"], 4)
                    V2.post_norm(scale=0.5)
                    w.lo(C2["end"] + 3)

                @block.tensor
                def _(pe):
                    T = Tensor(pe)

                    def ffn(c0, g0, c1, g1, x):
                        for j in range(4):
                            T.pair(c0 + j, g0 + j, x=x if j == 0 else None)
                        with pe.Fori(0, 4) as i:
                            for j in range(4, 8):
                                T.pair(c0 + j, g0 + j, i)
                        T.pair(c0 + 20, g0 + 20)
                        T.pair(c0 + 21, g0 + 21)
                        pe.wait_ge(sem["groups_free"], 4 + g0 + 24)
                        T.long(c1, g1, 4, FFN2_TILES // 2, 2)
                        T.stats(4, 0, y=True)
                        T.spread()

                    def lru_gates(p):
                        pe.wait_ge(sem["c_ready"], p + 1)
                        for f in (2 * p, 2 * p + 1):
                            if f >= 2:
                                pe.wait_ge(sem["sig_ready"], f - 1)
                            for n, wn in enumerate(("w_a", "w_x")):
                                c = P2[wn] + f * P
                                last = pe.matmul(aux[1 + f % 2][:, n * S:(n + 1) * S], par2[:, c:c + P], Cg[:, f, :],
                                                 start=True, stop=True)
                            last.then_inc(sem["gates_done"], 1)

                    def scores(hd):
                        pe.wait_ge(sem["qk_ready"], 8)
                        pe.wait_ge(sem["sig_ready"], 8)
                        if hd:
                            pe.wait_ge(sem["sm_ready"], hd)
                        for t, c0 in ((0, 0), (1, P)):
                            for k in range(2):
                                u = 2 * hd + k
                                last = pe.matmul(aux[1][:, t * S:t * S + S - c0], k2[:, u, t * P:(t + 1) * P],
                                                 q2[:, u, c0:S], start=k == 0, stop=k == 1)
                        last.then_inc(sem["scores_done"], 1)

                    def values(hd):
                        pe.wait_ge(sem["sm_ready"], hd + 1)
                        pe.wait_ge(sem["groups_free"], 4 + G2["v"] + 2 * hd + 2)
                        if hd:
                            pe.wait_ge(sem["sq_ready"], T.pieces)
                        for e in range(4):
                            o = aux[2 + e // 2][:, e % 2 * S:(e % 2 + 1) * S]
                            c = hd * 512 + e * P
                            pe.matmul(o, V[:, 0, c:c + P], SM[:, 0:S], start=True, stop=True, skip_group_check=True)
                            last = pe.matmul(o[:, P:S], V[:, 1, c:c + P], SM[:, S:RSPAN], start=False, stop=True,
                                             skip_group_check=True)
                        last.then_inc(sem["pv_done"], 1)

                    T.stats(4, 0)
                    T.spread()
                    ffn(C2["f1in"], G2["f1in"], C2["f1out"], G2["f1out"], 0)
                    T.stats(4, 0)
                    T.spread()

                    for s in range(C2["xa"], C2["lru"]):
                        g = (G2["xa"] if s < C2["v"] else G2["v"]) + s - (C2["xa"] if s < C2["v"] else C2["v"])
                        if C2["v"] <= s < C2["ya"]:
                            T.arrive(s)
                            T.bank(g)
                            for t in range(2):
                                o = main[:, g % 4, t * S:(t + 1) * S].rearrange("p (f c) -> p f c", f=2)
                                for kt in range(KT):
                                    w_h, w_l = (x[:, s % RING, :].rearrange("p (f k c) -> p k f c", f=2, k=KT)[:, kt]
                                                for x in (whi, wlo))
                                    x_h, x_l = (x[:, kt, t * P:(t + 1) * P] for x in (xhi, xlo))
                                    pe.matmul(o, x_h, w_h, start=kt == 0, stop=False)
                                    pe.matmul(o, x_l, w_h, start=False, stop=False)
                                    last = pe.matmul(o, x_h, w_l, start=False, stop=kt == KT - 1)
                            last.then_inc(sem["split_free"], 1)
                        else:
                            T.pair(s, g, x=4 if s == C2["xa"] else None)
                        if s == 40:
                            pe.wait_ge(sem["big_par_in"], 16)
                        if 40 <= s <= 43:
                            lru_gates(s - 40)
                        if s in (54, 56, 58, 60):
                            T.spread()
                        if s in (53, 55, 57, 59):
                            T.stats(2, 1)
                        if s in (52, 54, 56, 58):
                            values((s - 52) // 2)
                        if s in (51, 53, 55, 57):
                            scores((s - 51) // 2)
                    pe.wait_ge(sem["prod_ready"], 4)
                    for p in range(4):
                        T.from_units(C2["lru"] + p, G2["lru"] + p, bhi, blo, 16)
                    for p in range(4):
                        T.pair(C2["ga"] + p, G2["ga"] + p)
                    with pe.Fori(0, 2) as i:
                        for j in range(4):
                            T.pair(C2["g"] + j, G2["g"] + j, i)
                    pe.wait_ge(sem["prod_ready"], 12)
                    for n in range(8):
                        s, g = C2["ret"] + n, G2["ret"] + n // 2
                        T.arrive(s)
                        if n % 2 == 0:
                            T.bank(g)
                        for t in range(16):
                            last = T.tile(main[:, g % 4, n % 2 * S:(n % 2 + 1) * S], s, t, bhi[:, t, :], blo[:, t, :],
                                          t == 0, t == 15)
                        last.then_inc(sem["split_free"], 1)
                    for p in range(4):
                        T.pair(C2["gb"] + p, G2["gb"] + p)
                    with pe.Fori(0, 3) as i:
                        for j in range(4):
                            T.pair(C2["sc"] + j, G2["sc"] + j, i)
                    pe.wait_ge(sem["prod_ready"], 16)
                    for p in range(4):
                        T.from_units(C2["sco"] + p, G2["sco"] + p, bhi, blo, 16)
                    for p in range(4):
                        T.pair(C2["gc"] + p, G2["gc"] + p)
                    pe.wait_ge(sem["prod_ready"], 20)
                    for p in range(4):
                        T.from_units(C2["mix"] + p, G2["mix"] + p, bhi, blo, 0)
                    T.stats(4, 0, y=True)
                    T.spread()
                    T.stats(4, 0)
                    T.spread()
                    ffn(C2["f2in"], G2["f2in"], C2["f2out"], G2["f2out"], 8)
            clear_all()

        with nc.Block() as block:
            @block.sync
            def _(sp):
                sp.dma_start(out, h[:, :, :]).then_inc(sem["out_done"], 16)
                sp.wait_ge(sem["out_done"], 16)



def constants():
    c = np.zeros((P, K["end"]), np.float32)
    c[:, 0:P] = np.eye(P)
    for base in (0, 64):
        for r in range(8):
            c[base + r + 8, K["swap"] + base + r] = -1.0
            c[base + r, K["swap"] + base + r + 8] = 1.0
    t = np.arange(P)
    c[:, K["tri"]:K["tri"] + P] = np.where(t[None, :] <= t[:, None], 0.0, MASKED)
    tok = np.arange(S)
    decay = np.zeros((P, RET_HEADS * RSPAN), np.float32)
    for hd in range(RET_HEADS):
        log_g = math.log1p(-2.0 ** (-5.0 - hd))
        d = np.exp(log_g * np.abs(tok[None, :] - tok[:, None])) / 16.0
        d = np.where(tok[:, None] // 64 <= tok[None, :] // 64, d, 0.0)
        decay[:, hd * RSPAN:hd * RSPAN + S] = d[0:P, :]
        decay[:, hd * RSPAN + S:(hd + 1) * RSPAN] = d[P:S, P:S]
    for n, win in enumerate((2, 4, 8, 16)):
        f, lo = n // 2, 64 * (n % 2)
        c[lo:lo + 64, K["rcount"] + f * S:K["rcount"] + (f + 1) * S] = 1.0 / np.minimum(tok + 1, win)
    for base in (0, 64):
        for r in range(16):
            c[base + r, K["freq"]] = np.float32(500000.0) ** np.float32(-(2 * (r % 8)) / 16)
    c[:, K["freq"] + 1] = np.float32(10000.0) ** (-np.arange(P, dtype=np.float32) / np.float32(P))
    return c, decay


def tiles(m):
    k, n = m.shape
    return m.reshape(k // P, P, n // P, P).transpose(2, 0, 1, 3).reshape(-1, P, P)


def chunks(t, per=CHUNK_TILES):
    c = t.reshape(-1, per, P, P).transpose(0, 2, 1, 3).reshape(-1, P, per * P)
    out = np.zeros((c.shape[0], P, CHUNK), np.float32)
    out[:, :, 0:per * P] = c
    return out


def units_of(v):
    v = v.reshape(v.shape[0] // P, P, -1)
    return v.transpose(1, 0, 2).reshape(P, -1)


def blocks(w, n):
    out = np.zeros((P, n, P), np.float32)
    for f in range(n):
        out[0:64, f, 0:64] = w[2 * f]
        out[64:P, f, 64:P] = w[2 * f + 1]
    return out.reshape(P, n * P)


def feature_major(x):
    return np.ascontiguousarray(x.T.reshape(-1, P, S).transpose(1, 0, 2))


def lay_out(v):
    w1, w2, par1, par2, ps = [], [], [], [], []
    heads = [half * 4 + f for f in range(4) for half in range(2)]
    for l in range(LAYERS):
        w = v["w_in"][l]
        q, k, vv, qi, ki, wi, conv, pool = np.split(w, [512, 640, 768, 1792, 1856, 1872, 2384], axis=1)
        q = q.reshape(D, HEADS, 64)[:, heads].reshape(D, 512)
        wi_ = np.zeros((D, P), np.float32)
        wi_[:, 0:IDX_HEADS] = wi
        order = [ki, ki, wi_, k, vv, qi, q, conv[:, 0:128], conv[:, 256:384], conv[:, 128:256], conv[:, 384:512], pool]
        w_out = v["w_out"][l]
        w_out = np.concatenate([w_out[0:512].reshape(HEADS, 64, D)[heads].reshape(512, D), w_out[512:]], axis=0)
        w1 += [chunks(tiles(np.concatenate(order, axis=1))), chunks(tiles(w_out)), chunks(tiles(v["w_up"][l])),
               chunks(tiles(v["w_down"][l])), chunks(tiles(v["ple_gate"][l])), chunks(tiles(v["ple_proj"][l]))]
        cp = v["conv_pw"][l]
        par1.append(np.concatenate(
            [units_of(v[n][l]) for n in ("norm_mix_pre", "norm_mix_post", "norm_mlp_pre", "norm_mlp_post")]
            + [units_of(v["conv_dw"][l].T), units_of(v["conv_b"][l]), units_of(v["conv_ln_g"][l]),
               units_of(v["conv_ln_b"][l]), units_of(v["pool_scale"][l]), units_of(cp), blocks(v["pool_w"][l], 2)],
            axis=1))
        ps.append(feature_major(v["p"][l, 0]).reshape(P, 2 * S))

        def ffn(n):
            w = v[n + "_w_in_2"][l]
            both = np.stack([w[:, 0:FFN2].reshape(D, FFN2_TILES, P), w[:, FFN2:].reshape(D, FFN2_TILES, P)], axis=2)
            return [chunks(tiles(both.reshape(D, 2 * FFN2))), chunks(tiles(v[n + "_w_out_2"][l]), FFN2_TILES // 2)]

        m = v["w_mix_in_2"][l]
        xa, ya, q, k, vv, g, sb, sc, sh, gates = np.split(m, [1024, 2048, 3072, 4096, 6144, 8192, 9216, 10240, 11264], axis=1)
        ga, gb, gc = np.split(gates, 3, axis=1)
        thirds = np.stack([z.reshape(D, 4, 256) for z in (sc, sh, sb)], axis=2).reshape(D, 3072)
        w2 += ffn("ffn1") + [chunks(tiles(z)) for z in (
            xa, q, k, vv, ya, v["w_lru_out_2"][l], ga, g, v["w_ret_out_2"][l], gb, thirds, v["w_sc_out_2"][l], gc,
            v["w_mix_out_2"][l])] + ffn("ffn2")
        par2.append(np.concatenate(
            [units_of(v[n + "_2"][l]) for n in ("ffn1_pre_g", "ffn1_post_g", "mix_pre_g")]
            + [units_of(v["lru_conv_w_2"][l].T)]
            + [units_of(v[n + "_2"][l]) for n in ("lru_conv_b", "lru_b_a", "lru_b_x", "lru_lambda", "mix_post_g",
                                                  "ffn2_pre_g", "ffn2_post_g")]
            + [units_of(v["sc_conv_w_2"][l].T), blocks(v["lru_w_a_2"][l], 8), blocks(v["lru_w_x_2"][l], 8)], axis=1))
    consts, decay = constants()
    pos = np.stack([v["positions"].reshape(S), v["positions_2"].reshape(S)])
    return {
        "x": feature_major(v["x"][0]),
        "pos": np.ascontiguousarray(np.broadcast_to(pos[None], (P, 2, S))),
        "consts": consts,
        "decay": decay,
        "par1": np.concatenate(par1, axis=0),
        "par2": np.concatenate(par2, axis=0),
        "p": np.concatenate(ps, axis=0),
        "w": np.concatenate(w1 + w2 + [np.zeros((RING, P, CHUNK), np.float32)], axis=0).reshape(-1, CHUNK),
    }


def kernel(**inputs):
    import concourse.bacc as bacc
    from concourse import mybir
    from concourse.bass_utils import run_bass_kernel_spmd

    arrays = lay_out({k: np.asarray(v) for k, v in inputs.items()})
    nc = bacc.Bacc("TRN2", target_bir_lowering=False, num_devices=1)
    drams = {n: nc.dram_tensor(f"in_{n}", z.shape, mybir.dt.from_np(z.dtype), kind="ExternalInput").ap()
             for n, z in arrays.items()}
    out = nc.dram_tensor("out_h", (P, KT, S), mybir.dt.float32, kind="ExternalOutput").ap()
    build(nc, drams, out)
    r = run_bass_kernel_spmd(nc, [{f"in_{n}": z for n, z in arrays.items()}], core_ids=[0])
    got = np.asarray(r.results[0]["out_h"])
    return np.ascontiguousarray(got.transpose(1, 0, 2).reshape(1, D, S).transpose(0, 2, 1))
```

```python
import math
import numpy as np

P = 128
S = 256
D = 1024
KT = D // P
LAYERS = 2
RING = 4
RAW = 2
CHUNK_TILES = 16
CHUNK = CHUNK_TILES * P
FFN1 = 4096
FFN2 = 2816
FFN2_TILES = FFN2 // P
NARROW = FFN2_TILES // 2 * P
EPS = 1e-6
LN_EPS = 1e-5
TAPS = 31
TOPK = 64
IDX_HEADS = 16
HEADS = 8
RET_HEADS = 4
TAP_RING = 8
TAPS_BEFORE, TAPS_AFTER = 36, (7, 7, 6, 6)
MASKED = -3.0e38
TAKEN = -3.3e38
OFF = -1.0e30
C1 = dict(inp=0, out=11, up=15, down=31, gate=47, ple=51, end=52)
G1 = dict(inp=0, out=12, up=16, down=32, gate=36, ple=40)
C2 = dict(f1in=0, f1out=22, xa=38, q=42, k=46, v=50, ya=58, lru=62, ga=66, g=70, ret=78, gb=86,
          sc=90, sco=102, gc=106, mix=110, f2in=114, f2out=136, end=152)
G2 = dict(f1in=0, f1out=24, xa=28, q=32, k=36, v=40, ya=48, lru=52, ga=56, g=60, ret=68, gb=72,
          sc=76, sco=88, gc=92, mix=96, f2in=100, f2out=124)
P1 = dict(mix_pre=0, mix_post=8, mlp_pre=16, mlp_post=24, dw=32, conv_b=94, ln_g=96, ln_b=98,
          pool_scale=100, conv_pw=102, pool_w=614, end=870)
P2 = dict(f1_pre=0, f1_post=8, mix_pre=16, conv_w=24, conv_b=56, b_a=64, b_x=72, lam=80,
          mix_post=88, f2_pre=96, f2_post=104, sc_w=112, w_a=136, w_x=1160, end=2184)
K = dict(ident=0, swap=128, tri=256, rcount=384, freq=896, end=898)
RSPAN = 384


class Count:

    def __init__(self, sem):
        self.sem, self.n, self.dyn = sem, 0, None

    def value(self):
        return self.n if self.dyn is None else self.n + self.dyn


class Line:

    def __init__(self, eng, own):
        self.eng, self.own, self.last = eng, own, None

    def do(self, ins, count=None, by=1):
        count = count or self.own
        ins.then_inc(count.sem, by)
        count.n += by
        self.last = count
        return count.n

    def settle(self):
        if self.last is not None:
            self.eng.wait_ge(self.last.sem, self.last.value())

    def loop(self, times, per, last):
        return _Loop(self, times, per, last)


class _Loop:

    def __init__(self, line, times, per, last):
        self.line, self.times, self.per, self.last = line, times, per, last

    def __enter__(self):
        self.fori = self.line.eng.Fori(0, self.times)
        i = self.fori.__enter__()
        self.base = [c.n for c, _ in self.per]
        for c, k in self.per:
            c.dyn = i * k
        self.line.last = self.last
        return i

    def __exit__(self, *a):
        for (c, k), base in zip(self.per, self.base):
            assert c.n - base == k, (c.n - base, k)
            c.n, c.dyn = base + k * self.times, None
        return self.fori.__exit__(*a)


def build(nc, a, out):
    import concourse.bass as bass
    from concourse import mybir
    from contextlib import ExitStack

    f32, f32r, i32 = mybir.dt.float32, mybir.dt.float32r, mybir.dt.int32
    ACT, ALU, AX = mybir.ActivationFunctionType, mybir.AluOpType, mybir.AxisListType
    ds = bass.ds

    with ExitStack() as ctx:
        def psum(name):
            return ctx.enter_context(nc.psum_tensor(name, [P, 512], f32))

        place = [16640]

        def sb(name, units, dtype=f32, at=None, shape=None):
            shape = shape or [P, units, S]
            if at is None:
                at = place[0]
                place[0] += -(-int(np.prod(shape[1:])) * 4 // 32) * 32
                assert place[0] <= 229344, (name, place[0])
            return nc.alloc_sbuf_tensor_at(name, shape, dtype, offset=at)

        UNIT = S * 4
        raw = sb("raw", 0, shape=[P, RAW, CHUNK])
        whi = sb("whi", 0, f32r, shape=[P, RING, CHUNK])
        wlo = sb("wlo", 0, f32r, shape=[P, RING, CHUNK])
        h = sb("h", KT)
        sqy_at = place[0]
        xhi = sb("xhi", KT, f32r)
        sqy = sb("sqy", 0, at=sqy_at, shape=[P, 4, 512])
        HG = sb("HG", KT, at=sqy_at)
        y_at = place[0]
        xlo = sb("xlo", KT, f32r)
        Y = sb("Y", KT, at=y_at)
        hi_at = place[0]
        XF = sb("XF", KT, at=hi_at)
        bhi = sb("bhi", 32, f32r)
        lo_at = place[0]
        blo = sb("blo", 32, f32r)
        tS = sb("tS", 0, shape=[P, 2, 512])
        tX = sb("tX", 0, shape=[P, 2, 512])
        sq = sb("sq", 0, shape=[P, 2, 512])
        cst = sb("cst", 0, shape=[P, K["end"]])
        means = sb("means", 0, shape=[P, 3, P])
        half = sb("half", 0, shape=[P, 2])
        diag = sb("diag", 0, shape=[P, 2, P])
        var = sb("var", 0, shape=[P, 2])
        rstd = sb("rstd", 0, shape=[P, 2])
        small = sb("small", 0, shape=[P, 8, 8])
        trig2 = sb("trig2", 3)
        free_at = place[0]

        ident, swap = cst[:, 0:P], cst[:, K["swap"]:K["swap"] + P]
        tri = cst[:, K["tri"]:K["tri"] + P]

        trig1 = sb("trig1", 2)
        par1 = sb("par1", 0, shape=[P, P1["end"]])
        best = sb("best", 0, shape=[P, 2, 8])
        rmax = sb("rmax", 0, shape=[P, HEADS, 2])
        rsum = sb("rsum", 0, shape=[P, HEADS, 2])
        rinv = sb("rinv", 0, shape=[P, HEADS, 2])
        wi = sb("wi", 0, shape=[P, 2, IDX_HEADS])
        A0, B0 = hi_at + 8 * UNIT, lo_at + 8 * UNIT
        KI = sb("KI", 1, at=A0)
        KR = sb("KR", 1, at=A0 + 1 * UNIT)
        VP = sb("VP", 0, at=A0 + 2 * UNIT, shape=[P, 2, 2, P])
        QI = sb("QI", 8, at=A0 + 4 * UNIT)
        Q = sb("Q", 4, at=A0 + 12 * UNIT)
        acc = sb("acc", 0, at=A0 + 16 * UNIT, shape=[P, RSPAN])
        work = sb("work", 0, at=A0 + 18 * UNIT, shape=[P, 2, RSPAN])
        cacc = sb("cacc", 2, at=A0 + 22 * UNIT)
        YC = sb("YC", 0, at=B0, shape=[P, 2, TAPS - 1 + S])
        UP = sb("UP", 0, at=B0 + 3 * UNIT, shape=[P, 2, 16 + S])
        W2 = sb("W2", 0, at=B0 + 6 * UNIT, shape=[P, 2, 16 + S])
        W4 = sb("W4", 0, at=B0 + 9 * UNIT, shape=[P, 2, 16 + S])
        PO = sb("PO", 2, at=B0 + 12 * UNIT)
        bias = sb("bias", 0, at=B0 + 14 * UNIT, shape=[P, RSPAN])
        sm = sb("sm", 0, at=B0 + 16 * UNIT, shape=[P, 2, RSPAN])
        pt = sb("pt", 0, at=B0 + 19 * UNIT, shape=[P, 2, RSPAN])
        cact = sb("cact", 2, at=B0 + 22 * UNIT)
        tapd = sb("tapd", 0, at=hi_at + 4 * UNIT, shape=[P, TAP_RING, P])
        GATE = sb("GATE", KT, at=hi_at)
        PT = sb("PT", 2, at=free_at + 7 * UNIT)
        pthi = sb("pthi", 2, f32r, at=free_at + 9 * UNIT)
        ptlo = sb("ptlo", 2, f32r, at=free_at + 11 * UNIT)
        assert place[0] <= free_at + 7 * UNIT and free_at + 14 * UNIT <= 229344
        R1 = sb("R1", 1, at=free_at + 13 * UNIT)
        R2 = cst[:, K["rcount"]:K["rcount"] + S].unsqueeze(1)

        par2 = sb("par2", 0, at=free_at, shape=[P, P2["end"]])
        XA = sb("XA", 0, at=free_at + P2["end"] * 4, shape=[P, 8, 3 + S])
        assert free_at + P2["end"] * 4 + 8 * (3 + S) * 4 <= 229344, free_at
        Rg = sb("Rg", 8, at=hi_at + 8 * UNIT)
        Ag = sb("Ag", 8, at=hi_at)
        Ig = sb("Ig", 8, at=lo_at)
        Cg = sb("Cg", 8, at=lo_at + 8 * UNIT)
        RET = sb("RET", 16, at=hi_at)
        V = sb("V", 0, at=hi_at + 16 * UNIT, shape=[P, 2, 2048])
        q2 = sb("q2", 8, at=lo_at + 16 * UNIT)
        k2 = sb("k2", 8, at=lo_at + 24 * UNIT)
        O = sb("O", 8, at=hi_at + 24 * UNIT)
        MA = sb("MA", 8, at=lo_at + 24 * UNIT)
        DEC = sb("DEC", 0, at=free_at + 1 * UNIT, shape=[P, RET_HEADS * RSPAN])
        SCP = sb("SCP", 0, at=free_at + 1 * UNIT, shape=[P, 2, 2 + S])
        SCC = sb("SCC", 2, at=free_at + 4 * UNIT)
        SM = sb("SM", 0, at=free_at + P2["end"] * 4 + 8 * (3 + S) * 4, shape=[P, RSPAN])

        main = ctx.enter_context(nc.psum_tensor("main", [P, 4, 512], f32))
        aux = [psum(f"aux{n}") for n in range(4)]
        rb = aux[0][:, S:2 * S]
        ident2 = ident.unsqueeze(1).broadcast_to([P, 2, P])

        def stat(bank):
            return bank[:, 0:S]


        names = ("gain_ready round_ready xf_ready big_par_in mean_done decay_in par_in w_in0 w_in1 w_hi w_lo split_free groups_free credit act_out sq_ready stat_done "
                 "var_ready rstd_ready diag_ready rb_ready rb_used gate_in tap_ready tap_used conv_done h_ready x_ready act_own dve_own "
                 "pool_own hid_ready perm_done aux_ready aux_free prod_ready scores_done probs_ready "
                 "pt_done pt_ready pv_done c_ready gates_done sig_ready exp_ready root_in root_ready "
                 "coef_ready relu_used pads_ready ha_ready qk_ready sm_ready ret_ready pool_in pool_out p_in wi_ready dots_done "
                 "relu_ready v_ready out_done cst_in").split()
        sem = {n: ctx.enter_context(nc.semaphore(n)) for n in names}
        numbers = range(min(x.num for x in sem.values()), max(x.num for x in sem.values()) + 1)
        assert len(numbers) == len(names)

        def clear_all():
            with nc.Block() as block:
                @block.gpsimd
                def _(pool):
                    pool.sem_clear(numbers)

        with nc.Block() as block:
            ang = sq[:, 0, 0:S]
            turns = sq[:, 0, S:512]
            posf = sq[:, 1, 0:S]
            first = nc.alloc_sbuf_tensor_at("first", [P, RING - RAW, CHUNK], f32, offset=lo_at)
            start = [raw[:, 0, :], raw[:, 1, :], first[:, 0, :], first[:, 1, :]]
            posi = nc.alloc_sbuf_tensor_at("posi", [P, 2, S], i32, offset=hi_at)

            @block.sync
            def _(sp):
                sp.dma_start(posi[:, :, :], a["pos"]).then_inc(sem["cst_in"], 16)
                sp.dma_start(cst[:, :], a["consts"]).then_inc(sem["cst_in"], 16)
                for s in range(RING):
                    if s >= RAW:
                        sp.wait_ge(sem[f"w_in{s % RAW}"], 16)
                    sp.dma_start(start[s], a["w"][s * P:(s + 1) * P, :]).then_inc(sem[f"w_in{s % RAW}"], 16)
                sp.dma_start(h[:, :, :], a["x"]).then_inc(sem["out_done"], 16)

            @block.gpsimd
            def _(pool):
                pool.memset(half[:, :], -0.5)
                for n, width in enumerate((1024, 512, 256)):
                    pool.memset(means[:, n, :], 1.0 / width)

            @block.scalar
            def _(act):
                for s in range(RING):
                    act.wait_ge(sem[f"w_in{s % RAW}"], 16 * (s // RAW + 1))
                    act.activation(whi[:, s, :], start[s], ACT.Copy).then_inc(sem["w_hi"], 1)
                for m, t in ((0, trig1), (1, trig2)):
                    act.wait_ge(sem["x_ready"], m + 1)
                    act.activation(t[:, 1, :], Y[:, 2 * m, :], ACT.Sin)
                    ins = act.activation(t[:, 0, :], Y[:, 2 * m + 1, :], ACT.Sin).then_inc(sem["act_out"], 1)

            @block.vector
            def _(dve):
                line = Line(dve, Count(sem["dve_own"]))
                do, settle = line.do, line.settle
                dve.wait_ge(sem["cst_in"], 32)
                c1 = 6.28125
                c2 = float(np.float32(np.floor((2 * math.pi - c1) * 2 ** 20) / 2 ** 20))
                c3 = float(np.float32(2 * math.pi - c1 - c2))
                magic = 12582912.0
                pi = float(np.nextafter(np.float32(math.pi), np.float32(0)))
                for m in range(2):
                    do(dve.tensor_copy(posf, posi[:, m, :]))
                    settle()
                    do(dve.tensor_scalar(ang, posf, cst[:, K["freq"] + m:K["freq"] + m + 1], None, ALU.mult))
                    settle()
                    do(dve.tensor_scalar(turns, ang, 1.0 / (2 * math.pi), magic, ALU.mult, ALU.add))
                    settle()
                    do(dve.tensor_scalar(turns, turns, -magic, None, ALU.add))
                    for c in (c1, c2, c3):
                        settle()
                        do(dve.scalar_tensor_tensor(ang, turns, -c, ang, ALU.mult, ALU.add))
                    settle()
                    do(dve.tensor_scalar(Y[:, 2 * m, :], ang, -pi, pi, ALU.max, ALU.min))
                    settle()
                    do(dve.scalar_tensor_tensor(posf, Y[:, 2 * m, :], -1.0, Y[:, 2 * m, :], ALU.mult, ALU.max))
                    settle()
                    do(dve.tensor_scalar(Y[:, 2 * m + 1, :], posf, -1.0, math.pi / 2, ALU.mult, ALU.add))
                    settle()
                    dve.memset(small[:, 0, 0:1], 0.0).then_inc(sem["x_ready"], 1)
                    for s in (2 * m, 2 * m + 1):
                        dve.wait_ge(sem["w_hi"], s + 1)
                        dve.tensor_tensor(wlo[:, s, :], start[s], whi[:, s, :].bitcast(f32),
                                          ALU.subtract).then_inc(sem["w_lo"], 1)
                dve.wait_ge(sem["out_done"], 16)
                dve.wait_ge(sem["act_out"], 2)
                dve.tensor_copy(trig2[:, 2, :], trig2[:, 0, :])
        clear_all()


        class Stream:

            def __init__(self, line, end, narrow=()):
                self.line, self.end, self.narrow = line, end, narrow
                self.hi_n, self.lo_n = Count(sem["w_hi"]), Count(sem["w_lo"])

            def width(self, s, i):
                return NARROW if i is None and s in self.narrow else CHUNK

            def hi(self, s, i=None):
                if i is None and s < RING:
                    return
                e, k, n = self.line.eng, 0 if i is None else i, self.width(s, i)
                e.wait_ge(sem[f"w_in{s % RAW}"], 16 * ((s - RING) // RAW + 1) + k * 32)
                e.wait_ge(sem["split_free"], s - RING + 1 + k * 4)
                self.line.do(e.activation(whi[:, s % RING, 0:n], raw[:, s % RAW, 0:n], ACT.Copy), self.hi_n)

            def lo(self, s, i=None):
                if i is None and s < RING:
                    return
                e, k, n = self.line.eng, 0 if i is None else i, self.width(s, i)
                e.wait_ge(sem["w_hi"], s - RING + 1 + k * 4)
                self.line.do(e.tensor_tensor(wlo[:, s % RING, 0:n], raw[:, s % RAW, 0:n],
                                             whi[:, s % RING, 0:n].bitcast(f32), ALU.subtract), self.lo_n)

        def used(e, s, i=None):
            e.wait_ge(sem["split_free"], s + 1 + (0 if i is None else i * 4))

        def load_stream(sp, base, L, spans, end):
            def one(s, i, width):
                k = 0 if i is None else i
                if s >= RING + RAW:
                    sp.wait_ge(sem["w_lo"], s - RAW - RING + 1 + k * 2)
                sp.dma_start(raw[:, s % RAW, 0:width],
                             a["w"][ds(L * (end * P) + (base + s + k * 2) * P, P), 0:width])\
                  .then_inc(sem[f"w_in{s % RAW}"], 16)
            for c0, c1, width in spans:
                first = c0
                if c0 == RING:
                    one(RING, None, width)
                    one(RING + 1, None, width)
                    first = RING + RAW
                if c1 - first > 4:
                    with sp.Fori(0, (c1 - first) // 2) as i:
                        one(first, i, width)
                        one(first + 1, i, width)
                else:
                    for s in range(first, c1):
                        one(s, None, width)

        class Tensor:
            def __init__(self, pe):
                self.pe = pe
                self.norms = self.pieces = 0

            def tile(self, out_, s, t, hi_, lo_, first, last):
                w_h, w_l = whi[:, s % RING, t * P:(t + 1) * P], wlo[:, s % RING, t * P:(t + 1) * P]
                self.pe.matmul(out_, w_h, hi_, start=first, stop=False)
                self.pe.matmul(out_, w_h, lo_, start=False, stop=False)
                return self.pe.matmul(out_, w_l, hi_, start=False, stop=last)

            def arrive(self, s, i=None, step=4):
                if i is not None or s >= RING:
                    self.pe.wait_ge(sem["w_lo"], s - RING + 1 + (0 if i is None else i * step))

            def bank(self, g, i=None, step=4):
                self.pe.wait_ge(sem["groups_free"], g + 1 + (0 if i is None else i * step))

            def pair(self, s, g, i=None, tok=(False, False), cols=(P, P), x=None, norm=False):
                self.arrive(s, i)
                self.bank(g, i)
                for f in range(2):
                    if not tok[f]:
                        for kt in range(KT):
                            if norm and f == 0 and kt % 2 == 0:
                                self.stat_piece(kt // 2, 4, 0)
                            if x is not None and f == 0 and kt % 2 == 0:
                                self.pe.wait_ge(sem["x_ready"], x + kt // 2 + 1)
                            last = self.tile(main[:, g % 4, f * S:(f + 1) * S], s, f * KT + kt,
                                             xhi[:, kt, :], xlo[:, kt, :], kt == 0, kt == KT - 1)
                    else:
                        for t in range(2):
                            o = main[:, g % 4, f * S + t * P:f * S + t * P + cols[f]]
                            for kt in range(KT):
                                c = (f * KT + kt) * P
                                w_h, w_l = (w[:, s % RING, c:c + cols[f]] for w in (whi, wlo))
                                x_h, x_l = (z[:, kt, t * P:(t + 1) * P] for z in (xhi, xlo))
                                self.pe.matmul(o, x_h, w_h, start=kt == 0, stop=False)
                                self.pe.matmul(o, x_l, w_h, start=False, stop=False)
                                last = self.pe.matmul(o, x_h, w_l, start=False, stop=kt == KT - 1)
                last.then_inc(sem["split_free"], 1)
                if norm:
                    self.pieces += 4
                    self.norms += 1
                    self.spread()

            def from_units(self, s, g, hi_, lo_, base, ready=None, order=range(KT)):
                self.arrive(s)
                self.bank(g)
                for f in range(2):
                    for n, kt in enumerate(order):
                        if ready and f == 0:
                            self.pe.wait_ge(sem["prod_ready"], ready[kt])
                        last = self.tile(main[:, g % 4, f * S:(f + 1) * S], s, f * KT + kt,
                                         hi_[:, base + kt, :], lo_[:, base + kt, :], n == 0, n == KT - 1)
                last.then_inc(sem["split_free"], 1)

            def long(self, c0, g0, groups, tiles, per, full):
                with self.pe.Fori(0, groups) as i:
                    assert g0 % 4 == 0 and groups <= 4
                    self.bank(g0, i, 1)
                    for f in range(2):
                        for c in range(per):
                            n = f * per + c
                            s = c0 + n
                            self.arrive(s, i, 2 * per)
                            for t in range(tiles):
                                if f == 0 and c == per - 1 and t == tiles - 6:
                                    self.pe.wait_ge(sem["groups_free"], full)
                                last = self.tile(
                                    main[:, ds(i, 1), f * S:(f + 1) * S].rearrange("p a n -> p (a n)"),
                                    s, t, bhi[:, c * tiles + t, :], blo[:, c * tiles + t, :],
                                    c == 0 and t == 0, c == per - 1 and t == tiles - 1)
                            last.then_inc(sem["split_free"], 1)

            def stat_piece(self, p, pieces, col, src=None, y=False, at=aux[1]):
                if self.norms and p == 0:
                    self.pe.wait_ge(sem["var_ready"], self.norms)
                if src is None:
                    self.pe.wait_ge(sem["sq_ready"], self.pieces + p + 1)
                x = sqy[:, p, :] if y else sq[:, (self.pieces + p) % 2, :] if src is None else src
                for k in range(2):
                    last = self.pe.matmul(stat(at), means[:, col, :], x[:, k * S:(k + 1) * S],
                                          start=(p == 0 and k == 0), stop=(p == pieces - 1 and k == 1))
                last.then_inc(sem["stat_done" if src is None else "mean_done"], 1)

            def stats(self, pieces, col, src=None, y=False, at=aux[1]):
                for p in range(pieces):
                    self.stat_piece(p, pieces, col, src, y, at)
                self.pieces += pieces if src is None else 0
                self.norms += 1 if src is None else 0

            def spread(self):
                self.pe.wait_ge(sem["diag_ready"], self.norms)
                self.pe.matmul(rb, means[:, 0, :], diag[:, :, :].rearrange("p a b -> p (a b)"),
                               start=True, stop=True).then_inc(sem["rb_ready"], 1)

        class Scalar:
            def __init__(self, act, end, narrow=()):
                self.line = Line(act, Count(sem["act_own"]))
                self.act, self.do, self.settle = act, self.line.do, self.line.settle
                self.w = Stream(self.line, end, narrow)
                self.outs, self.sqs = Count(sem["act_out"]), Count(sem["sq_ready"])
                self.gained, self.rounded = Count(sem["gain_ready"]), Count(sem["round_ready"])
                self.h_seen = self.xf_seen = 0

            def gains(self, dst, src, p, par, gain):
                for kt in (2 * p, 2 * p + 1):
                    self.do(self.act.activation(dst[:, kt, :], src[:, kt, :], ACT.Copy,
                                                scale=par[:, gain + kt:gain + kt + 1]),
                            self.gained if kt % 2 else None)

            def product_out(self, c0, g0, per, par, gain):
                for p in range(4):
                    last_one = p == 3
                    for c in range(per):
                        if not (last_one and c == per - 1):
                            self.w.hi(c0 + p * per + c + 3)
                    self.act.wait_ge(sem["groups_free"], g0 + p + 5)
                    self.squares_y(p)
                    self.settle()
                    self.gains(Y, Y, p, par, gain)
                    if last_one:
                        self.w.hi(c0 + 4 * per + 2)

            def h_in(self, par, gain, wait=True):
                for p in range(4):
                    if wait:
                        self.act.wait_ge(sem["h_ready"], self.h_seen + p + 1)
                    self.squares(two(h, 2 * p), p)
                    if wait:
                        self.gains(HG, h, p, par, gain)
                    elif p:
                        if p == 1:
                            self.act.wait_ge(sem["par_in"], 16)
                        self.gains(HG, h, p - 1, par, gain)
                if not wait:
                    self.gains(HG, h, 3, par, gain)
                self.h_seen += 4 if wait else 0

            def late_x(self, par, gain, wait=True):
                for p in range(4):
                    if wait:
                        self.act.wait_ge(sem["h_ready"], self.h_seen + p + 1)
                    self.squares(two(h, 2 * p), p)
                    if not wait and p == 0:
                        self.act.wait_ge(sem["par_in"], 16)
                    self.gains(XF, h, p, par, gain)
                    self.settle()
                    self.do(self.act.activation(two(xhi, 2 * p), two(XF, 2 * p), ACT.Copy), self.rounded)
                self.h_seen += 4 if wait else 0

            def round_x(self):
                for p in range(4):
                    self.xf_seen += 1
                    self.act.wait_ge(sem["xf_ready"], self.xf_seen)
                    self.do(self.act.activation(two(xhi, 2 * p), tX[:, p % 2, :], ACT.Copy), self.rounded)

            def squares_y(self, p):
                self.do(self.act.activation(sqy[:, p, :], two(Y, 2 * p), ACT.Square), self.sqs)

            def squares(self, src, p):
                if self.sqs.n >= 2:
                    self.act.wait_ge(sem["stat_done"], self.sqs.n - 1)
                self.do(self.act.activation(sq[:, self.sqs.n % 2, :], src, ACT.Square), self.sqs)

        class Vector:
            def __init__(self, dve, end, narrow=()):
                self.line = Line(dve, Count(sem["dve_own"]))
                self.dve, self.do, self.settle = dve, self.line.do, self.line.settle
                self.w = Stream(self.line, end, narrow)
                self.free = Count(sem["groups_free"])
                self.vars, self.diags = Count(sem["var_ready"]), Count(sem["diag_ready"])
                self.xs, self.hs, self.xfs = Count(sem["x_ready"]), Count(sem["h_ready"]), Count(sem["xf_ready"])
                self.gained = self.rounds = 0
                self.stats = self.roots = self.took = 0

            def credits(self):
                self.do(self.dve.memset(small[:, 0, 1:2], 0.0), self.free, by=4)

            def factor(self, pieces, eps=EPS, scale=1.0, at=aux[1], between=None):
                self.stats += pieces
                self.dve.wait_ge(sem["stat_done"], self.stats)
                self.settle()
                self.do(self.dve.scalar_tensor_tensor(diag[:, :, :], stat(at).rearrange("p (a b) -> p a b", a=2),
                                                      eps, ident2, ALU.add, ALU.mult))
                self.settle()
                self.do(self.dve.tensor_reduce(var[:, :], diag[:, :, :], AX.X, ALU.add), self.vars)
                if between:
                    between()
                self.roots += 1
                self.dve.wait_ge(sem["rstd_ready"], self.roots)
                for t in range(2):
                    ins = self.dve.tensor_scalar(diag[:, t, :], ident, rstd[:, t:t + 1], scale * D, ALU.mult, ALU.mult)
                    self.do(ins, self.diags if t else None)

            def spread_done(self):
                self.dve.wait_ge(sem["rb_ready"], self.diags.n)

            def split(self, hi_, lo_, src, count, by=1):
                self.settle()
                self.do(self.dve.tensor_copy(hi_, src))
                self.settle()
                self.do(self.dve.tensor_tensor(lo_, src, hi_.bitcast(f32), ALU.subtract), count, by)

            def late_lo(self, p, src=XF):
                self.rounds += 1
                self.dve.wait_ge(sem["round_ready"], self.rounds)
                self.do(self.dve.tensor_tensor(two(xlo, 2 * p), two(src, 2 * p), two(xhi, 2 * p).bitcast(f32),
                                               ALU.subtract), self.xs)

            def late_norm(self, R, between=None):
                self.gained += 4
                self.factor(4, between=between)
                self.spread_done()
                self.settle()
                self.do(self.dve.tensor_copy(R, rb.unsqueeze(1)))
                self.settle()

            def post_norm(self, scale=1.0, late=None):
                self.factor(4, scale=scale)
                self.spread_done()
                rb2 = over(rb.unsqueeze(1), 2)

                def scaled(p):
                    self.dve.wait_ge(sem["gain_ready"], self.gained + p + 1)
                    return self.do(self.dve.tensor_tensor(units(tX[:, p % 2, :]), Y[:, 2 * p:2 * p + 2, :], rb2, ALU.mult))

                self.settle()
                n = scaled(0)
                for p in range(4):
                    self.dve.wait_ge(sem["dve_own"], n)
                    if p >= 1:
                        self.dve.wait_ge(sem["h_ready"], self.hs.n)
                    if p < 3:
                        n = scaled(p + 1)
                    self.do(self.dve.tensor_tensor(two(h, 2 * p), two(h, 2 * p), tX[:, p % 2, :], ALU.add), self.hs)
                    if late is not None and p:
                        self.late_lo(p - 1, late)
                if late is not None:
                    self.late_lo(3, late)
                self.gained += 4

            def pre_norm(self):
                self.factor(4)
                self.spread_done()
                rb2 = over(rb.unsqueeze(1), 2)
                base = self.rounds
                ahead = self.xfs.n

                def scaled(p):
                    self.dve.wait_ge(sem["gain_ready"], self.gained + p + 1)
                    self.do(self.dve.tensor_tensor(units(tX[:, p % 2, :]), HG[:, 2 * p:2 * p + 2, :], rb2, ALU.mult), self.xfs)

                self.settle()
                scaled(0)
                scaled(1)
                for p in range(4):
                    self.dve.wait_ge(sem["round_ready"], base + p + 1)
                    self.dve.wait_ge(sem["xf_ready"], ahead + min(p + 2, 4))
                    self.do(self.dve.tensor_tensor(two(xlo, 2 * p), tX[:, p % 2, :], two(xhi, 2 * p).bitcast(f32),
                                                   ALU.subtract), self.xs)
                    if p < 2:
                        self.settle()
                        scaled(p + 2)
                self.gained += 4
                self.rounds += 4

            def copy_out(self, dst, g, count=None):
                self.settle()
                self.do(self.dve.tensor_copy(dst, main[:, g % 4, :]), self.free)

            def product_out(self, c0, g0, per):
                for p in range(4):
                    for c in range(per):
                        if not (p == 3 and c == per - 1):
                            self.w.lo(c0 + p * per + c + 3)
                    used(self.dve, c0 + p * per + per - 1)
                    self.copy_out(two(Y, 2 * p), g0 + p)

        def two(t, u):
            return t[:, u:u + 2, :].rearrange("p a n -> p (a n)")

        def wide(t, u=0, n=8):
            return t[:, u:u + n, :].rearrange("p a n -> p (a n)")

        def over(t, n):
            return t.broadcast_to([P, n, S])

        def units(t):
            return t.rearrange("p (a n) -> p a n", n=S)

        def roots(pool, values):
            for v in values:
                pool.wait_ge(sem["var_ready"], v)
                pool.tensor_tensor(rstd[:, :], var[:, :], half[:, :], ALU.pow).then_inc(sem["rstd_ready"], 1)

        def last_lo(pool, end):
            pool.wait_ge(sem["w_lo"], end + 2 - RING)
            for s in (end + 2, end + 3):
                pool.wait_ge(sem["w_hi"], s - RING + 1)
                pool.tensor_tensor(wlo[:, s % RING, :], raw[:, s % RAW, :], whi[:, s % RING, :].bitcast(f32),
                                   ALU.subtract).then_inc(sem["w_lo"], 1)

        with nc.Fori(0, LAYERS) as L:
            with nc.Block() as block:
                @block.sync
                def _(sp):
                    load_stream(sp, 0, L, [(RING, C1["end"] + RING, CHUNK)], C1["end"])

                @block.gpsimd
                def _(pool):
                    line = Line(pool, Count(sem["pool_own"]))
                    do, settle = line.do, line.settle
                    pool.memset(VP[:, :, :, :], 0.0)
                    pool.memset(YC[:, :, 0:TAPS - 1], 0.0)
                    pool.memset(W2[:, :, :], 0.0)
                    pool.memset(W4[:, :, :], 0.0)
                    pool.memset(UP[:, :, 0:16], 0.0).then_inc(sem["pads_ready"], 1)
                    roots(pool, [1])
                    pool.wait_ge(sem["pads_ready"], 1)
                    pool.wait_ge(sem["pool_in"], 1)
                    end = 16 + S
                    do(pool.tensor_tensor(W2[:, :, 1:end], UP[:, :, 1:end], UP[:, :, 0:end - 1], ALU.add))
                    settle()
                    do(pool.tensor_tensor(W4[:, :, 3:end], W2[:, :, 3:end], W2[:, :, 1:end - 2], ALU.add))
                    settle()
                    do(pool.tensor_tensor(W2[:, 1, 7:end], W4[:, 1, 7:end], W4[:, 1, 3:end - 4], ALU.add))
                    settle()
                    do(pool.tensor_tensor(W4[:, 1, 15:end], W2[:, 1, 15:end], W2[:, 1, 7:end - 8], ALU.add))
                    settle()
                    for f in range(2):
                        rc = cst[:, K["rcount"] + f * S:K["rcount"] + (f + 1) * S]
                        for lo_p, w in ((0, W2), (64, W4)):
                            do(pool.tensor_tensor(PO[lo_p:lo_p + 64, f, :], w[lo_p:lo_p + 64, f, 16:end],
                                                  rc[lo_p:lo_p + 64, :], ALU.mult))
                    settle()
                    pool.tensor_tensor(PO[:, :, :], PO[:, :, :], UP[:, :, 16:end], ALU.subtract).then_inc(sem["pool_out"], 1)
                    roots(pool, [2, 3, 4, 5])
                    last_lo(pool, C1["end"])

                @block.scalar
                def _(act):
                    cut = P1["conv_pw"]
                    act.dma_start(par1[:, 0:cut], a["par1"][ds(L * P, P), 0:cut]).then_inc(sem["par_in"], 16)
                    act.dma_start(par1[:, cut:], a["par1"][ds(L * P, P), cut:P1["end"]]).then_inc(sem["big_par_in"], 16)
                    act.dma_start(PT[:, :, :].rearrange("p a n -> p (a n)"), a["p"][ds(L * P, P), :]).then_inc(sem["p_in"], 16)
                    A = Scalar(act, C1["end"])
                    do, settle, w = A.do, A.settle, A.w
                    A.h_in(par1, P1["mix_pre"], wait=False)
                    A.round_x()

                    def relus(p):
                        for hd in range(4 * p, 4 * p + 4):
                            act.wait_ge(sem["dots_done"], hd + 1)
                            if hd >= 2:
                                act.wait_ge(sem["relu_used"], hd - 1)
                            act.activation(sm[:, hd % 2, :], aux[2 + hd % 2][:, 0:RSPAN], ACT.Relu)\
                               .then_inc(sem["relu_ready"], 1)

                    taps = Count(sem["tap_ready"])

                    def tap_diagonals(end):
                        while taps.n < end:
                            n = taps.n
                            if n >= TAP_RING:
                                act.wait_ge(sem["tap_used"], n - TAP_RING + 1)
                            do(act.activation(tapd[:, n % TAP_RING, :], ident, ACT.Copy,
                                              scale=par1[:, P1["dw"] + n:P1["dw"] + n + 1]), taps)

                    tap_diagonals(TAP_RING)
                    for s in range(11):
                        w.hi(s + 3)
                        if 6 <= s <= 9:
                            relus(s - 6)
                        used(act, s)
                        if s >= 2 and s < 10:
                            act.wait_ge(sem["perm_done"], s - 1)
                        if s < 8:
                            n = S if s < 2 else 2 * S
                            do(act.activation(tS[:, s % 2, 0:n], main[:, s % 4, 0:n], ACT.Copy), A.outs)
                        elif s < 10:
                            do(act.activation(tS[:, s % 2, 0:S], main[:, s % 4, S:2 * S], ACT.Sigmoid), A.outs)

                    exps_n = Count(sem["exp_ready"])

                    def exps(hh):
                        act.wait_ge(sem["sm_ready"], hh + 1)
                        for t, (c0, c1) in enumerate(((0, P), (P, RSPAN))):
                            do(act.activation(sm[:, hh % 2, c0:c1], sm[:, hh % 2, c0:c1], ACT.Exp,
                                              bias=rmax[:, hh, t:t + 1], accum_out=rsum[:, hh, t:t + 1]),
                               exps_n if t else None)

                    def turned(hh):
                        act.wait_ge(sem["pt_done"], hh + 1)
                        if hh >= 2:
                            act.wait_ge(sem["pv_done"], hh - 1)
                        act.activation(work[:, hh % 2, :], aux[1][:, 0:RSPAN], ACT.Copy).then_inc(sem["pt_ready"], 1)

                    tap_end = min(TAPS_BEFORE + TAP_RING, 2 * TAPS)
                    tap_diagonals(tap_end)
                    exps(0)
                    for hh in range(HEADS):
                        if hh + 1 < HEADS:
                            exps(hh + 1)
                        if hh == 4:
                            act.wait_ge(sem["conv_done"], 1)
                            for f in range(2):
                                ins = act.activation(cacc[:, f, :], aux[0][:, f * S:(f + 1) * S], ACT.Identity,
                                                     bias=par1[:, P1["conv_b"] + f:P1["conv_b"] + f + 1])
                            do(ins, Count(sem["c_ready"]))
                        if hh == 5:
                            act.wait_ge(sem["ha_ready"], 1)
                            A.squares(two(cacc, 0), 0)
                        if hh == 7:
                            act.wait_ge(sem["ha_ready"], 2)
                            for f in range(2):
                                ins = act.activation(cact[:, f, :], cacc[:, f, :], ACT.Silu,
                                                     bias=par1[:, P1["ln_b"] + f:P1["ln_b"] + f + 1],
                                                     scale=par1[:, P1["ln_g"] + f:P1["ln_g"] + f + 1])
                            do(ins, Count(sem["sig_ready"]))
                        turned(hh)
                        if hh < len(TAPS_AFTER):
                            tap_end = min(tap_end + TAPS_AFTER[hh], 2 * TAPS)
                            tap_diagonals(tap_end)

                    A.product_out(C1["out"], G1["out"], 1, par1, P1["mix_post"])
                    A.late_x(par1, P1["mlp_pre"])
                    with A.line.loop(4, [(w.hi_n, 4), (A.outs, 4)], A.outs) as i:
                        for j in range(4):
                            s, g = C1["up"] + j, G1["up"] + j
                            w.hi(s + 3, i)
                            act.wait_ge(sem["gate_in"], j + 1 + i * 4)
                            act.wait_ge(sem["groups_free"], g + 3 + i * 4)
                            do(act.activation(tX[:, j % 2, :], tS[:, j % 2, :], ACT.Square), A.outs)
                    A.product_out(C1["down"], G1["down"], 4, par1, P1["mlp_post"])
                    for p in range(4):
                        act.wait_ge(sem["h_ready"], A.h_seen + p + 1)
                        do(act.activation(two(xhi, 2 * p), two(h, 2 * p), ACT.Copy), A.rounded)
                    for p in range(4):
                        s = C1["gate"] + p
                        w.hi(s + 3)
                        used(act, s)
                        do(act.activation(two(GATE, 2 * p), main[:, p, :], ACT.Sigmoid), A.outs)
                    w.hi(C1["end"] + 2)
                    w.hi(C1["end"] + 3)

                @block.vector
                def _(dve):
                    V1 = Vector(dve, C1["end"])
                    do, settle, w = V1.do, V1.settle, V1.w
                    qk, sms, prods, normals = (Count(sem[n]) for n in ("qk_ready", "sm_ready", "prod_ready", "ha_ready"))
                    V1.credits()
                    dve.wait_ge(sem["par_in"], 16)
                    V1.pre_norm()
                    dve.wait_ge(sem["p_in"], 16)
                    do(dve.tensor_copy(acc[:, 0:P], tri))
                    do(dve.memset(acc[:, P:2 * P], 0.0))
                    do(dve.tensor_copy(acc[:, 2 * P:3 * P], tri))
                    dve.wait_ge(sem["pads_ready"], 1)
                    cos, sin = trig1[:, 0:1, :], trig1[:, 1:2, :]
                    rope_to = {0: (KI, 0, 1), 1: (KR, 0, 1)}
                    for p in range(4):
                        rope_to[2 + p] = (QI, 2 * p, 2)
                    for p in range(2):
                        rope_to[6 + p] = (Q, 2 * p, 2)

                    def rope_finish(s):
                        t, u, n = rope_to[s]
                        dve.wait_ge(sem["perm_done"], s + 1)
                        settle()
                        do(dve.tensor_tensor(units(tX[:, s % 2, 0:n * S]), units(aux[1][:, 0:n * S]),
                                             over(sin, n), ALU.mult), aux_free)
                        settle()
                        do(dve.tensor_tensor(t[:, u:u + n, :], t[:, u:u + n, :], units(tX[:, s % 2, 0:n * S]),
                                             ALU.add), qk)

                    aux_free = Count(sem["aux_free"])
                    reads = Count(sem["relu_used"])

                    def index_sum(p):
                        for hd in range(4 * p, 4 * p + 4):
                            dve.wait_ge(sem["relu_ready"], hd + 1)
                            settle()
                            for t, (c0, c1) in enumerate(((0, P), (P, RSPAN))):
                                do(dve.scalar_tensor_tensor(acc[:, c0:c1], sm[:, hd % 2, c0:c1],
                                                            wi[:, t, hd:hd + 1], acc[:, c0:c1],
                                                            ALU.mult, ALU.add), reads if t else None)

                    for s in range(11):
                        w.lo(s + 3)
                        if 2 <= s <= 9:
                            rope_finish(s - 2)
                        if 6 <= s <= 9:
                            index_sum(s - 6)
                        bank = main[:, s % 4, :]
                        if s < 10:
                            dve.wait_ge(sem["act_out"], s + 1)
                        else:
                            used(dve, s)
                        settle()
                        if s < 8:
                            t, u, n = rope_to[s]
                            if s == 0:
                                wts = bank[:, S:2 * S].rearrange("p (t c) -> p t c", t=2)[:, :, 0:IDX_HEADS]
                                do(dve.tensor_scalar(wi[:, :, :], wts, 1.0 / 32, None, ALU.mult))
                            if s == 1:
                                vs = bank[:, S:2 * S].rearrange("p (t c) -> p t c", t=2)
                                for kv in range(2):
                                    do(dve.tensor_copy(VP[:, kv, :, kv * 64:kv * 64 + 64], vs[:, :, kv * 64:kv * 64 + 64]))
                            do(dve.tensor_tensor(t[:, u:u + n, :], units(bank[:, 0:n * S]), over(cos, n), ALU.mult), V1.free)
                        elif s < 10:
                            do(dve.tensor_tensor(YC[:, s - 8, TAPS - 1:], bank[:, 0:S], tS[:, s % 2, 0:S], ALU.mult), V1.free)
                        else:
                            do(dve.tensor_copy(UP[:, :, 16:], units(bank)), V1.free, by=2)
                            settle()
                            dve.memset(small[:, 0, 2:3], 0.0).then_inc(sem["pool_in"], 1)

                    spans = ((0, P), (P, RSPAN))
                    cur = acc[:, :]
                    for r in range(TOPK // 8):
                        nxt = work[:, r % 2, :]
                        settle()
                        for t, (c0, c1) in enumerate(spans):
                            do(dve.max(best[:, t, :], cur[:, c0:c1]))
                        settle()
                        for t, (c0, c1) in enumerate(spans):
                            do(dve.match_replace(nxt[:, c0:c1], best[:, t, :], cur[:, c0:c1], TAKEN))
                        cur = nxt
                    settle()
                    do(dve.tensor_scalar(bias[:, :], cur, TAKEN, OFF, ALU.not_equal, ALU.mult))
                    settle()
                    do(dve.tensor_tensor(bias[:, 0:P], bias[:, 0:P], tri, ALU.add))
                    do(dve.tensor_tensor(bias[:, 2 * P:], bias[:, 2 * P:], tri, ALU.add))

                    def masked(hh):
                        dve.wait_ge(sem["scores_done"], hh + 1)
                        settle()
                        do(dve.scalar_tensor_tensor(sm[:, hh % 2, :], aux[2 + hh % 2][:, 0:RSPAN], 0.125, bias[:, :],
                                                    ALU.mult, ALU.add))
                        settle()
                        for t, (c0, c1) in enumerate(spans):
                            do(dve.tensor_reduce(rmax[:, hh, t:t + 1], sm[:, hh % 2, c0:c1], AX.X, ALU.max,
                                                 negate=True), sms if t else None)

                    probs = Count(sem["probs_ready"])

                    def normed(hh):
                        dve.wait_ge(sem["exp_ready"], hh + 1)
                        if hh >= 2:
                            dve.wait_ge(sem["pt_done"], hh - 1)
                        do(dve.reciprocal(rinv[:, hh, :], rsum[:, hh, :]))
                        settle()
                        for t, (c0, c1) in enumerate(spans):
                            do(dve.tensor_scalar(pt[:, hh % 2, c0:c1], sm[:, hh % 2, c0:c1],
                                                 rinv[:, hh, t:t + 1], None, ALU.mult), probs if t else None)

                    def attended(f):
                        dve.wait_ge(sem["pv_done"], 2 * f + 2)
                        V1.split(bhi[:, f, :], blo[:, f, :], main[:, f, 0:S], prods)

                    masked(0)
                    for hh in range(HEADS):
                        if hh + 1 < HEADS:
                            masked(hh + 1)
                        if hh == 5:
                            dve.wait_ge(sem["mean_done"], 1)
                            settle()
                            do(dve.tensor_tensor(cacc[:, :, :], cacc[:, :, :], over(stat(aux[0]).unsqueeze(1), 2),
                                                 ALU.subtract), normals)
                        if hh == 6:
                            V1.factor(1, eps=LN_EPS, at=aux[0])
                        if hh == 7:
                            V1.spread_done()
                            do(dve.tensor_tensor(cacc[:, :, :], cacc[:, :, :], over(rb.unsqueeze(1), 2), ALU.mult), normals)
                        normed(hh)
                        if hh % 2 and hh > 1:
                            attended(hh // 2 - 1)
                    dve.wait_ge(sem["aux_ready"], 1)
                    for f in range(2):
                        do(dve.tensor_scalar(tX[:, 0, f * S:(f + 1) * S], aux[2][:, f * S:(f + 1) * S],
                                             par1[:, P1["pool_scale"] + f:P1["pool_scale"] + f + 1], None, ALU.mult))
                    V1.split(two(bhi, 6), two(blo, 6), tX[:, 0, :], prods)
                    attended(HEADS // 2 - 1)
                    dve.wait_ge(sem["aux_ready"], 2)
                    V1.split(two(bhi, 4), two(blo, 4), aux[3][:, :], prods)

                    V1.product_out(C1["out"], G1["out"], 1)
                    V1.post_norm(late=XF)
                    V1.late_norm(R1[:, :, :], between=lambda: w.lo(C1["up"] + 2))
                    gate = Count(sem["gate_in"])
                    with V1.line.loop(4, [(w.lo_n, 4), (gate, 4), (V1.free, 4), (V1.line.own, 4)], V1.free) as i:
                        for j in range(4):
                            s = C1["up"] + j
                            used(dve, s, i)
                            do(dve.scalar_tensor_tensor(units(tS[:, j % 2, :]), units(main[:, j, :]), 0.0,
                                                        over(R1[:, :, :], 2), ALU.max, ALU.mult), gate)
                            w.lo(s + 3, i)
                            dve.wait_ge(sem["act_out"], 10 + j + 1 + i * 4)
                            settle()
                            uh = bhi[:, ds(i * 8 + 2 * j, 2), :]
                            ul = blo[:, ds(i * 8 + 2 * j, 2), :]
                            do(dve.tensor_copy(uh, units(tX[:, j % 2, :])))
                            settle()
                            do(dve.tensor_tensor(ul, units(tX[:, j % 2, :]), uh.bitcast(f32), ALU.subtract), V1.free)
                    V1.product_out(C1["down"], G1["down"], 4)
                    V1.post_norm(late=h)
                    w.lo(C1["gate"] + 2)
                    V1.split(two(pthi, 0), two(ptlo, 0), two(PT, 0), V1.xs)
                    for p in range(4):
                        w.lo(C1["gate"] + p + 3)
                        dve.wait_ge(sem["act_out"], 26 + p + 1)
                        do(dve.memset(small[:, 6, p:p + 1], 0.0), V1.free)
                    used(dve, C1["ple"])
                    for p in range(4):
                        settle()
                        do(dve.tensor_tensor(tX[:, p % 2, :], main[:, p, :], two(GATE, 2 * p), ALU.mult), V1.free)
                        settle()
                        do(dve.tensor_tensor(two(h, 2 * p), two(h, 2 * p), tX[:, p % 2, :], ALU.add))

                @block.tensor
                def _(pe):
                    T = Tensor(pe)
                    T.stats(4, 0)
                    T.spread()

                    def swap_rows(s):
                        n = S if s < 2 else 2 * S
                        pe.wait_ge(sem["act_out"], s + 1)
                        if s:
                            pe.wait_ge(sem["aux_free"], s)
                        pe.matmul(aux[1][:, 0:n], swap, tS[:, s % 2, 0:n], start=True, stop=True).then_inc(sem["perm_done"], 1)

                    def pairs(out_, q_, k_, off):
                        pe.matmul(out_[:, 0:P], q_[off:off + 64, 0:P], k_[off:off + 64, 0:P], start=True, stop=True)
                        return pe.matmul(out_[:, P:RSPAN], q_[off:off + 64, P:S], k_[off:off + 64, :], start=True, stop=True)

                    def dots(p):
                        pe.wait_ge(sem["qk_ready"], 3 + p)
                        for hd in range(4 * p, 4 * p + 4):
                            if hd >= 2:
                                pe.wait_ge(sem["relu_ready"], hd - 1)
                            pairs(aux[2 + hd % 2], QI[:, hd // 2, :], KI[:, 0, :], 64 * (hd % 2)).then_inc(sem["dots_done"], 1)

                    for s in range(11):
                        T.pair(s, s, tok=(False, s < 2), cols=(P, IDX_HEADS if s == 0 else P),
                               x=0 if s == 0 else None)
                        if 1 <= s <= 8:
                            swap_rows(s - 1)
                        if 5 <= s <= 8:
                            dots(s - 5)

                    def scores(hh):
                        if hh < 2:
                            pe.wait_ge(sem["relu_ready"], IDX_HEADS)
                            pe.wait_ge(sem["qk_ready"], 8)
                        else:
                            pe.wait_ge(sem["sm_ready"], hh - 1)
                        pairs(aux[2 + hh % 2], Q[:, hh // 2, :], KR[:, 0, :], 64 * (hh % 2)).then_inc(sem["scores_done"], 1)

                    def turn(hh):
                        pe.wait_ge(sem["probs_ready"], hh + 1)
                        if hh:
                            pe.wait_ge(sem["pt_ready"], hh)
                        for n in range(3):
                            last = pe.transpose(aux[1][:, n * P:(n + 1) * P], pt[:, hh % 2, n * P:(n + 1) * P], ident)
                        last.then_inc(sem["pt_done"], 1)

                    def mix_values(hh):
                        f, kv = hh // 2, hh % 2
                        pe.wait_ge(sem["pt_ready"], hh + 1)
                        o = main[:, f, 0:S]
                        pe.matmul(o, VP[:, kv, 0, :], work[:, hh % 2, 0:S], start=kv == 0, stop=kv == 1,
                                  skip_group_check=True)
                        pe.matmul(o[:, P:S], VP[:, kv, 1, :], work[:, hh % 2, S:RSPAN], start=False,
                                  stop=kv == 1, skip_group_check=True).then_inc(sem["pv_done"], 1)

                    taken = [0]

                    def taps(count):
                        for n in range(taken[0], taken[0] + count):
                            f, k = divmod(n, TAPS)
                            if k == 0:
                                pe.wait_ge(sem["groups_free"], 4 + 8 + f + 1)
                            pe.wait_ge(sem["tap_ready"], n + 1)
                            last = pe.matmul(aux[0][:, f * S:(f + 1) * S], tapd[:, n % TAP_RING, :],
                                             YC[:, f, k:k + S], start=k == 0, stop=k == TAPS - 1)
                            last.then_inc(sem["tap_used" if n < 2 * TAPS - 1 else "conv_done"], 1)
                        taken[0] += count

                    scores(0)
                    scores(1)
                    taps(TAPS_BEFORE)
                    pe.wait_ge(sem["groups_free"], 4 + 12)
                    for hh in range(HEADS):
                        if hh + 2 < HEADS:
                            scores(hh + 2)
                        turn(hh)
                        if hh:
                            mix_values(hh - 1)
                        if hh < len(TAPS_AFTER):
                            taps(TAPS_AFTER[hh])
                        if hh == 4:
                            pe.wait_ge(sem["c_ready"], 1)
                            T.stats(1, 2, src=cacc[:, :, :].rearrange("p a n -> p (a n)"), at=aux[0])
                        if hh == 5:
                            T.stats(1, 2, at=aux[0])
                        if hh == 6:
                            T.spread()
                            pe.wait_ge(sem["big_par_in"], 16)
                            pe.wait_ge(sem["pool_out"], 1)
                            pe.wait_ge(sem["sm_ready"], 7)
                            for f in range(2):
                                last = pe.matmul(aux[2][:, f * S:(f + 1) * S],
                                                 par1[:, P1["pool_w"] + f * P:P1["pool_w"] + (f + 1) * P], PO[:, f, :],
                                                 start=True, stop=True)
                            last.then_inc(sem["aux_ready"], 1)
                    mix_values(HEADS - 1)
                    pe.wait_ge(sem["sig_ready"], 1)
                    for f in range(2):
                        for k in range(2):
                            c = P1["conv_pw"] + (k * 2 + f) * P
                            last = pe.matmul(aux[3][:, f * S:(f + 1) * S], par1[:, c:c + P], cact[:, k, :],
                                             start=k == 0, stop=k == 1)
                    last.then_inc(sem["aux_ready"], 1)

                    for p in range(4):
                        T.from_units(C1["out"] + p, G1["out"] + p, bhi, blo, 0,
                                     ready=(1, 2, 3, 5, 6, 6, 4, 4) if p == 0 else None,
                                     order=(0, 1, 2, 6, 7, 3, 4, 5))
                    T.stats(4, 0, y=True)
                    T.spread()
                    for j in range(4):
                        T.pair(C1["up"] + j, G1["up"] + j, x=4 if j == 0 else None, norm=j == 0)
                    with pe.Fori(0, 3) as i:
                        for j in range(4):
                            T.pair(C1["up"] + 4 + j, G1["up"] + 4 + j, i)
                    T.long(C1["down"], G1["down"], 4, 16, 2, 4 + 32)
                    T.stats(4, 0, y=True)
                    T.spread()
                    for p in range(4):
                        T.pair(C1["gate"] + p, G1["gate"] + p, x=8 if p == 0 else None)
                    pe.wait_ge(sem["x_ready"], 13)
                    T.arrive(C1["ple"])
                    for g in range(4):
                        T.bank(G1["ple"] + g)
                        for f in range(2):
                            for k in range(2):
                                last = T.tile(main[:, g, f * S:(f + 1) * S], C1["ple"], (2 * g + f) * 2 + k,
                                              pthi[:, k, :], ptlo[:, k, :], k == 0, k == 1)
                    last.then_inc(sem["split_free"], 1)
            clear_all()

        with nc.Fori(0, LAYERS) as L:
            with nc.Block() as block:
                narrow = {*range(22, 38), *range(136, 152)}

                @block.sync
                def _(sp):
                    load_stream(sp, LAYERS * C1["end"], L, [(RING, 22, CHUNK), (22, 38, NARROW), (38, 136, CHUNK),
                                                            (136, 152, NARROW), (152, 156, CHUNK)], C2["end"])

                @block.gpsimd
                def _(pool):
                    pool.memset(XA[:, :, 0:3], 0.0).then_inc(sem["pads_ready"], 1)
                    roots(pool, range(1, 11))
                    last_lo(pool, C2["end"])

                @block.scalar
                def _(act):
                    cut = P2["w_a"]
                    act.dma_start(par2[:, 0:cut], a["par2"][ds(L * P, P), 0:cut]).then_inc(sem["par_in"], 16)
                    act.dma_start(par2[:, cut:], a["par2"][ds(L * P, P), cut:P2["end"]]).then_inc(sem["big_par_in"], 16)
                    A = Scalar(act, C2["end"], narrow)
                    do, settle, w = A.do, A.settle, A.w
                    A.late_x(par2, P2["f1_pre"], wait=False)
                    act.wait_ge(sem["root_in"], 1)
                    act.activation(small[:, 2, :], small[:, 1, :], ACT.Exp, scale=-1.0).then_inc(sem["root_ready"], 1)

                    def gates_in(c0, first):
                        def one(j, i=None):
                            w.hi(c0 + j + 3, i)
                            act.wait_ge(sem["gate_in"], first + j + 1 + (0 if i is None else i * 4))
                            do(act.activation(tS[:, j % 2, 0:S], tS[:, j % 2, 0:S], ACT.Silu), A.outs)
                        for j in range(4):
                            one(j)
                        with A.line.loop(4, [(w.hi_n, 4), (A.outs, 4)], A.outs) as i:
                            for j in range(4):
                                one(4 + j, i)
                        one(20)
                        one(21)

                    def evac(s, g, func):
                        used(act, s)
                        act.wait_ge(sem["groups_free"], g + 3)
                        do(act.activation(tS[:, g % 2, :], main[:, g % 4, :], func), A.outs)

                    gates_in(C2["f1in"], 0)
                    A.product_out(C2["f1out"], G2["f1out"], 4, par2, P2["f1_post"])
                    A.h_in(par2, P2["mix_pre"])
                    A.round_x()
                    act.wait_ge(sem["coef_ready"], 1)

                    def sigmoids(p):
                        for f in (2 * p, 2 * p + 1):
                            act.wait_ge(sem["gates_done"], f + 1)
                            bank = aux[1 + f % 2]
                            act.activation(Rg[:, f, :], bank[:, 0:S], ACT.Sigmoid,
                                           bias=par2[:, P2["b_a"] + f:P2["b_a"] + f + 1])
                            do(act.activation(Ig[:, f, :], bank[:, S:2 * S], ACT.Sigmoid,
                                              bias=par2[:, P2["b_x"] + f:P2["b_x"] + f + 1]), sigs)

                    def decays(half_):
                        settle()
                        for f in range(4 * half_, 4 * half_ + 4):
                            do(act.activation(Ag[:, f, :], Rg[:, f, :], ACT.Exp, scale=small[:, 7, f:f + 1]))
                        settle()
                        for f in range(4 * half_, 4 * half_ + 4):
                            do(act.activation(Rg[:, f, :], Rg[:, f, :], ACT.Tanh, scale=small[:, 7, f:f + 1]),
                               exps if f % 4 == 3 else None)

                    def retained(hd):
                        act.wait_ge(sem["pv_done"], hd + 1)
                        if hd == 0:
                            act.wait_ge(sem["ha_ready"], 2)
                        for n in range(2):
                            do(act.activation(two(RET, 4 * hd + 2 * n), aux[2 + n][:, :], ACT.Copy), rets)
                            A.squares(aux[2 + n][:, :], n)

                    sigs, exps, rets = (Count(sem[n]) for n in ("sig_ready", "exp_ready", "ret_ready"))
                    for s in range(C2["xa"], C2["mix"]):
                        w.hi(s + 3)
                        if 41 <= s <= 44:
                            sigmoids(s - 41)
                        if s in (45, 46):
                            decays(s - 45)
                        if s == 46:
                            act.wait_ge(sem["gates_done"], 8)
                            act.dma_start(DEC[:, :], a["decay"]).then_inc(sem["decay_in"], 16)
                        if s == 49:
                            act.wait_ge(sem["root_in"], 2)
                            act.activation(wide(Rg), wide(Rg), ACT.Sqrt, scale=-1.0).then_inc(sem["root_ready"], 1)
                        if s in (53, 55, 57, 59):
                            retained((s - 53) // 2)
                        for name, func in (("ya", ACT.Gelu_apprx_tanh), ("ga", ACT.Sigmoid), ("gb", ACT.Sigmoid),
                                           ("gc", ACT.Sigmoid), ("g", ACT.Silu)):
                            n = 8 if name == "g" else 4
                            if C2[name] <= s < C2[name] + n:
                                evac(s, G2[name] + s - C2[name], func)
                    A.product_out(C2["mix"], G2["mix"], 1, par2, P2["mix_post"])
                    A.late_x(par2, P2["f2_pre"])
                    gates_in(C2["f2in"], 22)
                    A.product_out(C2["f2out"], G2["f2out"], 4, par2, P2["f2_post"])
                    w.hi(C2["end"] + 3)

                @block.vector
                def _(dve):
                    V2 = Vector(dve, C2["end"], narrow)
                    do, settle, w = V2.do, V2.settle, V2.w
                    qk, sms, prods, cs, has, roots_in = (
                        Count(sem[n]) for n in ("qk_ready", "sm_ready", "prod_ready", "c_ready", "ha_ready", "root_in"))
                    V2.credits()
                    dve.wait_ge(sem["par_in"], 16)
                    for p in range(4):
                        V2.late_lo(p)
                    V2.late_norm(R2)
                    gate = Count(sem["gate_in"])

                    lam = par2[:, P2["lam"]:P2["lam"] + 8]
                    relu_, e_, t_, t2_, s_, coef = (small[:, n, :] for n in (0, 2, 3, 4, 5, 7))
                    settle()
                    do(dve.tensor_scalar(relu_, lam, -1.0, 0.0, ALU.mult, ALU.max))
                    do(dve.scalar_tensor_tensor(small[:, 1, :], lam, -1.0, lam, ALU.mult, ALU.max), roots_in)
                    dve.wait_ge(sem["root_ready"], 1)
                    do(dve.tensor_scalar(t_, e_, 2.0, None, ALU.add))
                    settle()
                    do(dve.reciprocal(s_, t_))
                    settle()
                    do(dve.tensor_tensor(t_, s_, e_, ALU.mult))
                    settle()
                    do(dve.tensor_tensor(t2_, t_, t_, ALU.mult))
                    settle()
                    do(dve.tensor_scalar(s_, t2_, 1.0 / 17, None, ALU.mult))
                    for n in range(15, 2, -2):
                        settle()
                        do(dve.scalar_tensor_tensor(s_, s_, 1.0 / n, t2_, ALU.add, ALU.mult))
                    settle()
                    do(dve.scalar_tensor_tensor(s_, s_, 1.0, t_, ALU.add, ALU.mult))
                    settle()
                    do(dve.scalar_tensor_tensor(s_, s_, 2.0, relu_, ALU.mult, ALU.add))
                    settle()
                    do(dve.tensor_scalar(coef, s_, -8.0, None, ALU.mult), Count(sem["coef_ready"]))
                    settle()

                    def hidden(c0, g0, outs):
                        def one(j, i=None, by=1):
                            k = 0 if i is None else i * 4
                            used(dve, c0 + j, i)
                            do(dve.tensor_tensor(tS[:, j % 2, 0:S], main[:, j % 4, 0:S], R2[:, 0, :], ALU.mult), gate)
                            w.lo(c0 + j + 3, i)
                            dve.wait_ge(sem["act_out"], outs + j + 1 + k)
                            settle()
                            x = tX[:, j % 2, 0:S]
                            do(dve.tensor_tensor(x, tS[:, j % 2, 0:S], main[:, j % 4, S:2 * S], ALU.mult))
                            settle()
                            do(dve.tensor_tensor(x, x, R2[:, 0, :], ALU.mult))
                            if i is None:
                                uh, ul = bhi[:, j, :], blo[:, j, :]
                            else:
                                uh, ul = (u[:, ds(i * 4 + j, 1), :].rearrange("p a n -> p (a n)") for u in (bhi, blo))
                            V2.split(uh, ul, x, V2.free, by)
                        for j in range(4):
                            one(j)
                        with V2.line.loop(4, [(w.lo_n, 4), (gate, 4), (V2.free, 4), (V2.line.own, 12)], V2.free) as i:
                            for j in range(4):
                                one(4 + j, i)
                        one(20)
                        one(21, by=3)

                    hidden(C2["f1in"], G2["f1in"], 0)
                    V2.product_out(C2["f1out"], G2["f1out"], 4)
                    V2.post_norm(scale=0.5)
                    w.lo(C2["xa"] + 2)
                    V2.pre_norm()

                    rb_used = Count(sem["rb_used"])
                    cos_sin, sin_cos = trig2[:, 0:2, :], trig2[:, 1:3, :]
                    took = [22]

                    def take():
                        took[0] += 1
                        dve.wait_ge(sem["act_out"], took[0])
                        settle()

                    def before(s):
                        if s == 45:
                            dve.wait_ge(sem["sig_ready"], 8)
                            settle()
                            do(dve.tensor_tensor(wide(Ig), wide(Ig), wide(Cg), ALU.mult))
                        if s == 47:
                            dve.wait_ge(sem["exp_ready"], 2)
                            settle()
                            do(dve.tensor_tensor(wide(Cg), wide(Ag), wide(Ag), ALU.mult))
                        if s == 48:
                            settle()
                            do(dve.scalar_tensor_tensor(wide(Rg), wide(Cg), 1.0, wide(Rg), ALU.add, ALU.mult), roots_in)
                        if s == 50:
                            dve.wait_ge(sem["root_ready"], 2)
                            settle()
                            do(dve.tensor_tensor(wide(Ig), wide(Ig), wide(Rg), ALU.mult))
                        if s in (51, 52):
                            settle()
                            for f in range((s - 51) * 4, (s - 50) * 4):
                                do(dve.tensor_tensor_scan(XA[:, f, 3:], Ag[:, f, :], Ig[:, f, :], 0.0,
                                                          ALU.mult, ALU.add), has if f % 4 == 3 else None)
                        if s in (52, 54, 56, 58):
                            hd = (s - 52) // 2
                            dve.wait_ge(sem["scores_done"], hd + 1)
                            if hd:
                                dve.wait_ge(sem["pv_done"], hd)
                            dve.wait_ge(sem["decay_in"], 16)
                            do(dve.tensor_tensor(SM[:, :], aux[1][:, 0:RSPAN], DEC[:, hd * RSPAN:(hd + 1) * RSPAN],
                                                 ALU.mult), sms)
                        if s in (54, 56, 58, 60):
                            V2.factor(2, at=aux[0])
                        if s in (55, 57, 59, 61):
                            hd = (s - 55) // 2
                            V2.spread_done()
                            dve.wait_ge(sem["ret_ready"], 2 * hd + 2)
                            settle()
                            do(dve.tensor_tensor(RET[:, 4 * hd:4 * hd + 4, :], RET[:, 4 * hd:4 * hd + 4, :],
                                                 over(rb.unsqueeze(1), 4), ALU.mult), rb_used)

                    for s in range(C2["xa"], C2["mix"]):
                        w.lo(s + 3)
                        before(s)
                        if s < C2["q"]:
                            p = s - C2["xa"]
                            used(dve, s)
                            dve.wait_ge(sem["pads_ready"], 1)
                            settle()
                            g = G2["xa"] + p
                            do(dve.tensor_copy(XA[:, 2 * p:2 * p + 2, 3:], units(main[:, g % 4, :])), V2.free)
                            for k in range(4):
                                settle()
                                for f in (2 * p, 2 * p + 1):
                                    wk = par2[:, P2["conv_w"] + f * 4 + k:P2["conv_w"] + f * 4 + k + 1]
                                    count = cs if k == 3 and f % 2 else None
                                    if k == 0:
                                        do(dve.tensor_scalar(Cg[:, f, :], XA[:, f, 0:S], wk,
                                                             par2[:, P2["conv_b"] + f:P2["conv_b"] + f + 1],
                                                             ALU.mult, ALU.add))
                                    else:
                                        do(dve.scalar_tensor_tensor(Cg[:, f, :], XA[:, f, k:k + S], wk, Cg[:, f, :],
                                                                    ALU.mult, ALU.add), count)
                        elif s < C2["v"]:
                            dst, u, g = ((q2, 2 * (s - C2["q"]), G2["q"] + s - C2["q"]) if s < C2["k"] else
                                         (k2, 2 * (s - C2["k"]), G2["k"] + s - C2["k"]))
                            used(dve, s)
                            settle()
                            bank = units(main[:, g % 4, :])
                            do(dve.tensor_tensor(units(tX[:, 0, :]), bank, cos_sin, ALU.mult))
                            do(dve.tensor_tensor(units(tX[:, 1, :]), bank, sin_cos, ALU.mult), V2.free)
                            settle()
                            do(dve.tensor_tensor(dst[:, u, :], tX[:, 0, 0:S], tX[:, 0, S:], ALU.subtract))
                            do(dve.tensor_tensor(dst[:, u + 1, :], tX[:, 1, 0:S], tX[:, 1, S:], ALU.add), qk)
                        elif s < C2["ya"]:
                            p = s - C2["v"]
                            used(dve, s)
                            settle()
                            do(dve.tensor_copy(V[:, :, p * S:(p + 1) * S], units(main[:, (G2["v"] + p) % 4, :])), V2.free)
                        elif s < C2["lru"]:
                            p = s - C2["ya"]
                            take()
                            if p == 3:
                                dve.wait_ge(sem["pv_done"], RET_HEADS)
                            do(dve.tensor_tensor(units(tX[:, p % 2, :]), units(tS[:, p % 2, :]),
                                                 XA[:, 2 * p:2 * p + 2, 3:], ALU.mult), V2.free)
                            V2.split(two(bhi, 16 + 2 * p), two(blo, 16 + 2 * p), tX[:, p % 2, :], prods)
                        elif s < C2["ga"]:
                            p = s - C2["lru"]
                            used(dve, s)
                            V2.copy_out(two(O, 2 * p), G2["lru"] + p)
                        elif s < C2["g"]:
                            p = s - C2["ga"]
                            take()
                            do(dve.tensor_tensor(two(MA, 2 * p), tS[:, p % 2, :], two(O, 2 * p), ALU.mult), V2.free)
                        elif s < C2["ret"]:
                            p = s - C2["g"]
                            take()
                            do(dve.tensor_tensor(tX[:, p % 2, :], tS[:, p % 2, :], two(RET, 2 * p), ALU.mult), V2.free)
                            V2.split(two(bhi, 2 * p), two(blo, 2 * p), tX[:, p % 2, :], prods)
                        elif s < C2["gb"]:
                            p = (s - C2["ret"]) // 2
                            if (s - C2["ret"]) % 2:
                                used(dve, s)
                                V2.copy_out(two(O, 2 * p), G2["ret"] + p)
                        elif s < C2["sc"]:
                            p = s - C2["gb"]
                            if p == 0:
                                do(dve.memset(SCP[:, :, 0:2], 0.0))
                            take()
                            do(dve.tensor_tensor(tX[:, p % 2, :], tS[:, p % 2, :], two(O, 2 * p), ALU.mult), V2.free)
                            settle()
                            do(dve.tensor_tensor(two(MA, 2 * p), two(MA, 2 * p), tX[:, p % 2, :], ALU.add))
                        elif s < C2["sco"]:
                            p, part = divmod(s - C2["sc"], 3)
                            g = G2["sc"] + s - C2["sc"]
                            used(dve, s)
                            settle()
                            bank = units(main[:, g % 4, :])
                            if part == 0:
                                do(dve.tensor_copy(tX[:, 0, :], main[:, g % 4, :]), V2.free)
                            elif part == 1:
                                do(dve.tensor_tensor(SCP[:, :, 2:], bank, units(tX[:, 0, :]), ALU.mult), V2.free)
                                for k in range(3):
                                    settle()
                                    for f in range(2):
                                        c = P2["sc_w"] + (2 * p + f) * 3 + k
                                        if k == 0:
                                            do(dve.tensor_scalar(SCC[:, f, :], SCP[:, f, 0:S], par2[:, c:c + 1],
                                                                 None, ALU.mult))
                                        else:
                                            do(dve.scalar_tensor_tensor(SCC[:, f, :], SCP[:, f, k:k + S],
                                                                        par2[:, c:c + 1], SCC[:, f, :],
                                                                        ALU.mult, ALU.add))
                            else:
                                do(dve.tensor_tensor(units(tX[:, 1, :]), bank, SCC[:, :, :], ALU.mult), V2.free)
                                V2.split(two(bhi, 16 + 2 * p), two(blo, 16 + 2 * p), tX[:, 1, :], prods)
                        elif s < C2["gc"]:
                            p = s - C2["sco"]
                            used(dve, s)
                            V2.copy_out(two(O, 2 * p), G2["sco"] + p)
                        else:
                            p = s - C2["gc"]
                            take()
                            do(dve.tensor_tensor(tX[:, 0, :], tS[:, p % 2, :], two(O, 2 * p), ALU.mult), V2.free)
                            settle()
                            do(dve.tensor_tensor(tX[:, 1, :], tX[:, 0, :], two(MA, 2 * p), ALU.add))
                            V2.split(two(bhi, 2 * p), two(blo, 2 * p), tX[:, 1, :], prods)
                    V2.product_out(C2["mix"], G2["mix"], 1)
                    V2.post_norm(late=XF)
                    V2.late_norm(R2, between=lambda: w.lo(C2["f2in"] + 2))
                    hidden(C2["f2in"], G2["f2in"], took[0])
                    V2.product_out(C2["f2out"], G2["f2out"], 4)
                    V2.post_norm(scale=0.5)

                @block.tensor
                def _(pe):
                    T = Tensor(pe)

                    def ffn(c0, g0, c1, g1, x):
                        for j in range(4):
                            T.pair(c0 + j, g0 + j, x=x if j == 0 else None, norm=j == 0)
                        with pe.Fori(0, 4) as i:
                            for j in range(4, 8):
                                T.pair(c0 + j, g0 + j, i)
                        T.pair(c0 + 20, g0 + 20)
                        T.pair(c0 + 21, g0 + 21)
                        T.long(c1, g1, 4, FFN2_TILES // 2, 2, 4 + g0 + 24)
                        T.stats(4, 0, y=True)
                        T.spread()

                    def lru_gates(p):
                        pe.wait_ge(sem["c_ready"], p + 1)
                        for f in (2 * p, 2 * p + 1):
                            if f >= 2:
                                pe.wait_ge(sem["sig_ready"], f - 1)
                            for n, wn in enumerate(("w_a", "w_x")):
                                c = P2[wn] + f * P
                                last = pe.matmul(aux[1 + f % 2][:, n * S:(n + 1) * S], par2[:, c:c + P], Cg[:, f, :],
                                                 start=True, stop=True)
                            last.then_inc(sem["gates_done"], 1)

                    def scores(hd):
                        pe.wait_ge(sem["qk_ready"], 8)
                        pe.wait_ge(sem["sig_ready"], 8)
                        if hd:
                            pe.wait_ge(sem["sm_ready"], hd)
                        for t, c0 in ((0, 0), (1, P)):
                            for k in range(2):
                                u = 2 * hd + k
                                last = pe.matmul(aux[1][:, t * S:t * S + S - c0], k2[:, u, t * P:(t + 1) * P],
                                                 q2[:, u, c0:S], start=k == 0, stop=k == 1)
                        last.then_inc(sem["scores_done"], 1)

                    def values(hd):
                        pe.wait_ge(sem["sm_ready"], hd + 1)
                        pe.wait_ge(sem["groups_free"], 4 + G2["v"] + 2 * hd + 2)
                        if hd:
                            pe.wait_ge(sem["sq_ready"], T.pieces)
                        for e in range(4):
                            o = aux[2 + e // 2][:, e % 2 * S:(e % 2 + 1) * S]
                            c = hd * 512 + e * P
                            pe.matmul(o, V[:, 0, c:c + P], SM[:, 0:S], start=True, stop=True, skip_group_check=True)
                            last = pe.matmul(o[:, P:S], V[:, 1, c:c + P], SM[:, S:RSPAN], start=False, stop=True,
                                             skip_group_check=True)
                        last.then_inc(sem["pv_done"], 1)

                    ffn(C2["f1in"], G2["f1in"], C2["f1out"], G2["f1out"], 0)
                    T.stats(4, 0)
                    T.spread()

                    for s in range(C2["xa"], C2["lru"]):
                        g = (G2["xa"] if s < C2["v"] else G2["v"]) + s - (C2["xa"] if s < C2["v"] else C2["v"])
                        if C2["v"] <= s < C2["ya"]:
                            T.arrive(s)
                            T.bank(g)
                            for t in range(2):
                                o = main[:, g % 4, t * S:(t + 1) * S].rearrange("p (f c) -> p f c", f=2)
                                for kt in range(KT):
                                    w_h, w_l = (x[:, s % RING, :].rearrange("p (f k c) -> p k f c", f=2, k=KT)[:, kt]
                                                for x in (whi, wlo))
                                    x_h, x_l = (x[:, kt, t * P:(t + 1) * P] for x in (xhi, xlo))
                                    pe.matmul(o, x_h, w_h, start=kt == 0, stop=False)
                                    pe.matmul(o, x_l, w_h, start=False, stop=False)
                                    last = pe.matmul(o, x_h, w_l, start=False, stop=kt == KT - 1)
                            last.then_inc(sem["split_free"], 1)
                        else:
                            T.pair(s, g, x=4 if s == C2["xa"] else None)
                        if s == 40:
                            pe.wait_ge(sem["big_par_in"], 16)
                        if 40 <= s <= 43:
                            lru_gates(s - 40)
                        if s in (54, 56, 58, 60):
                            T.spread()
                        if s in (53, 55, 57, 59):
                            if s > 53:
                                pe.wait_ge(sem["rb_used"], (s - 53) // 2)
                            T.stats(2, 1, at=aux[0])
                        if s in (52, 54, 56, 58):
                            values((s - 52) // 2)
                        if s in (51, 53, 55, 57):
                            scores((s - 51) // 2)
                    for p in range(4):
                        T.from_units(C2["lru"] + p, G2["lru"] + p, bhi, blo, 16,
                                     ready=[0 + kt // 2 + 1 for kt in range(KT)] if p == 0 else None)
                    for p in range(4):
                        T.pair(C2["ga"] + p, G2["ga"] + p)
                    with pe.Fori(0, 2) as i:
                        for j in range(4):
                            T.pair(C2["g"] + j, G2["g"] + j, i)
                    for n in range(8):
                        s, g = C2["ret"] + n, G2["ret"] + n // 2
                        T.arrive(s)
                        if n % 2 == 0:
                            T.bank(g)
                        for t in range(16):
                            if n == 0:
                                pe.wait_ge(sem["prod_ready"], 4 + t // 2 + 1)
                            last = T.tile(main[:, g % 4, n % 2 * S:(n % 2 + 1) * S], s, t, bhi[:, t, :], blo[:, t, :],
                                          t == 0, t == 15)
                        last.then_inc(sem["split_free"], 1)
                    for p in range(4):
                        T.pair(C2["gb"] + p, G2["gb"] + p)
                    with pe.Fori(0, 3) as i:
                        for j in range(4):
                            T.pair(C2["sc"] + j, G2["sc"] + j, i)
                    for p in range(4):
                        T.from_units(C2["sco"] + p, G2["sco"] + p, bhi, blo, 16,
                                     ready=[12 + kt // 2 + 1 for kt in range(KT)] if p == 0 else None)
                    for p in range(4):
                        T.pair(C2["gc"] + p, G2["gc"] + p)
                    for p in range(4):
                        T.from_units(C2["mix"] + p, G2["mix"] + p, bhi, blo, 0,
                                     ready=[16 + kt // 2 + 1 for kt in range(KT)] if p == 0 else None)
                    T.stats(4, 0, y=True)
                    T.spread()
                    ffn(C2["f2in"], G2["f2in"], C2["f2out"], G2["f2out"], 8)
            clear_all()

        with nc.Block() as block:
            @block.sync
            def _(sp):
                sp.dma_start(out, h[:, :, :]).then_inc(sem["out_done"], 16)
                sp.wait_ge(sem["out_done"], 16)



def constants():
    c = np.zeros((P, K["end"]), np.float32)
    c[:, 0:P] = np.eye(P)
    for base in (0, 64):
        for r in range(8):
            c[base + r + 8, K["swap"] + base + r] = -1.0
            c[base + r, K["swap"] + base + r + 8] = 1.0
    t = np.arange(P)
    c[:, K["tri"]:K["tri"] + P] = np.where(t[None, :] <= t[:, None], 0.0, MASKED)
    tok = np.arange(S)
    decay = np.zeros((P, RET_HEADS * RSPAN), np.float32)
    for hd in range(RET_HEADS):
        log_g = math.log1p(-2.0 ** (-5.0 - hd))
        d = np.exp(log_g * np.abs(tok[None, :] - tok[:, None])) / 16.0
        d = np.where(tok[:, None] // 64 <= tok[None, :] // 64, d, 0.0)
        decay[:, hd * RSPAN:hd * RSPAN + S] = d[0:P, :]
        decay[:, hd * RSPAN + S:(hd + 1) * RSPAN] = d[P:S, P:S]
    for n, win in enumerate((2, 4, 8, 16)):
        f, lo = n // 2, 64 * (n % 2)
        c[lo:lo + 64, K["rcount"] + f * S:K["rcount"] + (f + 1) * S] = 1.0 / np.minimum(tok + 1, win)
    for base in (0, 64):
        for r in range(16):
            c[base + r, K["freq"]] = np.float32(500000.0) ** np.float32(-(2 * (r % 8)) / 16)
    c[:, K["freq"] + 1] = np.float32(10000.0) ** (-np.arange(P, dtype=np.float32) / np.float32(P))
    return c, decay


def tiles(m):
    k, n = m.shape
    return m.reshape(k // P, P, n // P, P).transpose(2, 0, 1, 3).reshape(-1, P, P)


def chunks(t, per=CHUNK_TILES):
    c = t.reshape(-1, per, P, P).transpose(0, 2, 1, 3).reshape(-1, P, per * P)
    out = np.zeros((c.shape[0], P, CHUNK), np.float32)
    out[:, :, 0:per * P] = c
    return out


def units_of(v):
    v = v.reshape(v.shape[0] // P, P, -1)
    return v.transpose(1, 0, 2).reshape(P, -1)


def blocks(w, n):
    out = np.zeros((P, n, P), np.float32)
    for f in range(n):
        out[0:64, f, 0:64] = w[2 * f]
        out[64:P, f, 64:P] = w[2 * f + 1]
    return out.reshape(P, n * P)


def feature_major(x):
    return np.ascontiguousarray(x.T.reshape(-1, P, S).transpose(1, 0, 2))


def lay_out(v):
    w1, w2, par1, par2, ps = [], [], [], [], []
    heads = [half * 4 + f for f in range(4) for half in range(2)]
    for l in range(LAYERS):
        w = v["w_in"][l]
        q, k, vv, qi, ki, wi, conv, pool = np.split(w, [512, 640, 768, 1792, 1856, 1872, 2384], axis=1)
        q = q.reshape(D, HEADS, 64)[:, heads].reshape(D, 512)
        wi_ = np.zeros((D, P), np.float32)
        wi_[:, 0:IDX_HEADS] = wi
        order = [ki, ki, wi_, k, vv, qi, q, conv[:, 0:128], conv[:, 256:384], conv[:, 128:256], conv[:, 384:512], pool]
        w_out = v["w_out"][l]
        w_out = np.concatenate([w_out[0:512].reshape(HEADS, 64, D)[heads].reshape(512, D), w_out[512:]], axis=0)
        w1 += [chunks(tiles(np.concatenate(order, axis=1))), chunks(tiles(w_out)), chunks(tiles(v["w_up"][l])),
               chunks(tiles(v["w_down"][l])), chunks(tiles(v["ple_gate"][l])), chunks(tiles(v["ple_proj"][l]))]
        cp = v["conv_pw"][l]
        par1.append(np.concatenate(
            [units_of(v[n][l]) for n in ("norm_mix_pre", "norm_mix_post", "norm_mlp_pre", "norm_mlp_post")]
            + [units_of(v["conv_dw"][l].T), units_of(v["conv_b"][l]), units_of(v["conv_ln_g"][l]),
               units_of(v["conv_ln_b"][l]), units_of(v["pool_scale"][l]), units_of(cp), blocks(v["pool_w"][l], 2)],
            axis=1))
        ps.append(feature_major(v["p"][l, 0]).reshape(P, 2 * S))

        def ffn(n):
            w = v[n + "_w_in_2"][l]
            both = np.stack([w[:, 0:FFN2].reshape(D, FFN2_TILES, P), w[:, FFN2:].reshape(D, FFN2_TILES, P)], axis=2)
            return [chunks(tiles(both.reshape(D, 2 * FFN2))), chunks(tiles(v[n + "_w_out_2"][l]), FFN2_TILES // 2)]

        m = v["w_mix_in_2"][l]
        xa, ya, q, k, vv, g, sb, sc, sh, gates = np.split(m, [1024, 2048, 3072, 4096, 6144, 8192, 9216, 10240, 11264], axis=1)
        ga, gb, gc = np.split(gates, 3, axis=1)
        thirds = np.stack([z.reshape(D, 4, 256) for z in (sc, sh, sb)], axis=2).reshape(D, 3072)
        w2 += ffn("ffn1") + [chunks(tiles(z)) for z in (
            xa, q, k, vv, ya, v["w_lru_out_2"][l], ga, g, v["w_ret_out_2"][l], gb, thirds, v["w_sc_out_2"][l], gc,
            v["w_mix_out_2"][l])] + ffn("ffn2")
        par2.append(np.concatenate(
            [units_of(v[n + "_2"][l]) for n in ("ffn1_pre_g", "ffn1_post_g", "mix_pre_g")]
            + [units_of(v["lru_conv_w_2"][l].T)]
            + [units_of(v[n + "_2"][l]) for n in ("lru_conv_b", "lru_b_a", "lru_b_x", "lru_lambda", "mix_post_g",
                                                  "ffn2_pre_g", "ffn2_post_g")]
            + [units_of(v["sc_conv_w_2"][l].T), blocks(v["lru_w_a_2"][l], 8), blocks(v["lru_w_x_2"][l], 8)], axis=1))
    consts, decay = constants()
    pos = np.stack([v["positions"].reshape(S), v["positions_2"].reshape(S)])
    return {
        "x": feature_major(v["x"][0]),
        "pos": np.ascontiguousarray(np.broadcast_to(pos[None], (P, 2, S))),
        "consts": consts,
        "decay": decay,
        "par1": np.concatenate(par1, axis=0),
        "par2": np.concatenate(par2, axis=0),
        "p": np.concatenate(ps, axis=0),
        "w": np.concatenate(w1 + w2 + [np.zeros((RING, P, CHUNK), np.float32)], axis=0).reshape(-1, CHUNK),
    }


def kernel(**inputs):
    import concourse.bacc as bacc
    from concourse import mybir
    from concourse.bass_utils import run_bass_kernel_spmd

    arrays = lay_out({k: np.asarray(v) for k, v in inputs.items()})
    nc = bacc.Bacc("TRN2", target_bir_lowering=False, num_devices=1)
    drams = {n: nc.dram_tensor(f"in_{n}", z.shape, mybir.dt.from_np(z.dtype), kind="ExternalInput").ap()
             for n, z in arrays.items()}
    out = nc.dram_tensor("out_h", (P, KT, S), mybir.dt.float32, kind="ExternalOutput").ap()
    build(nc, drams, out)
    r = run_bass_kernel_spmd(nc, [{f"in_{n}": z for n, z in arrays.items()}], core_ids=[0])
    got = np.asarray(r.results[0]["out_h"])
    return np.ascontiguousarray(got.transpose(1, 0, 2).reshape(1, D, S).transpose(0, 2, 1))
```
